# Optimizing a Trainium2 kernel written in Bass

```python
import jax, jax.numpy as jnp
from jax import lax
import numpy as np

D_MODEL = 1024
BATCH = 1
SEQ = 256
DEPTH = 1
DEC_BATCH = 1
DEC_SEQ = 512
PAST_LEN = 128

D_REC = 512
N_REC_HEADS = 8
REC_HEAD = D_REC // N_REC_HEADS
CONV_W = 4
CONV_LEFT = 2
LRU_C = 8.0
D_SGU = 512
N_SGU_HEADS = 8
SGU_HEAD = D_SGU // N_SGU_HEADS
CHUNK = 128
D_MIX = D_REC + D_SGU
D_IN = 2 * D_REC + 2 * D_SGU
N_GROUPS = 4
N_EXP_PER_GROUP = 4
N_EXPERTS = N_GROUPS * N_EXP_PER_GROUP
TOP_K = 2
D_EXPERT = 512
D_PLE = 256
EPS = 1e-6

kernel_name = "hymba_style_rglru_sgu_hiermoe_encoder"

def rms_norm(x, g):
    xf = x.astype(jnp.float32)
    y = xf * lax.rsqrt(jnp.mean(xf * xf, axis=-1, keepdims=True) + EPS)
    return (y * g.astype(jnp.float32)).astype(x.dtype)

def layer_norm(x, g, b):
    xf = x.astype(jnp.float32)
    mu = jnp.mean(xf, axis=-1, keepdims=True)
    xc = xf - mu
    var = jnp.mean(xc * xc, axis=-1, keepdims=True)
    y = xc * lax.rsqrt(var + EPS) * g.astype(jnp.float32) + b.astype(jnp.float32)
    return y.astype(x.dtype)

def centred_depthwise_conv(x, w, b):
    s = x.shape[1]
    xp = jnp.pad(x, ((0, 0), (CONV_LEFT, CONV_W - 1 - CONV_LEFT), (0, 0)))
    return sum(xp[:, k:k + s] * w[k] for k in range(CONV_W)) + b

def _lru_combine(left, right):
    a_l, h_l = left
    a_r, h_r = right
    return a_l * a_r, a_r * h_l + h_r

def rg_lru_direction(x, w_a, b_a, w_x, b_x, lam, reverse):
    bsz, s, _ = x.shape
    xh = x.reshape(bsz, s, N_REC_HEADS, REC_HEAD)
    r = jax.nn.sigmoid(jnp.einsum('bshi,hij->bshj', xh, w_a).reshape(bsz, s, D_REC) + b_a)
    i = jax.nn.sigmoid(jnp.einsum('bshi,hij->bshj', xh, w_x).reshape(bsz, s, D_REC) + b_x)
    log_a = -LRU_C * r * jax.nn.softplus(-lam.astype(jnp.float32))
    a = jnp.exp(log_a)
    mult = jnp.sqrt(-jnp.expm1(2.0 * log_a))
    _, h = lax.associative_scan(_lru_combine, (a, mult * (i * x)), axis=1, reverse=reverse)
    return h

def recurrent_group(xr, gr, conv_w, conv_b, w_a, b_a, w_x, b_x, lam):
    xc = centred_depthwise_conv(xr, conv_w, conv_b).astype(jnp.float32)
    h = (rg_lru_direction(xc, w_a[0], b_a[0], w_x[0], b_x[0], lam[0], False)
         + rg_lru_direction(xc, w_a[1], b_a[1], w_x[1], b_x[1], lam[1], True))
    return h.astype(xr.dtype) * jax.nn.gelu(gr)

def spatial_gating_group(u, v, ln_g, ln_b, w_s, b_s):
    bsz, s, _ = v.shape
    vn = layer_norm(v, ln_g, ln_b).reshape(bsz, s // CHUNK, CHUNK, N_SGU_HEADS, SGU_HEAD)
    mixed = jnp.einsum('hts,bnshc->bnthc', w_s, vn) + b_s.T[:, :, None]
    return u * mixed.reshape(bsz, s, D_SGU)

def hierarchical_moe(n, w_rg, b_rg, w_re, b_re, w1, w3, w2):
    bsz, s, d = n.shape
    t = n.reshape(bsz * s, d)
    g_prob = jax.nn.softmax((t @ w_rg).astype(jnp.float32) + b_rg.astype(jnp.float32), axis=-1)
    g_top, g_idx = lax.top_k(g_prob, 1)
    e_logits = ((t @ w_re).astype(jnp.float32) + b_re.astype(jnp.float32)).reshape(-1, N_GROUPS, N_EXP_PER_GROUP)
    e_logits = jnp.take_along_axis(e_logits, g_idx[:, :, None], axis=1)[:, 0]
    e_top, e_idx = lax.top_k(jax.nn.softmax(e_logits, axis=-1), TOP_K)
    weights = g_top * (e_top / jnp.sum(e_top, axis=-1, keepdims=True))
    expert_id = g_idx * N_EXP_PER_GROUP + e_idx
    gate = jnp.einsum('mk,mke->me', weights,
                      jax.nn.one_hot(expert_id, N_EXPERTS, dtype=jnp.float32)).astype(n.dtype)
    out = jnp.zeros_like(t)
    for e in range(N_EXPERTS):
        hdn = jax.nn.silu(t @ w1[e]) * (t @ w3[e])
        out = out + gate[:, e:e + 1] * (hdn @ w2[e])
    return out.reshape(bsz, s, d)

def encoder_trunk(x, p, W):
    h = x
    for l in range(DEPTH):
        n = rms_norm(h, W['g_mix'][l])
        z = n @ W['w_in'][l]
        xr, gr, zu, zv = jnp.split(z, [D_REC, 2 * D_REC, 2 * D_REC + D_SGU], axis=-1)
        y_rec = recurrent_group(xr, gr, W['conv_w'][l], W['conv_b'][l], W['lru_w_a'][l], W['lru_b_a'][l],
                                W['lru_w_x'][l], W['lru_b_x'][l], W['lru_lambda'][l])
        y_sgu = spatial_gating_group(jax.nn.gelu(zu), jax.nn.gelu(zv), W['sgu_ln_g'][l], W['sgu_ln_b'][l],
                                     W['sgu_w_s'][l], W['sgu_b_s'][l])
        merged = jnp.concatenate([rms_norm(y_rec, W['g_rec_out'][l]), rms_norm(y_sgu, W['g_sgu_out'][l])], axis=-1)
        h = h + merged @ W['w_out'][l]
        h = h + hierarchical_moe(rms_norm(h, W['g_ffn'][l]), W['w_router_group'][l], W['b_router_group'][l],
                                 W['w_router_expert'][l], W['b_router_expert'][l],
                                 W['w_exp_gate'][l], W['w_exp_up'][l], W['w_exp_down'][l])
        gate = jax.nn.sigmoid(rms_norm(h, W['g_ple'][l]) @ W['w_ple_gate'][l])
        h = h + gate * (p[l] @ W['w_ple_proj'][l])
    return rms_norm(h, W['g_final'])

def setup_inputs(seed: int = 0) -> dict:
    key = jax.random.key(seed)
    ks = jax.random.split(key, 40)
    f32 = jnp.float32

    def nrm(i, shape, scale):
        return scale * jax.random.normal(ks[i], shape, f32)

    def gain(i, shape):
        return 1.0 + 0.1 * jax.random.normal(ks[i], shape, f32)

    u = jax.random.uniform(ks[10], (DEPTH, 2, D_REC), f32, minval=0.9, maxval=0.999)
    s = u ** (1.0 / LRU_C)
    lru_lambda = jnp.log(s) - jnp.log1p(-s)
    return {
        "x_prompt": nrm(0, (BATCH, SEQ, D_MODEL), 1.0),
        "x_sample": nrm(1, (DEC_BATCH, DEC_SEQ, D_MODEL), 1.0),
        "p_prompt": nrm(2, (DEPTH, BATCH, SEQ, D_PLE), 1.0),
        "p_sample": nrm(3, (DEPTH, DEC_BATCH, DEC_SEQ, D_PLE), 1.0),
        "g_mix": gain(4, (DEPTH, D_MODEL)),
        "w_in": nrm(5, (DEPTH, D_MODEL, D_IN), D_MODEL ** -0.5),
        "conv_w": nrm(6, (DEPTH, CONV_W, D_REC), CONV_W ** -0.5),
        "conv_b": nrm(7, (DEPTH, D_REC), 0.02),
        "lru_w_a": nrm(8, (DEPTH, 2, N_REC_HEADS, REC_HEAD, REC_HEAD), REC_HEAD ** -0.5),
        "lru_b_a": nrm(9, (DEPTH, 2, D_REC), 0.1),
        "lru_w_x": nrm(11, (DEPTH, 2, N_REC_HEADS, REC_HEAD, REC_HEAD), REC_HEAD ** -0.5),
        "lru_b_x": nrm(12, (DEPTH, 2, D_REC), 0.1),
        "lru_lambda": lru_lambda,
        "sgu_ln_g": gain(13, (DEPTH, D_SGU)),
        "sgu_ln_b": nrm(14, (DEPTH, D_SGU), 0.02),
        "sgu_w_s": nrm(15, (DEPTH, N_SGU_HEADS, CHUNK, CHUNK), CHUNK ** -0.5),
        "sgu_b_s": gain(16, (DEPTH, N_SGU_HEADS, CHUNK)),
        "g_rec_out": gain(17, (DEPTH, D_REC)),
        "g_sgu_out": gain(18, (DEPTH, D_SGU)),
        "w_out": nrm(19, (DEPTH, D_MIX, D_MODEL), D_MIX ** -0.5),
        "g_ffn": gain(20, (DEPTH, D_MODEL)),
        "w_router_group": nrm(21, (DEPTH, D_MODEL, N_GROUPS), D_MODEL ** -0.5),
        "b_router_group": nrm(22, (DEPTH, N_GROUPS), 0.01),
        "w_router_expert": nrm(23, (DEPTH, D_MODEL, N_EXPERTS), D_MODEL ** -0.5),
        "b_router_expert": nrm(24, (DEPTH, N_EXPERTS), 0.01),
        "w_exp_gate": nrm(25, (DEPTH, N_EXPERTS, D_MODEL, D_EXPERT), D_MODEL ** -0.5),
        "w_exp_up": nrm(26, (DEPTH, N_EXPERTS, D_MODEL, D_EXPERT), D_MODEL ** -0.5),
        "w_exp_down": nrm(27, (DEPTH, N_EXPERTS, D_EXPERT, D_MODEL), D_EXPERT ** -0.5),
        "g_ple": gain(28, (DEPTH, D_MODEL)),
        "w_ple_gate": nrm(29, (DEPTH, D_MODEL, D_MODEL), D_MODEL ** -0.5),
        "w_ple_proj": nrm(30, (DEPTH, D_PLE, D_MODEL), D_PLE ** -0.5),
        "g_final": gain(31, (D_MODEL,)),
    }

def reference(x_prompt, x_sample, p_prompt, p_sample, g_mix, w_in, conv_w, conv_b, lru_w_a, lru_b_a,
              lru_w_x, lru_b_x, lru_lambda, sgu_ln_g, sgu_ln_b, sgu_w_s, sgu_b_s, g_rec_out, g_sgu_out,
              w_out, g_ffn, w_router_group, b_router_group, w_router_expert, b_router_expert,
              w_exp_gate, w_exp_up, w_exp_down, g_ple, w_ple_gate, w_ple_proj, g_final):
    W = {
        'g_mix': g_mix, 'w_in': w_in, 'conv_w': conv_w, 'conv_b': conv_b,
        'lru_w_a': lru_w_a, 'lru_b_a': lru_b_a, 'lru_w_x': lru_w_x, 'lru_b_x': lru_b_x,
        'lru_lambda': lru_lambda, 'sgu_ln_g': sgu_ln_g, 'sgu_ln_b': sgu_ln_b,
        'sgu_w_s': sgu_w_s, 'sgu_b_s': sgu_b_s, 'g_rec_out': g_rec_out, 'g_sgu_out': g_sgu_out,
        'w_out': w_out, 'g_ffn': g_ffn, 'w_router_group': w_router_group,
        'b_router_group': b_router_group, 'w_router_expert': w_router_expert,
        'b_router_expert': b_router_expert, 'w_exp_gate': w_exp_gate, 'w_exp_up': w_exp_up,
        'w_exp_down': w_exp_down, 'g_ple': g_ple, 'w_ple_gate': w_ple_gate,
        'w_ple_proj': w_ple_proj, 'g_final': g_final,
    }
    y_prompt = encoder_trunk(x_prompt, p_prompt, W)
    y_sample = encoder_trunk(x_sample, p_sample, W)
    return (y_prompt, y_sample)


_drawn_inputs = setup_inputs


def setup_inputs(seed=0):
    import zlib

    import numpy as np

    out = dict(_drawn_inputs(seed))
    spreads = {}
    factors = {'lru_b_a': 2.974,
     'sgu_ln_b': 3.462,
     'b_router_group': 3.594,
     'b_router_expert': 15.054,
     'g_ple': 4.012}
    for name, (base, spread) in spreads.items():
        noise = np.random.default_rng([zlib.crc32(name.encode()), seed]).standard_normal(out[name].shape)
        drawn = base * np.exp(spread * noise) if base else spread * noise
        out[name] = __import__('jax').numpy.asarray(drawn.astype(out[name].dtype))
    for name, factor in factors.items():
        out[name] = (out[name] * factor).astype(out[name].dtype)
    return out
```

```python
from contextlib import ExitStack

import concourse.bass as bass
from concourse import mybir

F32 = mybir.dt.float32
BF16 = mybir.dt.bfloat16
I32 = mybir.dt.int32
ALU = mybir.AluOpType
ACT = mybir.ActivationFunctionType
AX = mybir.AxisListType

P = 128
D = 1024
KD = D // P
NPROMPT, NSAMPLE = 256, 512
NTOK = NPROMPT + NSAMPLE
NT = NTOK // P
SEGS = [(0, NPROMPT), (NPROMPT, NSAMPLE)]
DR = 512
C4 = DR // P
NH = 8
HD = DR // NH
NG, NEG = 4, 4
NE = NG * NEG
DE = 512
F4 = DE // P
DPLE = 256
EPS = 1e-6
CAP = 160
CAP2 = CAP - P
MAX_OVER = 2 * NTOK // CAP
NROUND = NE + MAX_OVER
NSLOT = NROUND * CAP
MASKED = -3.0e38

CONV_W, CONV_B, B_A, B_X, LAM, G_REC, G_SGU, B_S = 0, 16, 20, 28, 36, 44, 48, 52
NPAR = 60


def hybrid_encoder_kernel(nc, x_prompt, x_sample, p_prompt, p_sample, g_mix, w_in, conv_w, conv_b, lru_w_a,
                          lru_b_a, lru_w_x, lru_b_x, lru_lambda, sgu_ln_g, sgu_ln_b, sgu_w_s, sgu_b_s,
                          g_rec_out, g_sgu_out, w_out, g_ffn, w_router_group, b_router_group,
                          w_router_expert, b_router_expert, w_exp_gate, w_exp_up, w_exp_down, g_ple,
                          w_ple_gate, w_ple_proj, g_final, y_prompt, y_sample):
    n2_dram = nc.dram_tensor("n2_scratch", (NTOK, D), F32, kind="Internal").ap()
    y_dram = nc.dram_tensor("y_scratch", (NSLOT, D), F32, kind="Internal").ap()

    def token_rows(prompt, sample, i):
        src, at = (prompt, i) if i < 2 else (sample, i - 2)
        return src[at * P:(at + 1) * P, :]

    with ExitStack() as ctx:
        def sb(name, shape, dt=F32):
            return ctx.enter_context(nc.sbuf_tensor(name, shape, dt))

        def sem(name):
            return ctx.enter_context(nc.semaphore(name))

        ring = sb("ring", [P, 6, 4096])
        h = sb("h", [P, NT, D])
        regT = sb("regT", [P, KD * NTOK])
        regN = sb("regN", [P, NT * D])
        regR = sb("regR", [P, 5 * NTOK])
        regX = sb("regX", [P, C4 * NTOK])
        wsT = sb("wsT", [P, NH, P])

        def slot3(s):
            return ring[:, s, :].rearrange("p (k n) -> p k n", k=KD)

        early = ring[:, 5, :]
        wbd = early[:, 0:2048]
        w_s = early[:, 2048:3072].rearrange("p (h s) -> p h s", h=NH)
        ln_g = early[:, 3072:3584]
        ln_b = early[:, 3584:4096]
        nT = regT[:, :].rearrange("p (k t) -> p k t", k=KD)
        ysT = regT[:, 0:C4 * NTOK].rearrange("p (c t) -> p c t", c=C4)
        ntok = regN[:, :].rearrange("p (i d) -> p i d", i=NT)
        v_tm = regN[:, 0:NT * DR].rearrange("p (i d) -> p i d", i=NT)
        u_tm = regN[:, NT * DR:2 * NT * DR].rearrange("p (i d) -> p i d", i=NT)
        gr = regN[:, 0:C4 * NTOK].rearrange("p (c t) -> p c t", c=C4)
        TR, TI, A0, TT, HF = (regR[:, j * NTOK:(j + 1) * NTOK] for j in range(5))
        zeros = regR[:, NTOK:NTOK + D]
        xc = regX[:, :].rearrange("p (c t) -> p c t", c=C4)

        ident = sb("ident", [P, P])
        ones = sb("ones", [P, 2])
        gB = sb("gB", [P, D])
        par_rows = regR[0:NPAR, 0:P]
        chan = sb("chan", [P, NPAR])
        wr = sb("wr", [P, KD, NG + NE])
        br = sb("br", [P, NG + NE])
        tri = sb("tri", [P, P], BF16)
        onesb = sb("onesb", [P, P], BF16)
        tokid = sb("tokid", [P, NT, 2], BF16)
        iota = sb("iota", [P, CAP])
        iota16 = sb("iota16", [P, NE])
        small = sb("small", [P, 400])
        rankm = sb("rankm", [P, NE + 2, NT])
        table = sb("table", [P, 64], I32)
        slots = sb("slots", [P, 2, NT], I32)
        idsi = sb("idsi", [P, 2, 2], I32)
        idsf = sb("idsf", [P, 2, 2])
        offs = sb("offs", [P, MAX_OVER])
        iota_o = regR[:, 2200:2200 + CAP]
        onehot = regR[:, 2400:2400 + NT * CAP // 2].bitcast(BF16).rearrange("p (i s) -> p i s", i=NT)

        taken = [0]

        def tiny(n):
            at = taken[0]
            taken[0] += n
            assert taken[0] <= 400
            return small[:, at:at + n]

        nhalf = tiny(8)
        iotaj = tiny(MAX_OVER)
        moe = {}
        at = 0
        for b in range(2):
            moe["xg", b] = regT[:, at:at + D]
            moe["y", b] = regN[:, at:at + D]
            at += D
        for b in range(2):
            moe["xg2", b] = regT[0:CAP2, at:at + D]
            moe["y2", b] = regN[0:CAP2, at:at + D]
            at += D
        for b in range(2):
            moe["xT", b] = (regT if b == 0 else regN)[:, at:at + KD * CAP].rearrange("p (k s) -> p k s", k=KD)
        p_tm = regX[:, 0:NT * DPLE].rearrange("p (i d) -> p i d", i=NT)
        pT = regX[:, NT * DPLE:2 * NT * DPLE].rearrange("p (k t) -> p k t", k=2)
        sig = regR[:, 0:1024].rearrange("p (b n) -> p b n", b=2)
        pgm = regR[:, 1024:2048].rearrange("p (b n) -> p b n", b=2)
        silu = regR[:, 0:F4 * CAP].rearrange("p (f s) -> p f s", f=F4)
        hid = regR[:, F4 * CAP:2 * F4 * CAP].rearrange("p (f s) -> p f s", f=F4)

        bank = [ctx.enter_context(nc.psum_tensor(f"bank{b}", [P, 512], F32)) for b in range(8)]

        x_in = [sem(f"x_in{i}") for i in range(NT)]
        ring_in = [sem(f"ring_in{s}") for s in range(6)]
        par_in = sem("par_in")
        wbd_in, ws_in, ln_in, wr_in, gB_in = sem("wbd_in"), sem("ws_in"), sem("ln_in"), sem("wr_in"), sem("gB_in")
        consts = sem("consts")
        filled = sem("filled")
        act_drained = sem("act_drained")
        dve_drained = sem("dve_drained")
        act_seq, dve_seq, pool_seq = sem("act_seq"), sem("dve_seq"), sem("pool_seq")
        sumsq_done, rstd_done, norm_done = sem("sumsq_done"), sem("rstd_done"), sem("norm_done")
        ln_var, ln_rstd, v_ready = sem("ln_var"), sem("ln_rstd"), sem("v_ready")
        zeroed = sem("zeroed")
        halves_ready, exp_lam, decay_ready = sem("halves_ready"), sem("exp_lam"), sem("decay_ready")
        rec_exp, rec_m2, rec_mult = sem("rec_exp"), sem("rec_m2"), sem("rec_mult")
        scan_part, rec_sum = sem("scan_part"), sem("rec_sum")
        us_sq, us_rstd, us_scaled = sem("us_sq"), sem("us_rstd"), sem("us_scaled")
        rec_y, rec_sq, rec_g = sem("rec_y"), sem("rec_sq"), sem("rec_g")
        rr_rstd = sem("rr_rstd")
        h_ready = sem("h_ready")
        n2_stored = sem("n2_stored")
        route_max, route_exp, chosen, routed = sem("route_max"), sem("route_exp"), sem("chosen"), sem("routed")
        ids_sum, ramp_ready = sem("ids_sum"), sem("ramp_ready")
        turn_go, gather_go = sem("turn_go"), sem("gather_go")
        onehot_ready, ids_full, ids_ready = sem("onehot_ready"), sem("ids_full"), sem("ids_ready")
        gathered = [sem("gathered0"), sem("gathered1")]
        t_full, t_drained = sem("t_full"), sem("t_drained")
        gu_full, silu_done, hid_done = sem("gu_full"), sem("silu_done"), sem("hid_done")
        ylo_full, yhi_full = sem("ylo_full"), sem("yhi_full")
        ylo_drained, yhi_drained = sem("ylo_drained"), sem("yhi_drained")
        y_stored = [sem("y_stored0"), sem("y_stored1")]
        yg_in = [sem(f"yg_in{b}") for b in range(4)]
        p_in = sem("p_in")
        moe_added = sem("moe_added")
        stored = sem("stored")

        groups = [("par", "dve")]
        groups += [(f"nT{i}{j}", "act" if j else "dve") for i in range(NT) for j in range(2)]
        groups += [(f"xr{c}{s}", "dve") for c in range(C4) for s in range(2)]
        groups += [(f"wsT{j}", "act") for j in range(2)]
        fillers = [[f"v{2 * j + a}" for a in range(2)] for j in range(3)]
        fillers += [[f"u{2 * j + a}" for a in range(2)] for j in range(3)]
        fillers += [[f"mix{hh}" for hh in range(NH)], [f"gr{c}{s}" for c in range(C4) for s in range(2)]]
        for unit in range(8):
            groups += [(f"gate{unit}{g}{s}", "act") for g in range(2) for s in range(2)]
            groups += [(x, "dve" if x[:3] == "mix" else "act") for x in fillers[unit]]
        groups += [(f"ysT{c}{s}", "act" if s else "dve") for c in range(C4) for s in range(2)]
        groups += [("ssq", "dve")]
        groups += [(f"out{i}{j}{g}", "dve") for i in range(NT) for j in range(2) for g in "rs"]
        groups += [(f"n2T{i}{j}", "act" if j else "dve") for i in range(NT) for j in range(2)]
        groups += [("route", "dve"), ("rank", "dve"), ("total", "dve")]
        number = {name: n for n, (name, _) in enumerate(groups)}
        drain_count, seen = {}, {"act": 0, "dve": 0}
        for name, who in groups:
            seen[who] += 1
            drain_count[name] = seen[who]
        NGROUP = len(groups)
        late = [(f"n3T{i}{j}", "act" if j else "dve") for i in range(NT) for j in range(2)]
        late += [(f"pT{k}{s}", "act" if s else "dve") for k in range(2) for s in range(2)]
        late += [(f"{g}{i}{j}", "act" if g == "pg" else "dve") for i in range(NT) for j in range(2) for g in ("pg", "pp")]
        for n, (name, who) in enumerate(late):
            number[name] = NGROUP + n
            seen[who] += 1
            drain_count[name] = seen[who]
        allgroups = groups + late
        drainer = dict(allgroups)

        def ps(name):
            return bank[number[name] % 8]

        def wait_full(eng, name):
            eng.wait_ge(filled, number[name] + 1)

        def wait_drained(eng, name):
            eng.wait_ge(act_drained if drainer[name] == "act" else dve_drained, drain_count[name])

        def wait_bank(pe, name):
            n = number[name]
            if n >= 8 and not NGROUP <= n < NGROUP + 8:
                wait_drained(pe, allgroups[n - 8][0])

        class Chain:

            def __init__(self, eng, s):
                self.eng, self.sem, self.n = eng, s, 0

            def link(self, ins):
                self.n += 1
                ins.then_inc(self.sem, 1)
                self.eng.wait_ge(self.sem, self.n)

        ssum, rstd = tiny(6 * 3), tiny(6 * 3)
        fsum, frstd = tiny(6), tiny(6)
        bn, mv, lvar, lrstd = tiny(6 * NT), tiny(2 * NT), tiny(NT), tiny(NT)
        usum, urstd, rsum, rrstd = tiny(NT), tiny(NT), tiny(NT), tiny(NT)
        hb = tiny(16)
        nlam, lab, lexp, lden, ls, ls2, lpoly, sp = (tiny(8) for _ in range(8))
        c4, c2 = tiny(8), tiny(8)
        wt1, wt2 = tiny(NT), tiny(NT)
        slotf = tiny(2 * NT).rearrange("p (a i) -> p a i", a=2)
        first = taken[0]

        def tiny(n):
            at = taken[0] - first
            taken[0] += n
            assert at + n <= 5 * NTOK - 2900
            return regR[:, 2900 + at:2900 + at + n]

        logit = tiny(NT * 20).rearrange("p (i n) -> p i n", i=NT)
        gmax, gidx, gsum, gtop = tiny(NT), tiny(NT), tiny(NT), tiny(NT)
        gsh, gexp, gone = (tiny(NT * 4).rearrange("p (i n) -> p i n", i=NT) for _ in range(3))
        el, el2, one1, one2, cand = (tiny(NT * 4).rearrange("p (i n) -> p i n", i=NT) for _ in range(5))
        e16 = tiny(NT * NE).rearrange("p (i g e) -> p i g e", i=NT, g=NG)
        m1, m2, i1, i2, xe, den = (tiny(NT) for _ in range(6))
        work = [regR[:, j * 160:j * 160 + NT * NE] for j in range(10)]
        oh1, oh2, chose, prefix, rank, slotm, lt = (w.rearrange("p (i e) -> p i e", i=NT) for w in work[:7])
        pick = work[7].rearrange("p (i e) -> p i e", i=NT)
        choseb = sb("choseb", [P, NT * NE], BF16)
        nexp, over, incl, excl, base = (tiny(NE) for _ in range(5))
        oq = regR[:, 1600:1600 + 4 * NE].rearrange("p (q e) -> p q e", q=4)
        ojn = regR[:, 1700:1700 + MAX_OVER * NE].rearrange("p (j e) -> p j e", j=MAX_OVER)
        oj2 = regR[:, 1900:1900 + MAX_OVER * NE].rearrange("p (j e) -> p j e", j=MAX_OVER)
        jexp, jfirst, jcnt = (tiny(MAX_OVER) for _ in range(3))

        T_NUM, T_EXP, T_COUNT = 0, 1, 16

        def moe_slots(par):
            return (1, 2, 3) if par == 0 else (4, 5, 0)

        block = ctx.enter_context(nc.Block())

        @block.sync
        def _(sp):
            for i in range(NT):
                sp.dma_start(h[:, i, :], token_rows(x_prompt, x_sample, i)).then_inc(x_in[i], 16)

            def load_in(s, col):
                sp.dma_start(slot3(s), w_in[:, col:col + DR].rearrange("(k p) n -> p k n", p=P)).then_inc(ring_in[s], 16)

            load_in(0, 0)
            load_in(1, 3 * DR)
            load_in(2, 2 * DR)
            load_in(3, DR)
            sp.dma_start(slot3(4), w_out[:, 0:512].rearrange("(k p) n -> p k n", p=P)).then_inc(ring_in[4], 16)
            sp.wait_ge(consts, 15)
            more_rows = y_dram[NE * CAP:, :]
            whole = MAX_OVER * CAP // P
            sp.dma_start(more_rows[0:whole * P, :].rearrange("(a p) d -> p a d", p=P),
                         zeros.unsqueeze(1).to_broadcast([P, whole, D])).then_inc(zeroed, 16)
            sp.dma_start(more_rows[whole * P:, :], zeros[0:MAX_OVER * CAP - whole * P, :]).then_inc(zeroed, 16)
            wait_full(sp, f"xr{C4 - 1}1")
            sp.dma_start(slot3(0), w_out[:, 512:1024].rearrange("(k p) n -> p k n", p=P)).then_inc(ring_in[0], 16)

            def load_expert(par, e, waits):
                for s, src, wait in zip(moe_slots(par), (w_exp_gate, w_exp_up, w_exp_down), waits):
                    for sm, value in wait:
                        sp.wait_ge(sm, value)
                    w = src[bass.ds(e, 1), :, :].rearrange("a r n -> (a r) n")
                    if src is w_exp_down:
                        dst = ring[:, s, :].rearrange("p (k n) -> p k n", k=F4)
                    else:
                        dst = slot3(s)
                    sp.dma_start(dst, w.rearrange("(k p) n -> p k n", p=P)).then_inc(ring_in[s], 16)

            full = lambda name: (filled, number[name] + 1)
            load_expert(0, 0, ([full("v5")], [full("u5")], [full("gr31")]))
            load_expert(1, 1, ([full(f"out{NT - 1}1s")], [full("gate711"), (v_ready, NT)], [full(f"out{NT - 1}1s")]))
            with sp.Fori(1, NE // 2) as i:
                for par in range(2):
                    done = 2 * i + par - 1
                    gu, down = [(gu_full, 2 * done)], [(yhi_full, 2 * done)]
                    load_expert(par, 2 * i + par, (gu, gu, down))
            sp.wait_ge(routed, 1)
            more = sp.value_load(table[0:1, T_NUM:T_NUM + 1], min_val=0, max_val=MAX_OVER)
            with sp.If(more > 0):
                with sp.Fori(0, more) as j:
                    e = sp.value_load(table[0:1, bass.ds(j + T_EXP, 1)], min_val=0, max_val=NE - 1)
                    gu, down = [(gu_full, 2 * (NE + j))], [(yhi_full, 2 * (NE + j))]
                    load_expert(0, e, (gu, gu, down))
            sp.wait_ge(yhi_full, 2 * (NE + more))
            for a, s in enumerate((4, 5)):
                sp.dma_start(slot3(s), w_ple_gate[:, a * 512:(a + 1) * 512].rearrange("(k p) n -> p k n", p=P)).then_inc(ring_in[s], 16)
            sp.dma_start(ring[:, 0, 0:2 * D].rearrange("p (k n) -> p k n", k=2),
                         w_ple_proj.rearrange("(k p) n -> p k n", p=P)).then_inc(ring_in[0], 16)
            for i in range(NT):
                sp.wait_ge(norm_done, 3 * NT + i + 1)
                sp.dma_start(token_rows(y_prompt, y_sample, i), ntok[:, i, :]).then_inc(stored, 16)
            sp.wait_ge(stored, 16 * NT)

        @block.gpsimd
        def _(pool):
            nc.gpsimd.memset(wbd, 0.0).then_inc(consts, 1)
            nc.gpsimd.memset(zeros, 0.0).then_inc(consts, 1)
            nc.gpsimd.memset(ident[:], 0.0).then_inc(consts, 1)
            nc.gpsimd.memset(tri[:], 1.0).then_inc(consts, 1)
            pool.wait_ge(consts, 4)
            nc.gpsimd.affine_select(out=ident[:], in_=ident[:], compare_op=ALU.not_equal, fill=1.0, base=0,
                                    pattern=[[-1, P]], channel_multiplier=1).then_inc(consts, 1)
            nc.gpsimd.affine_select(out=tri[:], in_=tri[:], compare_op=ALU.is_gt, fill=0.0, base=0,
                                    pattern=[[1, P]], channel_multiplier=-1).then_inc(consts, 1)
            nc.gpsimd.memset(ones[:], 1.0).then_inc(consts, 1)
            nc.gpsimd.memset(onesb[:], 1.0).then_inc(consts, 1)
            nc.gpsimd.memset(nhalf, -0.5).then_inc(consts, 1)
            nc.gpsimd.memset(rankm[:, NE:NE + 2, :], -1.0).then_inc(consts, 1)
            nc.gpsimd.iota(iota[:], pattern=[[1, CAP]], base=0, channel_multiplier=0,
                           allow_small_or_imprecise_dtypes=True).then_inc(consts, 1)
            nc.gpsimd.iota(iota16[:], pattern=[[1, NE]], base=0, channel_multiplier=0,
                           allow_small_or_imprecise_dtypes=True).then_inc(consts, 1)
            nc.gpsimd.iota(iotaj, pattern=[[1, MAX_OVER]], base=0, channel_multiplier=0,
                           allow_small_or_imprecise_dtypes=True).then_inc(consts, 1)
            nc.gpsimd.iota(tokid[:, :, 0:1], pattern=[[0, NT], [0, 1]], base=0, channel_multiplier=1,
                           allow_small_or_imprecise_dtypes=True).then_inc(consts, 1)
            nc.gpsimd.iota(tokid[:, :, 1:2], pattern=[[P, NT], [0, 1]], base=0, channel_multiplier=0,
                           allow_small_or_imprecise_dtypes=True).then_inc(consts, 1)
            ch = Chain(pool, pool_seq)
            pool.wait_ge(consts, 15)

            def rstd_of(src, dst, n, scale, out_sem):
                ch.link(nc.gpsimd.tensor_scalar(src, src, scale, EPS, ALU.mult, ALU.add))
                nc.gpsimd.tensor_tensor(dst, src, nhalf[:, 0:n], ALU.pow).then_inc(out_sem, 1)

            def norm_rstd(k, tiles=range(NT)):
                for i in tiles:
                    pool.wait_ge(sumsq_done, k * NT + i + 1)
                    a = k * NT + i
                    rstd_of(ssum[:, a:a + 1], rstd[:, a:a + 1], 1, 1.0 / D, rstd_done)

            norm_rstd(0)
            for i in range(NT):
                pool.wait_ge(ln_var, i + 1)
                ch.link(nc.gpsimd.tensor_scalar(lvar[:, i:i + 1], mv[:, 2 * i + 1:2 * i + 2], 1.0, EPS, ALU.mult, ALU.add))
                nc.gpsimd.tensor_tensor(lrstd[:, i:i + 1], lvar[:, i:i + 1], nhalf[:, 0:1], ALU.pow).then_inc(ln_rstd, 1)
            pool.wait_ge(us_sq, NT)
            rstd_of(usum, urstd, NT, 1.0 / DR, us_rstd)
            wait_drained(pool, "ssq")
            rstd_of(rsum, rrstd, NT, 1.0 / DR, rr_rstd)
            norm_rstd(1)
            for i in range(NT):
                pool.wait_ge(n2_stored, 16 * (i + 1))

            def gather(r, par, ids_at):
                pool.wait_ge(ids_ready, 2 * (ids_at + 1))
                pool.sem_inc(gather_go, 1)
                nc.gpsimd.indirect_dma_start(moe["xg", par], None, n2_dram,
                                             bass.IndirectOffsetOnAxis(ap=idsi[:, par, 0:1], axis=0)).then_inc(gathered[par], 16)
                nc.gpsimd.indirect_dma_start(moe["xg2", par], None, n2_dram,
                                             bass.IndirectOffsetOnAxis(ap=idsi[0:CAP2, par, 1:2], axis=0)).then_inc(gathered[par], 16)

            wait_full(pool, "route")
            gather(0, 0, 0)
            gather(1, 1, 1)
            with pool.Fori(1, NE // 2 + 1) as i:
                for par in range(2):
                    r = 2 * i + par
                    pool.wait_ge(t_full, 3 * (r - 1))
                    gather(r, par, r)
            more = pool.value_load(table[0:1, T_NUM:T_NUM + 1], min_val=0, max_val=MAX_OVER)
            with pool.If(more > 0):
                with pool.Fori(0, more) as j:
                    pool.wait_ge(t_full, 3 * (NE + 1 + j))
                    gather(NE + j, 0, NE + 2 + j)
            pool.wait_ge(yhi_full, 2 * (NE + more))
            pool.wait_ge(y_stored[0], 32 * (NE // 2 + more))
            pool.wait_ge(y_stored[1], 32 * (NE // 2))
            pool.sem_inc(gather_go, 1)
            for i in range(NT):
                for a in range(2):
                    n = 2 * i + a
                    if n >= 4:
                        pool.wait_ge(moe_added, n - 3)
                    nc.gpsimd.indirect_dma_start(ring[:, 1, (n % 4) * D:(n % 4 + 1) * D], None, y_dram,
                                                 bass.IndirectOffsetOnAxis(ap=slots[:, a, i:i + 1], axis=0)).then_inc(yg_in[n % 4], 16)
                if i >= 2:
                    norm_rstd(2, [i - 2])
            norm_rstd(2, [NT - 2, NT - 1])
            for i in range(NT):
                pool.wait_ge(sumsq_done, 3 * NT + i + 1)
                rstd_of(fsum[:, i:i + 1], frstd[:, i:i + 1], 1, 1.0 / D, rstd_done)

        @block.tensor
        def _(pe):
            pe.wait_ge(consts, 15)

            def transposes(name, parts):
                wait_bank(pe, name)
                at = 0
                for src, n in parts:
                    q = nc.tensor.transpose(ps(name)[:src.shape[1], at:at + n], src, ident[0:n, 0:n])
                    at += n
                q.then_inc(filled, 1)

            def product(name, out, pairs):
                wait_bank(pe, name)
                for k, (a, b) in enumerate(pairs):
                    q = nc.tensor.matmul(out, a, b, start=(k == 0), stop=(k == len(pairs) - 1))
                q.then_inc(filled, 1)

            def norm_transposes(prefix, k):
                for i in range(NT):
                    pe.wait_ge(norm_done, k * NT + i + 1)
                    for j in range(2):
                        transposes(f"{prefix}{i}{j}", [(ntok[:, i, (4 * j + a) * P:(4 * j + a + 1) * P], P) for a in range(4)])

            pe.wait_ge(par_in, 16 * 8)
            transposes("par", [(par_rows[:, :], NPAR)])
            norm_transposes("nT", 0)
            for i in range(NT):
                for j in range(2):
                    wait_drained(pe, f"nT{i}{j}")
            pe.wait_ge(ring_in[0], 16)
            for c in range(C4):
                for s, (t0, n) in enumerate(SEGS):
                    name = f"xr{c}{s}"
                    product(name, ps(name)[:, 0:n], [(slot3(0)[:, k, c * P:(c + 1) * P], nT[:, k, t0:t0 + n]) for k in range(KD)])
            pe.wait_ge(ws_in, 16)
            for j in range(2):
                transposes(f"wsT{j}", [(w_s[:, 4 * j + a, :], P) for a in range(4)])

            def filler(name):
                if name[0] in "vu":
                    i, s = int(name[1]), 1 if name[0] == "v" else 2
                    pe.wait_ge(ring_in[s], 16)
                    product(name, ps(name)[:, :], [(nT[:, k, i * P:(i + 1) * P], slot3(s)[:, k, :]) for k in range(KD)])
                elif name[:3] == "mix":
                    hh = int(name[3])
                    if hh == 0:
                        pe.wait_ge(v_ready, NT)
                        wait_drained(pe, "wsT1")
                    product(name, ps(name)[:, 0:NT * HD].rearrange("p (i c) -> p i c", i=NT),
                            [(wsT[:, hh, :], v_tm[:, :, hh * HD:(hh + 1) * HD])])
                else:
                    c, s = int(name[2]), int(name[3])
                    t0, n = SEGS[s]
                    pe.wait_ge(ring_in[3], 16)
                    product(name, ps(name)[:, 0:n], [(slot3(3)[:, k, c * P:(c + 1) * P], nT[:, k, t0:t0 + n]) for k in range(KD)])

            for unit in range(8):
                c, d = unit // 2, unit % 2
                wait_drained(pe, f"xr{c}1")
                if unit == 0:
                    pe.wait_ge(wbd_in, 16 * 8)
                for g in range(2):
                    w = wbd[:, ((d * 2 + g) * C4 + c) * P:((d * 2 + g) * C4 + c + 1) * P]
                    for s, (t0, n) in enumerate(SEGS):
                        name = f"gate{unit}{g}{s}"
                        product(name, ps(name)[:, 0:n], [(w, xc[:, c, t0:t0 + n])])
                for name in fillers[unit]:
                    filler(name)
            for c in range(C4):
                for s, tiles in enumerate(((0, 1, 2, 3), (4, 5))):
                    if c == 0:
                        pe.wait_ge(us_scaled, tiles[-1] + 1)
                    transposes(f"ysT{c}{s}", [(u_tm[:, i, c * P:(c + 1) * P], P) for i in tiles])
            pe.wait_ge(rec_sq, C4)
            wait_bank(pe, "ssq")
            for i in range(NT):
                for c in range(C4):
                    q = nc.tensor.matmul(ps("ssq")[:, i:i + 1], gr[:, c, i * P:(i + 1) * P], ones[:, 0:1],
                                         start=(c == 0), stop=(c == C4 - 1))
            q.then_inc(filled, 1)
            pe.wait_ge(rec_g, C4)
            for c in range(C4):
                for s in range(2):
                    wait_drained(pe, f"ysT{c}{s}")
            pe.wait_ge(ring_in[4], 16)
            pe.wait_ge(ring_in[0], 32)
            for i in range(NT):
                for j in range(2):
                    w = slot3((4, 0)[j])
                    for g, src in (("r", xc), ("s", ysT)):
                        name = f"out{i}{j}{g}"
                        product(name, ps(name)[:, :], [(src[:, c, i * P:(i + 1) * P], w[:, (4 if g == "s" else 0) + c, :]) for c in range(C4)])
            norm_transposes("n2T", 1)
            pe.wait_ge(wr_in, 16 * 4)
            wait_bank(pe, "route")
            for i in range(NT):
                for j in range(2):
                    wait_drained(pe, f"n2T{i}{j}")
                for k in range(KD):
                    q = nc.tensor.matmul(ps("route")[:, i * 20:(i + 1) * 20], nT[:, k, i * P:(i + 1) * P], wr[:, k, :],
                                         start=(k == 0), stop=(k == KD - 1))
            q.then_inc(filled, 1)
            pe.wait_ge(chosen, 1)
            product("rank", ps("rank")[:, 0:NT * NE], [(tri[:], choseb[:])])
            product("total", ps("total")[:, 0:NT * NE], [(onesb[:], choseb[:])])
            wait_drained(pe, "total")
            wait_drained(pe, "n2T51")

            def ids(at):
                pe.wait_ge(onehot_ready, at + 1)
                if not (isinstance(at, int) and at == 0):
                    pe.wait_ge(ids_ready, 2 * at)
                for t in range(NT):
                    nc.tensor.matmul(bank[5][:, 0:2], onehot[:, t, 0:P], tokid[:, t, :], start=(t == 0), stop=(t == NT - 1))
                for t in range(NT):
                    q = nc.tensor.matmul(bank[5][0:CAP2, 2:4], onehot[:, t, P:CAP], tokid[:, t, :], start=(t == 0), stop=(t == NT - 1))
                q.then_inc(ids_full, 1)

            def turn(part, par, t_at):
                if not (isinstance(t_at, int) and t_at == 0 and part == 0):
                    pe.wait_ge(t_drained, 3 * t_at + part)
                    pe.sem_inc(turn_go, 1)
                for a in range(4 if part < 2 else KD):
                    if part < 2:
                        k = 4 * part + a
                        q = nc.tensor.transpose(bank[4][:, a * P:(a + 1) * P], moe["xg", par][:, k * P:(k + 1) * P], ident[:])
                    else:
                        q = nc.tensor.transpose(bank[4][:, a * CAP2:(a + 1) * CAP2], moe["xg2", par][:, a * P:(a + 1) * P], ident[0:CAP2, 0:CAP2])
                q.then_inc(t_full, 1)

            def hidden(f, par, n):
                sg, su, _ = moe_slots(par)
                half, col = f // 2, (f % 2) * 256
                for b, s in ((2 * half, sg), (2 * half + 1, su)):
                    for k in range(KD):
                        q = nc.tensor.matmul(bank[b][:, col:col + n], slot3(s)[:, k, f * P:(f + 1) * P], moe["xT", par][:, k, 0:n],
                                             start=(k == 0), stop=(k == KD - 1))
                return q

            def down(par, lo, n, j):
                w = ring[:, moe_slots(par)[2], :].rearrange("p (k n) -> p k n", k=F4)
                for f in range(F4):
                    q = nc.tensor.matmul(bank[6 + j][0:n, :], hid[:, f, lo:lo + n], w[:, f, j * 512:(j + 1) * 512],
                                         start=(f == 0), stop=(f == F4 - 1))
                return q

            def by_size(count, body):
                with pe.If(count < 97):
                    body(96)
                with pe.Else():
                    with pe.If(count < 129):
                        body(P)
                    with pe.Else():
                        body(CAP)

            def one_round(r, par, loads, prev_hidden, turn_next):
                count = pe.value_load(table[0:1, bass.ds(r + T_COUNT, 1)], min_val=0, max_val=NTOK)
                sg, su, sd = moe_slots(par)
                pe.wait_ge(t_drained, 3 * (turn_next[1] if turn_next else r + 1))
                pe.wait_ge(ring_in[sg], loads[0])
                pe.wait_ge(ring_in[su], loads[1])
                for half in range(2):
                    if prev_hidden is not None:
                        pe.wait_ge(hid_done, 2 * prev_hidden + half + 1)

                    def body(n, half=half):
                        hidden(2 * half, par, n)
                        hidden(2 * half + 1, par, n).then_inc(gu_full, 1)
                    by_size(count, body)
                    if turn_next:
                        if half == 0:
                            pe.wait_ge(gathered[1 - par], turn_next[2])
                            ids(r + 2)
                        turn(half, 1 - par, turn_next[1])
                if turn_next:
                    turn(2, 1 - par, turn_next[1])
                pe.wait_ge(ring_in[sd], loads[2])
                pe.wait_ge(hid_done, 2 * (r + 1))
                if prev_hidden is not None:
                    pe.wait_ge(ylo_drained, 2 * r)
                    pe.wait_ge(yhi_drained, 2 * r)
                down(par, 0, P, 0).then_inc(ylo_full, 1)
                down(par, 0, P, 1).then_inc(yhi_full, 1)
                pe.wait_ge(ylo_drained, 2 * r + 1)
                pe.wait_ge(yhi_drained, 2 * r + 1)
                with pe.If(count < 129):
                    pe.sem_inc(ylo_full, 1)
                    pe.sem_inc(yhi_full, 1)
                with pe.Else():
                    down(par, P, CAP2, 0).then_inc(ylo_full, 1)
                    down(par, P, CAP2, 1).then_inc(yhi_full, 1)

            before = {0: 2, 1: 1, 2: 1, 3: 1, 4: 1, 5: 0}

            pe.wait_ge(routed, 1)
            ids(0)
            ids(1)
            pe.wait_ge(gathered[0], 32)
            for part in range(3):
                turn(part, 0, 0)

            def main_round(i, par, first):
                r = 2 * i + par
                loads = [16 * (before[s] + 1 + i) for s in moe_slots(par)]
                count = 32 * (i + 1) if par == 0 else 32 * (i + 2)
                one_round(r, par, loads, None if first else r - 1, (None, r + 1, count))

            main_round(0, 0, True)
            main_round(0, 1, False)
            with pe.Fori(1, NE // 2) as i:
                main_round(i, 0, False)
                main_round(i, 1, False)
            more = pe.value_load(table[0:1, T_NUM:T_NUM + 1], min_val=0, max_val=MAX_OVER)
            with pe.If(more > 0):
                with pe.Fori(0, more) as j:
                    ids(NE + 2 + j)
                    pe.wait_ge(gathered[0], 32 * (NE // 2 + 2 + j))
                    for part in range(3):
                        turn(part, 0, NE + 1 + j)
                    pe.wait_ge(t_drained, 3 * (NE + 2 + j))
                    one_round(NE + j, 0, [16 * (before[s] + 1 + NE // 2 + j) for s in moe_slots(0)], NE - 1 + j, None)
            pe.wait_ge(ylo_drained, 2 * (NE + more))
            pe.wait_ge(yhi_drained, 2 * (NE + more))
            pe.wait_ge(t_drained, 3 * (NE + 1 + more))
            pe.wait_ge(ids_ready, 2 * (NE + 2 + more))
            pe.wait_ge(gathered[1], 32 * (NE // 2 + 1))
            norm_transposes("n3T", 2)
            pe.wait_ge(p_in, 16 * NT)
            for k in range(2):
                for s, tiles in enumerate(((0, 1, 2, 3), (4, 5))):
                    transposes(f"pT{k}{s}", [(p_tm[:, i, k * P:(k + 1) * P], P) for i in tiles])
            for i in range(NT):
                for j in range(2):
                    wait_drained(pe, f"n3T{i}{j}")
            for k in range(2):
                for s in range(2):
                    wait_drained(pe, f"pT{k}{s}")
            pe.wait_ge(ring_in[4], 16 * (1 + NE // 2 + 1))
            pe.wait_ge(ring_in[5], 16 * (NE // 2 + 1))
            pe.wait_ge(ring_in[0], 16 * (2 + NE // 2 + 1))
            for i in range(NT):
                for j in range(2):
                    name = f"pg{i}{j}"
                    product(name, ps(name)[:, :], [(nT[:, k, i * P:(i + 1) * P], slot3((4, 5)[j])[:, k, :]) for k in range(KD)])
                    name = f"pp{i}{j}"
                    product(name, ps(name)[:, :], [(pT[:, k, i * P:(i + 1) * P], ring[:, 0, k * D + j * 512:k * D + (j + 1) * 512]) for k in range(2)])


        @block.scalar
        def _(act):
            rows = lambda w, pat, **kw: w.rearrange(pat, **kw)
            for at_row, src in ((CONV_W, rows(conv_w, "k (c p) -> (k c) p", p=P)), (CONV_B, rows(conv_b, "o (c p) -> (o c) p", p=P)),
                                (B_A, rows(lru_b_a, "d (c p) -> (d c) p", p=P)), (B_X, rows(lru_b_x, "d (c p) -> (d c) p", p=P)),
                                (LAM, rows(lru_lambda, "d (c p) -> (d c) p", p=P)), (G_REC, rows(g_rec_out, "o (c p) -> (o c) p", p=P)),
                                (G_SGU, rows(g_sgu_out, "o (c p) -> (o c) p", p=P)), (B_S, sgu_b_s)):
                act.dma_start(par_rows[at_row:at_row + src.shape[0], :], src).then_inc(par_in, 16)
            act.dma_start(gB[:], g_mix[0].partition_broadcast(P)).then_inc(gB_in, 16)
            act.wait_ge(consts, 1)
            for g, src in enumerate((lru_w_a, lru_w_x)):
                for d in range(2):
                    for half in range(2):
                        lo = half * HD
                        dst = wbd[lo:lo + HD, (d * 2 + g) * C4 * P:(d * 2 + g + 1) * C4 * P].rearrange("i (c j) -> i c j", c=C4)[:, :, lo:lo + HD]
                        act.dma_start(dst, src[d].rearrange("(c s) i j -> s i c j", s=2)[half]).then_inc(wbd_in, 16)
            act.dma_start(w_s, sgu_w_s.rearrange("h t s -> t h s")).then_inc(ws_in, 16)
            act.dma_start(ln_g, sgu_ln_g[0].partition_broadcast(P)).then_inc(ln_in, 16)
            act.dma_start(ln_b, sgu_ln_b[0].partition_broadcast(P)).then_inc(ln_in, 16)
            act.dma_start(wr[:, :, 0:NG], w_router_group.rearrange("(k p) n -> p k n", p=P)).then_inc(wr_in, 16)
            act.dma_start(wr[:, :, NG:], w_router_expert.rearrange("(k p) n -> p k n", p=P)).then_inc(wr_in, 16)
            act.dma_start(br[:, 0:NG], b_router_group[0].partition_broadcast(P)).then_inc(wr_in, 16)
            act.dma_start(br[:, NG:], b_router_expert[0].partition_broadcast(P)).then_inc(wr_in, 16)
            ch = Chain(act, act_seq)

            def sumsq(k, i, dst, ready, value):
                act.wait_ge(ready, value)
                nc.scalar.activation(ntok[:, i, :], h[:, i, :], ACT.Square, accum_out=dst).then_inc(sumsq_done, 1)

            def drain(name, out, func=ACT.Identity, view=None, **kw):
                wait_full(act, name)
                nc.scalar.activation(out, ps(name)[:, 0:out.free_size()] if view is None else view, func, **kw).then_inc(act_drained, 1)

            def drain_norm(prefix):
                for i in range(NT):
                    name = f"{prefix}{i}1"
                    drain(name, nT[:, 4:8, i * P:(i + 1) * P], view=ps(name)[:, :].rearrange("p (k t) -> p k t", k=4))

            for i in range(NT):
                sumsq(0, i, ssum[:, i:i + 1], x_in[i], 16)
            act.wait_ge(halves_ready, 1)
            nc.scalar.activation(lexp, lab, ACT.Exp, scale=-1.0).then_inc(exp_lam, 1)
            drain_norm("nT")
            act.wait_ge(norm_done, NT)
            act.dma_start(gB[:], g_ffn[0].partition_broadcast(P)).then_inc(gB_in, 16)
            for j in range(2):
                name = f"wsT{j}"
                drain(name, wsT[:, 4 * j:4 * j + 4, :], view=ps(name)[:, :].rearrange("p (h t) -> p h t", h=4))

            def fill(name):
                if name[0] == "v":
                    drain(name, v_tm[:, int(name[1]), :], ACT.Gelu_apprx_tanh)
                elif name[0] == "u":
                    drain(name, u_tm[:, int(name[1]), :], ACT.Gelu_apprx_tanh)
                elif name[:2] == "gr":
                    t0, n = SEGS[int(name[3])]
                    wait_full(act, "mix7")
                    drain(name, gr[:, int(name[2]), t0:t0 + n], ACT.Gelu_apprx_tanh)

            for unit in range(8):
                c, d = unit // 2, unit % 2
                col = d * C4 + c
                if unit == 0:
                    act.wait_ge(decay_ready, 1)
                    act.wait_ge(zeroed, 32)
                else:
                    act.wait_ge(scan_part, 2 * unit)
                    if unit >= 2:
                        act.wait_ge(rec_sum, unit // 2)
                for g, dst in enumerate((TR, TI)):
                    for s, (t0, n) in enumerate(SEGS):
                        drain(f"gate{unit}{g}{s}", dst[:, t0:t0 + n], ACT.Tanh, scale=0.5, bias=hb[:, g * 8 + col:g * 8 + col + 1])
                act.wait_ge(act_drained, drain_count[f"gate{unit}01"])
                nc.scalar.activation(A0, TR, ACT.Exp, scale=c4[:, col:col + 1], bias=c4[:, col:col + 1]).then_inc(rec_exp, 1)
                nc.scalar.activation(TT, TR, ACT.Tanh, scale=c2[:, col:col + 1], bias=c2[:, col:col + 1]).then_inc(rec_exp, 1)
                for name in fillers[unit]:
                    fill(name)
                act.wait_ge(rec_m2, unit + 1)
                nc.scalar.activation(TR, TR, ACT.Sqrt, scale=0.25).then_inc(rec_mult, 1)
                if unit == 6:
                    for i in range(NT):
                        act.wait_ge(dve_drained, drain_count["mix7"])
                        nc.scalar.activation(v_tm[:, i, :], u_tm[:, i, :], ACT.Square, accum_out=usum[:, i:i + 1]).then_inc(us_sq, 1)
                        act.wait_ge(us_sq, i + 1)
            for c in range(C4):
                drain(f"ysT{c}1", ysT[:, c, 512:768], scale=chan[:, G_SGU + c:G_SGU + c + 1])
            for c in range(C4):
                act.wait_ge(rec_y, c + 1)
                nc.scalar.activation(gr[:, c, :], xc[:, c, :], ACT.Square).then_inc(rec_sq, 1)
            wait_full(act, "ssq")
            for i in range(NT):
                sumsq(1, i, ssum[:, NT + i:NT + i + 1], dve_drained, drain_count[f"out{i}1s"])
            for i in range(NT):
                act.wait_ge(norm_done, NT + i + 1)
                act.dma_start(n2_dram[i * P:(i + 1) * P, :], ntok[:, i, :]).then_inc(n2_stored, 16)
                act.wait_ge(n2_stored, 16 * (i + 1))
            act.dma_start(gB[:], g_ple[0].partition_broadcast(P)).then_inc(gB_in, 16)
            drain_norm("n2T")
            act.wait_ge(route_max, 1)
            nc.scalar.activation(gexp, gsh, ACT.Exp).then_inc(route_exp, 1)
            nc.scalar.activation(xe, m2, ACT.Exp).then_inc(route_exp, 1)

            def turned(part, par, t_at):
                act.wait_ge(t_full, 3 * t_at + part + 1)
                if part < 2:
                    nc.scalar.activation(moe["xT", par][:, 4 * part:4 * part + 4, 0:P],
                                         bank[4][:, :].rearrange("p (k s) -> p k s", k=4), ACT.Copy).then_inc(t_drained, 1)
                else:
                    nc.scalar.activation(moe["xT", par][:, :, P:CAP],
                                         bank[4][:, 0:KD * CAP2].rearrange("p (k s) -> p k s", k=KD), ACT.Copy).then_inc(t_drained, 1)

            def silu_half(r, half, first):
                act.wait_ge(gu_full, 2 * r + half + 1)
                if not first:
                    act.wait_ge(hid_done, 2 * r - 1 + half)
                nc.scalar.activation(silu[:, 2 * half:2 * half + 2, :],
                                     bank[2 * half][:, :].rearrange("p (f s) -> p f s", f=2)[:, :, 0:CAP], ACT.Silu).then_inc(silu_done, 1)

            def y_out(r, par, first, store_count):
                act.wait_ge(yhi_full, 2 * r + 1)
                if store_count is not None:
                    act.wait_ge(y_stored[par], store_count)
                nc.scalar.activation(moe["y", par][:, 512:D], bank[7][:, :], ACT.Copy).then_inc(yhi_drained, 1)
                act.wait_ge(yhi_full, 2 * r + 2)
                nc.scalar.activation(moe["y2", par][:, 512:D], bank[7][0:CAP2, :], ACT.Copy).then_inc(yhi_drained, 1)
                act.wait_ge(yhi_drained, 2 * r + 2)
                act.wait_ge(ylo_drained, 2 * r + 2)
                act.dma_start(y_dram[bass.ds(r * CAP, P), :], moe["y", par]).then_inc(y_stored[par], 16)
                act.dma_start(y_dram[bass.ds(r * CAP + P, CAP2), :], moe["y2", par]).then_inc(y_stored[par], 16)

            def main_round(i, par, first):
                r = 2 * i + par
                silu_half(r, 0, first)
                turned(0, 1 - par, r + 1)
                turned(1, 1 - par, r + 1)
                silu_half(r, 1, first)
                turned(2, 1 - par, r + 1)
                y_out(r, par, first, None if isinstance(i, int) else 32 * i)

            for part in range(3):
                turned(part, 0, 0)
            main_round(0, 0, True)
            main_round(0, 1, False)
            with act.Fori(1, NE // 2) as i:
                main_round(i, 0, False)
                main_round(i, 1, False)
            more = act.value_load(table[0:1, T_NUM:T_NUM + 1], min_val=0, max_val=MAX_OVER)
            with act.If(more > 0):
                with act.Fori(0, more) as j:
                    for part in range(3):
                        turned(part, 0, NE + 1 + j)
                    silu_half(NE + j, 0, False)
                    silu_half(NE + j, 1, False)
                    y_out(NE + j, 0, False, 32 * (NE // 2 + j))
            for i in range(NT):
                act.dma_start(p_tm[:, i, :], token_rows(p_prompt, p_sample, i)).then_inc(p_in, 16)
            act.wait_ge(y_stored[0], 32 * (NE // 2 + more))
            act.wait_ge(y_stored[1], 32 * (NE // 2))
            for i in range(NT):
                sumsq(2, i, ssum[:, 2 * NT + i:2 * NT + i + 1], moe_added, 2 * (i + 1))
            drain_norm("n3T")
            for k in range(2):
                drain(f"pT{k}1", pT[:, k, 512:768])
            act.wait_ge(norm_done, 3 * NT)
            act.dma_start(gB[:], g_final.partition_broadcast(P)).then_inc(gB_in, 16)
            for i in range(NT):
                for j in range(2):
                    n = 2 * i + j
                    name = f"pg{i}{j}"
                    if n >= 2:
                        wait_drained(act, f"pp{(n - 2) // 2}{n % 2}")
                    wait_full(act, name)
                    nc.scalar.activation(sig[:, n % 2, :], ps(name)[:, :], ACT.Sigmoid).then_inc(act_drained, 1)
                sumsq(3, i, fsum[:, i:i + 1], h_ready, 2 * (i + 1))


        @block.vector
        def _(dve):
            ch = Chain(dve, dve_seq)
            link = ch.link
            V = nc.vector

            def drain(name, make):
                wait_full(dve, name)
                make(ps(name)).then_inc(dve_drained, 1)

            def normalise(k, i, gain_loads, src, scale):
                dve.wait_ge(rstd_done, k * NT + i + 1)
                dve.wait_ge(gB_in, 16 * gain_loads)
                V.scalar_tensor_tensor(out=ntok[:, i, :], in0=h[:, i, :], scalar=scale[:, src:src + 1], in1=gB[:],
                                       op0=ALU.mult, op1=ALU.mult).then_inc(norm_done, 1)

            def drain_norm(prefix):
                for i in range(NT):
                    drain(f"{prefix}{i}0", lambda b, i=i: V.tensor_copy(nT[:, 0:4, i * P:(i + 1) * P], b[:, :].rearrange("p (k t) -> p k t", k=4)))

            drain("par", lambda b: V.tensor_copy(chan[:, :], b[:, 0:NPAR]))
            dve.wait_ge(dve_drained, 1)
            link(V.tensor_scalar(nlam, chan[:, LAM:LAM + 8], -1.0, None, ALU.mult))
            V.tensor_tensor(lab, chan[:, LAM:LAM + 8], nlam, ALU.max).then_inc(halves_ready, 1)
            link(V.tensor_scalar(hb, chan[:, B_A:B_A + 16], 0.5, None, ALU.mult))
            for i in range(NT):
                normalise(0, i, 1, i, rstd)
            dve.wait_ge(exp_lam, 1)
            link(V.tensor_scalar(lden, lexp, 2.0, None, ALU.add))
            link(V.reciprocal(lden, lden))
            link(V.tensor_tensor(ls, lexp, lden, ALU.mult))
            link(V.tensor_tensor(ls2, ls, ls, ALU.mult))
            link(V.tensor_scalar(lpoly, ls2, 1.0 / 15, 1.0 / 13, ALU.mult, ALU.add))
            for n in (11, 9, 7, 5, 3, 1):
                link(V.tensor_tensor(lpoly, lpoly, ls2, ALU.mult))
                link(V.tensor_scalar(lpoly, lpoly, 1.0 / n, None, ALU.add))
            link(V.scalar_tensor_tensor(out=lpoly, in0=lpoly, scalar=2.0, in1=ls, op0=ALU.mult, op1=ALU.mult))
            link(V.scalar_tensor_tensor(out=sp, in0=nlam, scalar=0.0, in1=lpoly, op0=ALU.max, op1=ALU.add))
            link(V.tensor_scalar(c4, sp, -4.0, None, ALU.mult))
            V.tensor_scalar(c2, sp, 2.0, None, ALU.mult).then_inc(decay_ready, 1)
            drain_norm("nT")
            for c in range(C4):
                for s, (t0, n) in enumerate(SEGS):
                    name = f"xr{c}{s}"
                    wait_full(dve, name)
                    x = ps(name)
                    tap = lambda k: chan[:, CONV_W + k * C4 + c:CONV_W + k * C4 + c + 1]
                    o = xc[:, c, t0:t0 + n]
                    link(V.tensor_scalar(o, x[:, 0:n], tap(2), chan[:, CONV_B + c:CONV_B + c + 1], ALU.mult, ALU.add))
                    link(V.scalar_tensor_tensor(out=o[:, 1:n], in0=x[:, 0:n - 1], scalar=tap(1), in1=o[:, 1:n], op0=ALU.mult, op1=ALU.add))
                    link(V.scalar_tensor_tensor(out=o[:, 2:n], in0=x[:, 0:n - 2], scalar=tap(0), in1=o[:, 2:n], op0=ALU.mult, op1=ALU.add))
                    V.scalar_tensor_tensor(out=o[:, 0:n - 1], in0=x[:, 1:n], scalar=tap(3), in1=o[:, 0:n - 1],
                                           op0=ALU.mult, op1=ALU.add).then_inc(dve_drained, 1)

            def fill(name):
                if name[0] == "v":
                    i = int(name[1])
                    v = v_tm[:, i, :]
                    dve.wait_ge(act_drained, drain_count[name])
                    dve.wait_ge(ln_in, 32)
                    link(V.bn_stats(bn[:, 6 * i:6 * i + 6], v))
                    V.bn_aggr(mv[:, 2 * i:2 * i + 2], bn[:, 6 * i:6 * i + 6]).then_inc(ln_var, 1)
                    dve.wait_ge(ln_rstd, i + 1)
                    link(V.tensor_scalar(v, v, mv[:, 2 * i:2 * i + 1], lrstd[:, i:i + 1], ALU.subtract, ALU.mult))
                    link(V.tensor_tensor(v, v, ln_g, ALU.mult))
                    V.tensor_tensor(v, v, ln_b, ALU.add).then_inc(v_ready, 1)
                elif name[:3] == "mix":
                    hh = int(name[3])
                    if hh == 0:
                        dve.wait_ge(act_drained, drain_count["u5"])
                    uu = u_tm[:, :, hh * HD:(hh + 1) * HD]
                    drain(name, lambda b: V.scalar_tensor_tensor(out=uu, in0=b[:, 0:NT * HD].rearrange("p (i c) -> p i c", i=NT),
                                                                 scalar=chan[:, B_S + hh:B_S + hh + 1], in1=uu, op0=ALU.add, op1=ALU.mult))

            for unit in range(8):
                c, d = unit // 2, unit % 2
                dve.wait_ge(act_drained, drain_count[f"gate{unit}11"])
                link(V.scalar_tensor_tensor(out=TI, in0=TI, scalar=1.0, in1=xc[:, c, :], op0=ALU.add, op1=ALU.mult))
                dve.wait_ge(rec_exp, 2 * (unit + 1))
                link(V.scalar_tensor_tensor(out=TT, in0=A0, scalar=1.0, in1=TT, op0=ALU.add, op1=ALU.mult))
                link(V.tensor_scalar(A0, TT, -1.0, 1.0, ALU.mult, ALU.add))
                V.scalar_tensor_tensor(out=TR, in0=A0, scalar=1.0, in1=TT, op0=ALU.add, op1=ALU.mult).then_inc(rec_m2, 1)
                for name in fillers[unit]:
                    fill(name)
                dve.wait_ge(rec_mult, unit + 1)
                link(V.tensor_tensor(TI, TI, TR, ALU.mult))
                for s, (t0, n) in enumerate(SEGS):
                    if d == 0:
                        q = V.tensor_tensor_scan(HF[:, t0:t0 + n], A0[:, t0:t0 + n], TI[:, t0:t0 + n], 0.0, ALU.mult, ALU.add)
                    else:
                        rev = slice(t0 + n - 1, t0 - 1 if t0 else None, -1)
                        q = V.tensor_tensor_scan(TT[:, rev], A0[:, rev], TI[:, rev], 0.0, ALU.mult, ALU.add)
                    q.then_inc(scan_part, 1)
                dve.wait_ge(scan_part, 2 * (unit + 1))
                if d == 1:
                    V.tensor_tensor(xc[:, c, :], HF, TT, ALU.add).then_inc(rec_sum, 1)
                if unit == 6:
                    dve.wait_ge(us_rstd, 1)
                    for i in range(NT):
                        V.tensor_scalar(u_tm[:, i, :], u_tm[:, i, :], urstd[:, i:i + 1], None, ALU.mult).then_inc(us_scaled, 1)
            for c in range(C4):
                drain(f"ysT{c}0", lambda b, c=c: V.tensor_scalar(ysT[:, c, 0:512], b[:, :], chan[:, G_SGU + c:G_SGU + c + 1], None, ALU.mult))
            for c in range(C4):
                dve.wait_ge(rec_sum, c + 1)
                dve.wait_ge(act_drained, drain_count[f"gr{c}1"])
                V.tensor_tensor(xc[:, c, :], xc[:, c, :], gr[:, c, :], ALU.mult).then_inc(rec_y, 1)
            for c in range(C4):
                dve.wait_ge(rec_sq, c + 1)
                dve.wait_ge(rec_y, c + 1)
                V.tensor_scalar(xc[:, c, :], xc[:, c, :], chan[:, G_REC + c:G_REC + c + 1], None, ALU.mult).then_inc(rec_g, 1)
            drain("ssq", lambda b: V.tensor_copy(rsum, b[:, 0:NT]))
            for i in range(NT):
                if i == 0:
                    dve.wait_ge(rr_rstd, 1)
                for j in range(2):
                    hs = h[:, i, j * 512:(j + 1) * 512]
                    drain(f"out{i}{j}r", lambda b: V.scalar_tensor_tensor(out=hs, in0=b[:, :], scalar=rrstd[:, i:i + 1], in1=hs, op0=ALU.mult, op1=ALU.add))
                    dve.wait_ge(dve_drained, drain_count[f"out{i}{j}r"])
                    drain(f"out{i}{j}s", lambda b: V.tensor_tensor(hs, b[:, :], hs, ALU.add))
                    dve.wait_ge(dve_drained, drain_count[f"out{i}{j}s"])
                if i >= 1:
                    normalise(1, i - 1, 2, NT + i - 1, rstd)
            normalise(1, NT - 1, 2, 2 * NT - 1, rstd)
            drain_norm("n2T")

            b3 = lambda a: a.unsqueeze(2).to_broadcast([P, NT, 4])
            idx4 = iota[:, 0:4].unsqueeze(1).to_broadcast([P, NT, 4])
            dve.wait_ge(wr_in, 64)
            drain("route", lambda b: V.tensor_tensor(logit, b[:, 0:NT * 20].rearrange("p (i n) -> p i n", i=NT),
                                                     br[:, :].unsqueeze(1).to_broadcast([P, NT, 20]), ALU.add))
            dve.wait_ge(dve_drained, drain_count["route"])

            def first_max(x, mx, idx, onehot4):
                link(V.tensor_reduce(mx, x, AX.X, ALU.max))
                link(V.tensor_tensor(cand, x, b3(mx), ALU.is_equal))
                link(V.scalar_tensor_tensor(out=cand, in0=cand, scalar=-4.0, in1=idx4, op0=ALU.mult, op1=ALU.add))
                link(V.tensor_reduce(idx, cand, AX.X, ALU.min))
                link(V.tensor_scalar(idx, idx, 4.0, None, ALU.add))
                link(V.tensor_tensor(onehot4, idx4, b3(idx), ALU.is_equal))

            first_max(logit[:, :, 0:NG], gmax, gidx, gone)
            link(V.tensor_tensor(gsh, logit[:, :, 0:NG], b3(gmax), ALU.subtract))
            link(V.tensor_tensor(e16, logit[:, :, NG:].rearrange("p i (g e) -> p i g e", g=NG),
                                 gone.unsqueeze(3).to_broadcast([P, NT, NG, NEG]), ALU.mult))
            link(V.tensor_reduce(el, e16.rearrange("p i g e -> p i e g"), AX.X, ALU.add))
            first_max(el, m1, i1, one1)
            link(V.scalar_tensor_tensor(out=el2, in0=one1, scalar=MASKED, in1=el, op0=ALU.mult, op1=ALU.add))
            first_max(el2, m2, i2, one2)
            V.tensor_tensor(m2, m2, m1, ALU.subtract).then_inc(route_max, 1)
            dve.wait_ge(route_max, 1)
            for oh, one in ((oh1, one1), (oh2, one2)):
                o4 = oh.rearrange("p i (g e) -> p i g e", g=NG)
                link(V.tensor_copy(o4, gone.unsqueeze(3).to_broadcast([P, NT, NG, NEG])))
                link(V.tensor_tensor(o4, o4, one.unsqueeze(2).to_broadcast([P, NT, NG, NEG]), ALU.mult))
            link(V.tensor_tensor(chose, oh1, oh2, ALU.add))
            V.tensor_copy(choseb[:].rearrange("p (i e) -> p i e", i=NT), chose).then_inc(chosen, 1)
            dve.wait_ge(route_exp, 2)
            link(V.tensor_reduce(gsum, gexp, AX.X, ALU.add))
            link(V.tensor_scalar(den, xe, 1.0, None, ALU.add))
            link(V.tensor_tensor(den, den, gsum, ALU.mult))
            link(V.reciprocal(wt1, den))
            link(V.tensor_tensor(wt2, wt1, xe, ALU.mult))
            drain("rank", lambda b: V.tensor_copy(rank, b[:, 0:NT * NE].rearrange("p (i e) -> p i e", i=NT)))
            drain("total", lambda b: V.tensor_copy(pick, b[:, 0:NT * NE].rearrange("p (i e) -> p i e", i=NT)))
            dve.wait_ge(dve_drained, drain_count["total"])
            link(V.memset(prefix[:, 0, :], 0.0))
            for i in range(1, NT):
                link(V.tensor_tensor(prefix[:, i, :], prefix[:, i - 1, :], pick[:, i - 1, :], ALU.add))
            link(V.tensor_tensor(nexp, prefix[:, NT - 1, :], pick[:, NT - 1, :], ALU.add))
            link(V.tensor_tensor(rank, rank, prefix, ALU.add))
            for q in range(4):
                link(V.tensor_scalar(oq[:, q, :], nexp, float(CAP * (q + 1)), None, ALU.is_gt))
            link(V.tensor_reduce(over, oq.rearrange("p q e -> p e q"), AX.X, ALU.add))
            link(V.memset(base, 1.0))
            link(V.tensor_tensor_scan(incl, base, over, 0.0, ALU.mult, ALU.add))
            link(V.tensor_tensor(excl, incl, over, ALU.subtract))
            link(V.tensor_scalar(base, excl, float(CAP), float((NE - 1) * CAP), ALU.mult, ALU.add))
            link(V.tensor_scalar(lt, rank, float(CAP), None, ALU.is_lt))
            bE = lambda a: a.unsqueeze(1).to_broadcast([P, NT, NE])
            link(V.tensor_scalar(slotm, bE(iota16[:]), float(CAP), None, ALU.mult))
            link(V.tensor_tensor(slotm, slotm, bE(base), ALU.subtract))
            link(V.tensor_tensor(slotm, slotm, lt, ALU.mult))
            link(V.tensor_tensor(slotm, slotm, bE(base), ALU.add))
            link(V.tensor_tensor(slotm, slotm, rank, ALU.add))
            for a, oh in enumerate((oh1, oh2)):
                link(V.tensor_tensor(pick, oh, slotm, ALU.mult))
                link(V.tensor_reduce(slotf[:, a, :], pick, AX.X, ALU.add))
                link(V.tensor_copy(slots[:, a, :], slotf[:, a, :]))
            link(V.scalar_tensor_tensor(out=rank, in0=rank, scalar=1.0, in1=chose, op0=ALU.add, op1=ALU.mult))
            link(V.tensor_scalar(rankm[:, 0:NE, :], rank.rearrange("p i e -> p e i"), -1.0, None, ALU.add))
            bJ = lambda a: a.unsqueeze(1).to_broadcast([P, MAX_OVER, NE])
            jE = lambda a: a.unsqueeze(2).to_broadcast([P, MAX_OVER, NE])
            link(V.tensor_tensor(ojn, bJ(incl), jE(iotaj), ALU.is_le))
            link(V.tensor_reduce(jexp, ojn, AX.X, ALU.add))
            link(V.tensor_tensor(ojn, bJ(iota16[:]), jE(jexp), ALU.is_equal))
            link(V.tensor_tensor(oj2, ojn, bJ(excl), ALU.mult))
            link(V.tensor_reduce(jfirst, oj2, AX.X, ALU.add))
            link(V.tensor_tensor(oj2, ojn, bJ(nexp), ALU.mult))
            link(V.tensor_reduce(jcnt, oj2, AX.X, ALU.add))
            link(V.tensor_tensor(jfirst, iotaj, jfirst, ALU.subtract))
            link(V.tensor_scalar(offs[:], jfirst, 1.0, float(CAP), ALU.add, ALU.mult))
            link(V.tensor_tensor(jcnt, jcnt, offs[:], ALU.subtract))
            link(V.tensor_scalar(jcnt, jcnt, 0.0, None, ALU.max))
            link(V.tensor_scalar(jexp, jexp, float(NE - 1), None, ALU.min))
            link(V.memset(table[:], 0))
            link(V.tensor_copy(table[:, T_NUM:T_NUM + 1], incl[:, NE - 1:NE]))
            link(V.tensor_copy(table[:, T_EXP:T_EXP + MAX_OVER], jexp))
            link(V.tensor_copy(table[:, T_COUNT:T_COUNT + NE], nexp))
            V.tensor_copy(table[:, T_COUNT + NE:T_COUNT + NROUND], jcnt).then_inc(routed, 1)

            for b in range(4):
                link(V.memset(bank[b][:, :], 0.0))

            def make_onehot(at, e, ramp):
                if not (isinstance(at, int) and at == 0):
                    dve.wait_ge(ids_full, at)
                V.tensor_tensor(onehot, ramp.unsqueeze(1).to_broadcast([P, NT, CAP]),
                                rankm[:, bass.ds(e, 1), :].rearrange("p a i -> p (a i)").unsqueeze(2).to_broadcast([P, NT, CAP]),
                                ALU.is_equal).then_inc(onehot_ready, 1)

            def take_ids(at, par, gathered_before):
                dve.wait_ge(ids_full, at + 1)
                if gathered_before is not None:
                    dve.wait_ge(gathered[par], gathered_before)
                V.tensor_reduce(idsf[:, par, 0:1], bank[5][:, 0:2], AX.X, ALU.add).then_inc(ids_sum, 1)
                V.tensor_reduce(idsf[0:CAP2, par, 1:2], bank[5][0:CAP2, 2:4], AX.X, ALU.add).then_inc(ids_sum, 1)
                dve.wait_ge(ids_sum, 2 * at + 2)
                V.tensor_copy(idsi[:, par, 0:1], idsf[:, par, 0:1]).then_inc(ids_ready, 1)
                V.tensor_copy(idsi[0:CAP2, par, 1:2], idsf[0:CAP2, par, 1:2]).then_inc(ids_ready, 1)

            def hid_half(r, half):
                dve.wait_ge(silu_done, 2 * r + half + 1)
                V.tensor_tensor(hid[:, 2 * half:2 * half + 2, :], silu[:, 2 * half:2 * half + 2, :],
                                bank[2 * half + 1][:, :].rearrange("p (f s) -> p f s", f=2)[:, :, 0:CAP], ALU.mult).then_inc(hid_done, 1)

            def y_out(r, par, store_count):
                dve.wait_ge(ylo_full, 2 * r + 1)
                if store_count is not None:
                    dve.wait_ge(y_stored[par], store_count)
                V.tensor_copy(moe["y", par][:, 0:512], bank[6][:, :]).then_inc(ylo_drained, 1)
                dve.wait_ge(ylo_full, 2 * r + 2)
                V.tensor_copy(moe["y2", par][:, 0:512], bank[6][0:CAP2, :]).then_inc(ylo_drained, 1)

            dve.wait_ge(routed, 1)
            make_onehot(0, 0, iota[:])
            take_ids(0, 0, None)
            make_onehot(1, 1, iota[:])
            take_ids(1, 1, None)
            make_onehot(2, 2, iota[:])

            def main_round(i, par):
                r = 2 * i + par
                hid_half(r, 0)
                take_ids(r + 2, par, 32 * (i + 1))
                hid_half(r, 1)
                y_out(r, par, None if isinstance(i, int) else 32 * i)

            main_round(0, 0)
            make_onehot(3, 3, iota[:])
            main_round(0, 1)
            with dve.Fori(1, NE // 2) as i:
                for par in range(2):
                    make_onehot(2 * i + par + 2, 2 * i + par + 2, iota[:])
                    main_round(i, par)
            more = dve.value_load(table[0:1, T_NUM:T_NUM + 1], min_val=0, max_val=MAX_OVER)
            with dve.If(more > 0):
                with dve.Fori(0, more) as j:
                    e = dve.value_load(table[0:1, bass.ds(j + T_EXP, 1)], min_val=0, max_val=NE - 1)
                    dve.wait_ge(onehot_ready, NE + 2 + j)
                    V.tensor_scalar(iota_o, iota[:], offs[:, bass.ds(j, 1)], None, ALU.add).then_inc(ramp_ready, 1)
                    dve.wait_ge(ramp_ready, j + 1)
                    make_onehot(NE + 2 + j, e, iota_o)
                    take_ids(NE + 2 + j, 0, 32 * (NE // 2 + 1 + j))
                    hid_half(NE + j, 0)
                    hid_half(NE + j, 1)
                    y_out(NE + j, 0, 32 * (NE // 2 + j))
            for i in range(NT):
                for a, wt in enumerate((wt1, wt2)):
                    n = 2 * i + a
                    dve.wait_ge(yg_in[n % 4], 16 * (n // 4 + 1))
                    V.scalar_tensor_tensor(out=h[:, i, :], in0=ring[:, 1, (n % 4) * D:(n % 4 + 1) * D], scalar=wt[:, i:i + 1], in1=h[:, i, :],
                                           op0=ALU.mult, op1=ALU.add).then_inc(moe_added, 1)
                    dve.wait_ge(moe_added, n + 1)
                if i >= 1:
                    normalise(2, i - 1, 3, 2 * NT + i - 1, rstd)
            normalise(2, NT - 1, 3, 3 * NT - 1, rstd)
            drain_norm("n3T")
            for k in range(2):
                drain(f"pT{k}0", lambda b, k=k: V.tensor_copy(pT[:, k, 0:512], b[:, :]))
            for i in range(NT):
                for j in range(2):
                    n = 2 * i + j
                    dve.wait_ge(act_drained, drain_count[f"pg{i}{j}"])
                    wait_full(dve, f"pp{i}{j}")
                    V.tensor_tensor(pgm[:, n % 2, :], ps(f"pp{i}{j}")[:, :], sig[:, n % 2, :], ALU.mult).then_inc(dve_drained, 1)
                    dve.wait_ge(dve_drained, drain_count[f"pp{i}{j}"])
                    hs = h[:, i, j * 512:(j + 1) * 512]
                    V.tensor_tensor(hs, hs, pgm[:, n % 2, :], ALU.add).then_inc(h_ready, 1)
                    dve.wait_ge(h_ready, n + 1)
                if i >= 1:
                    normalise(3, i - 1, 4, i - 1, frstd)
            normalise(3, NT - 1, 4, NT - 1, frstd)


_INS = ["x_prompt", "x_sample", "p_prompt", "p_sample", "g_mix", "w_in", "conv_w", "conv_b", "lru_w_a", "lru_b_a",
        "lru_w_x", "lru_b_x", "lru_lambda", "sgu_ln_g", "sgu_ln_b", "sgu_w_s", "sgu_b_s", "g_rec_out", "g_sgu_out",
        "w_out", "g_ffn", "w_router_group", "b_router_group", "w_router_expert", "b_router_expert", "w_exp_gate",
        "w_exp_up", "w_exp_down", "g_ple", "w_ple_gate", "w_ple_proj", "g_final"]
_SQUEEZE = {"x_prompt": 1, "x_sample": 1, "p_prompt": 2, "p_sample": 2, "w_in": 1, "conv_w": 1, "lru_w_a": 1,
            "lru_b_a": 1, "lru_w_x": 1, "lru_b_x": 1, "lru_lambda": 1, "sgu_w_s": 1, "sgu_b_s": 1, "w_out": 1,
            "w_router_group": 1, "w_router_expert": 1, "w_exp_gate": 1, "w_exp_up": 1, "w_exp_down": 1,
            "w_ple_gate": 1, "w_ple_proj": 1}


def kernel(**inputs):
    import numpy as _np
    import concourse.bacc as _bacc
    from concourse import mybir as _mybir
    from concourse.bass_utils import run_bass_kernel_spmd as _run

    nc = _bacc.Bacc("TRN2", target_bir_lowering=False, num_devices=1, dynamic_dma_scratch_size=8192)
    arrays, args = {}, []
    for name in _INS:
        a = _np.ascontiguousarray(inputs[name])
        a = a.reshape(a.shape[_SQUEEZE.get(name, 0):])
        arrays[f"in_{name}"] = a
        args.append(nc.dram_tensor(f"in_{name}", a.shape, _mybir.dt.from_np(a.dtype), kind="ExternalInput").ap())
    for name, n in (("y_prompt", NPROMPT), ("y_sample", NSAMPLE)):
        args.append(nc.dram_tensor(name, (n, D), F32, kind="ExternalOutput").ap())
    hybrid_encoder_kernel(nc, *args)
    r = _run(nc, [arrays], core_ids=[0])
    return (r.results[0]["y_prompt"].reshape(1, NPROMPT, D), r.results[0]["y_sample"].reshape(1, NSAMPLE, D))
```

```python
from contextlib import ExitStack

import concourse.bass as bass
from concourse import mybir

F32 = mybir.dt.float32
F32R = mybir.dt.float32r
BF16 = mybir.dt.bfloat16
I32 = mybir.dt.int32
ALU = mybir.AluOpType
ACT = mybir.ActivationFunctionType
AX = mybir.AxisListType

P = 128
D = 1024
KD = D // P
NPROMPT, NSAMPLE = 256, 512
NTOK = NPROMPT + NSAMPLE
NT = NTOK // P
SEGS = [(0, NPROMPT), (NPROMPT, NSAMPLE)]
DR = 512
C4 = DR // P
NH = 8
HD = DR // NH
NG, NEG = 4, 4
NE = NG * NEG
DE = 512
F4 = DE // P
DPLE = 256
EPS = 1e-6
CAP = 160
CAP2 = CAP - P
MAX_OVER = 2 * NTOK // CAP
NROUND = NE + MAX_OVER
NSLOT = NROUND * CAP
CLASSES = (64, 80, 96, 112, 128, 144, 160)
NYG = 8
MASKED = -3.0e38

CONV_W, CONV_B, B_A, B_X, LAM, G_REC, G_SGU, B_S = 0, 16, 20, 28, 36, 44, 48, 52
NPAR = 60


def hybrid_encoder_kernel(nc, x_prompt, x_sample, p_prompt, p_sample, g_mix, w_in, conv_w, conv_b, lru_w_a,
                          lru_b_a, lru_w_x, lru_b_x, lru_lambda, sgu_ln_g, sgu_ln_b, sgu_w_s, sgu_b_s,
                          g_rec_out, g_sgu_out, w_out, g_ffn, w_router_group, b_router_group,
                          w_router_expert, b_router_expert, w_exp_gate, w_exp_up, w_exp_down, g_ple,
                          w_ple_gate, w_ple_proj, g_final, y_prompt, y_sample):
    n2_dram = nc.dram_tensor("n2_scratch", (NTOK, D), F32, kind="Internal").ap()
    y_dram = nc.dram_tensor("y_scratch", (NSLOT, D), F32, kind="Internal").ap()

    def token_rows(prompt, sample, i):
        src, at = (prompt, i) if i < 2 else (sample, i - 2)
        return src[at * P:(at + 1) * P, :]

    with ExitStack() as ctx:
        def sb(name, shape, dt=F32):
            return ctx.enter_context(nc.sbuf_tensor(name, shape, dt))

        def sem(name):
            return ctx.enter_context(nc.semaphore(name))

        big_at = [(nc.sbuf_usable_end - 4 * (6 * 4096 + 3 * NT * D + 5 * NTOK + C4 * NTOK)) // 32 * 32]

        def region(name, shape):
            at = big_at[0]
            big_at[0] += 4 * shape[1] * (shape[2] if len(shape) > 2 else 1)
            return (nc.alloc_sbuf_tensor_at(name, shape, F32, offset=at),
                    nc.alloc_sbuf_tensor_at(name + "_r", shape, F32R, offset=at))

        ring, ringR = region("ring", [P, 6, 4096])
        h, hR = region("h", [P, NT, D])
        regT, regTR = region("regT", [P, KD * NTOK])
        regN, _ = region("regN", [P, NT * D])
        regR, _ = region("regR", [P, 5 * NTOK])
        regX, regXR = region("regX", [P, C4 * NTOK])
        wsT = sb("wsT", [P, NH, P])

        def slot3(s):
            return ring[:, s, :].rearrange("p (k n) -> p k n", k=KD)

        early = ring[:, 5, :]
        wbd = early[:, 0:2048]
        w_s = early[:, 2048:3072].rearrange("p (h s) -> p h s", h=NH)
        ln_g = early[:, 3072:3584]
        ln_b = early[:, 3584:4096]
        nT = regT[:, :].rearrange("p (k t) -> p k t", k=KD)
        nT_hi = regTR[:, :].rearrange("p (i k t) -> p k i t", i=NT, k=KD)
        nT_lo = hR[:, :, :].rearrange("p i (k t) -> p k i t", k=KD)
        ys_hi = regTR[:, 0:C4 * NTOK].rearrange("p (c t) -> p c t", c=C4)
        ys_lo = regTR[:, C4 * NTOK:2 * C4 * NTOK].rearrange("p (c t) -> p c t", c=C4)
        xc_hi = ringR[:, 2, 0:C4 * NTOK].rearrange("p (c t) -> p c t", c=C4)
        xc_lo = regXR[:, :].rearrange("p (c t) -> p c t", c=C4)
        SPLIT = {"xr": (0, 1), "v": (2, 3), "u": (4, 0), "gr": (1, 2), "wo0": (3, 4), "wo1": (0, 1)}
        n2T_buf = regR[:, 0:2 * D].rearrange("p (b k t) -> p b k t", b=2, k=KD)
        ntok = regN[:, :].rearrange("p (i d) -> p i d", i=NT)
        v_tm = regN[:, 0:NT * DR].rearrange("p (i d) -> p i d", i=NT)
        u_tm = regN[:, NT * DR:2 * NT * DR].rearrange("p (i d) -> p i d", i=NT)
        gr = regN[:, 0:C4 * NTOK].rearrange("p (c t) -> p c t", c=C4)
        TR, TI, A0, TT, HF = (regR[:, j * NTOK:(j + 1) * NTOK] for j in range(5))
        xc = regX[:, :].rearrange("p (c t) -> p c t", c=C4)

        ident = sb("ident", [P, P])
        zeros = sb("zeros", [P, 512])
        ones = sb("ones", [P, 2])
        gB = sb("gB", [P, D])
        par_rows = regR[0:NPAR, 0:P]
        chan = sb("chan", [P, NPAR])
        wr = sb("wr", [P, KD, NG + NE])
        br = sb("br", [P, NG + NE])
        tri = sb("tri", [P, P], BF16)
        onesb = sb("onesb", [P, P], BF16)
        tokid = sb("tokid", [P, NT, 2], BF16)
        iota = sb("iota", [P, CAP])
        iota16 = sb("iota16", [P, NE])
        iota4 = sb("iota4", [P, 4])
        small = sb("small", [P, 400])
        rankm = sb("rankm", [P, NE + 2, NT])
        table = sb("table", [P, 64], I32)
        slots = sb("slots", [P, 2, NT], I32)
        idsi = sb("idsi", [P, 2, 2], I32)
        idsf = sb("idsf", [P, 2, 2])
        offs = sb("offs", [P, MAX_OVER])
        iota_o = regR[:, 2200:2200 + CAP]
        onehot = regR[:, 2400:2400 + NT * CAP // 2].bitcast(BF16).rearrange("p (i s) -> p i s", i=NT)

        taken = [0]

        def tiny(n):
            at = taken[0]
            taken[0] += n
            assert taken[0] <= 400
            return small[:, at:at + n]

        nhalf = tiny(8)
        iotaj = tiny(MAX_OVER)
        moe = {}
        at = 0
        for b in range(2):
            moe["xg", b] = regT[:, at:at + D]
            moe["y", b] = regN[:, at:at + D]
            at += D
        for b in range(2):
            moe["xg2", b] = regT[0:CAP2, at:at + D]
            moe["y2", b] = regN[0:CAP2, at:at + D]
            at += D
        for b in range(2):
            moe["xT", b] = (regT if b == 0 else regN)[:, at:at + KD * CAP].rearrange("p (k s) -> p k s", k=KD)
        p_tm = early[:, 2048:2048 + NT * DPLE].rearrange("p (i d) -> p i d", i=NT)
        pT = regX[:, 0:NT * DPLE].rearrange("p (k t) -> p k t", k=2)
        sig = regR[:, 0:1024].rearrange("p (b n) -> p b n", b=2)
        pgm = regR[:, 1024:2048].rearrange("p (b n) -> p b n", b=2)
        gF = regR[:, 2048:2048 + D]
        pp_sb = [ring[:, 0, n * 512:(n + 1) * 512] if n < 8 else ring[:, 3, (n - 4) * 512:(n - 3) * 512] for n in range(2 * NT)]
        silu = regR[:, 0:F4 * CAP].rearrange("p (f s) -> p f s", f=F4)
        hid = regR[:, F4 * CAP:2 * F4 * CAP].rearrange("p (f s) -> p f s", f=F4)

        bank = [ctx.enter_context(nc.psum_tensor(f"bank{b}", [P, 512], F32)) for b in range(8)]

        x_in = [sem(f"x_in{i}") for i in range(NT)]
        ring_in = [sem(f"ring_in{s}") for s in range(6)]
        par_in = sem("par_in")
        wbd_in, ws_in, ln_in, wr_in, gB_in = sem("wbd_in"), sem("ws_in"), sem("ln_in"), sem("wr_in"), sem("gB_in")
        consts = sem("consts")
        filled = sem("filled")
        act_drained = sem("act_drained")
        dve_drained = sem("dve_drained")
        act_seq, dve_seq, pool_seq = sem("act_seq"), sem("dve_seq"), sem("pool_seq")
        sumsq_done, rstd_done, norm_done = sem("sumsq_done"), sem("rstd_done"), sem("norm_done")
        ln_var, ln_rstd, v_ready = sem("ln_var"), sem("ln_rstd"), sem("v_ready")
        zeroed = sem("zeroed")
        halves_ready, exp_lam, decay_ready = sem("halves_ready"), sem("exp_lam"), sem("decay_ready")
        rec_exp, rec_m2, rec_mult = sem("rec_exp"), sem("rec_m2"), sem("rec_mult")
        scan_part, rec_sum = sem("scan_part"), sem("rec_sum")
        us_sq, us_rstd, us_scaled = sem("us_sq"), sem("us_rstd"), sem("us_scaled")
        rec_y, rec_sq, rec_g = sem("rec_y"), sem("rec_sq"), sem("rec_g")
        rr_rstd = sem("rr_rstd")
        h_ready = sem("h_ready")
        n2_stored = sem("n2_stored")
        hi_ready = {u: sem(f"hi_ready_{u}") for u in SPLIT}
        lo_ready = {u: sem(f"lo_ready_{u}") for u in SPLIT}
        nT_high, ys_high, rec_high = sem("nT_high"), sem("ys_high"), sem("rec_high")
        route_max, route_exp, chosen, routed = sem("route_max"), sem("route_exp"), sem("chosen"), sem("routed")
        ids_sum, ramp_ready = sem("ids_sum"), sem("ramp_ready")
        turn_go, gather_go = sem("turn_go"), sem("gather_go")
        last_over = sem("last_over")
        onehot_ready, ids_full, ids_ready = sem("onehot_ready"), sem("ids_full"), sem("ids_ready")
        gathered = [sem("gathered0"), sem("gathered1")]
        t_full, t_drained = sem("t_full"), sem("t_drained")
        gu_full, silu_done, hid_done = sem("gu_full"), sem("silu_done"), sem("hid_done")
        ylo_full, yhi_full = sem("ylo_full"), sem("yhi_full")
        tlo_full, thi_full = sem("tlo_full"), sem("thi_full")
        ylo_drained, yhi_drained = sem("ylo_drained"), sem("yhi_drained")
        y_stored = [sem("y_stored0"), sem("y_stored1")]
        yg_in = [sem(f"yg_in{b}") for b in range(NYG)]
        p_in = sem("p_in")
        moe_added = sem("moe_added")
        gF_in, pgm_done = sem("gF_in"), sem("pgm_done")
        fin_sumsq, fin_rstd, fin_norm = sem("fin_sumsq"), sem("fin_rstd"), sem("fin_norm")
        stored = sem("stored")

        groups = [(f"nT{i}{j}", "dve") for i in range(NT) for j in range(2)]
        groups += [("par", "dve")]
        groups += [(f"xr{c}{s}", "dve") for c in range(C4) for s in range(2)]
        groups += [(f"wsT{j}", "act") for j in range(2)]
        fillers = [[f"v{2 * j + a}" for a in range(2)] for j in range(3)]
        fillers += [[f"u{2 * j + a}" for a in range(2)] for j in range(3)]
        fillers += [[f"mix{hh}" for hh in range(NH)], [f"gr{c}{s}" for c in range(C4) for s in range(2)]]
        for unit in range(8):
            groups += [(f"gate{unit}{g}{s}", "act") for g in range(2) for s in range(2)]
            groups += [(x, "dve" if x[:3] == "mix" else "act") for x in fillers[unit]]
        groups += [(f"ysT{c}{s}", "dve") for c in range(C4) for s in range(2)]
        first_half = [("s", i) for i in range(4)] + [("ssq", 0)] + [("r", i) for i in range(4)]
        first_half += [(g, i) for i in range(4, NT) for g in "sr"]
        groups += [("ssq" if g == "ssq" else f"out{i}0{g}", "dve") for g, i in first_half]
        pT_groups = [(f"pT{k}{s}", "act" if s else "dve") for k in range(2) for s in range(2)]
        for i in range(NT + 2):
            if i < NT:
                groups += [(f"out{i}1{g}", "dve") for g in "sr"]
            if i == NT:
                groups += pT_groups
            if 1 <= i <= NT:
                groups += [(f"n2T{i - 1}{j}", "act" if j else "dve") for j in range(2)]
            if i >= 2:
                groups += [(f"route{i - 2}", "dve")]
        groups += [("rank", "dve")]
        number = {name: n for n, (name, _) in enumerate(groups)}
        drain_count, seen = {}, {"act": 0, "dve": 0}
        for name, who in groups:
            seen[who] += 1
            drain_count[name] = seen[who]
        NGROUP = len(groups)
        late = [(f"pp{i}{j}", "act") for i in range(NT - 2) for j in range(2)]
        for i in range(NT + 1):
            if i < NT:
                late += [(f"n3T{i}{j}", "act" if j else "dve") for j in range(2)]
            if i < 2:
                late += [(f"pp{NT - 2 + i}{j}", "act") for j in range(2)]
            if i >= 1:
                late += [(f"pg{i - 1}{j}", "act") for j in range(2)]
        for n, (name, who) in enumerate(late):
            number[name] = NGROUP + n
            seen[who] += 1
            drain_count[name] = seen[who]
        allgroups = groups + late
        drainer = dict(allgroups)

        def ps(name):
            return bank[number[name] % 8]

        def wait_full(eng, name):
            eng.wait_ge(filled, number[name] + 1)

        def wait_drained(eng, name):
            eng.wait_ge(act_drained if drainer[name] == "act" else dve_drained, drain_count[name])

        def wait_bank(pe, name):
            n = number[name]
            if n >= 8 and not NGROUP <= n < NGROUP + 8:
                wait_drained(pe, allgroups[n - 8][0])

        class Chain:

            def __init__(self, eng, s):
                self.eng, self.sem, self.n = eng, s, 0

            def link(self, ins):
                self.n += 1
                ins.then_inc(self.sem, 1)
                self.eng.wait_ge(self.sem, self.n)

        ssum, rstd = tiny(6 * 3), tiny(6 * 3)
        fsum, frstd = tiny(6), tiny(6)
        bn, mv, lvar, lrstd = tiny(6 * NT), tiny(2 * NT), tiny(NT), tiny(NT)
        usum, urstd, rsum, rrstd = tiny(NT), tiny(NT), tiny(NT), tiny(NT)
        hb = tiny(16)
        nlam, lab, lexp, lden, ls, ls2, lpoly, sp = (tiny(8) for _ in range(8))
        c4, c2 = tiny(8), tiny(8)
        wt1, wt2 = tiny(NT), tiny(NT)
        slotf = tiny(2 * NT).rearrange("p (a i) -> p a i", a=2)
        first = taken[0]

        def tiny(n):
            at = taken[0] - first
            taken[0] += n
            assert at + n <= 5 * NTOK - 2900
            return regR[:, 2900 + at:2900 + at + n]

        logit = tiny(NT * 20).rearrange("p (i n) -> p i n", i=NT)
        gmax, gidx, gsum, gtop = tiny(NT), tiny(NT), tiny(NT), tiny(NT)
        gsh, gexp, gone = (tiny(NT * 4).rearrange("p (i n) -> p i n", i=NT) for _ in range(3))
        el, el2, one1, one2, cand = (tiny(NT * 4).rearrange("p (i n) -> p i n", i=NT) for _ in range(5))
        e16 = tiny(NT * NE).rearrange("p (i g e) -> p i g e", i=NT, g=NG)
        m1, m2, i1, i2, xe, den = (tiny(NT) for _ in range(6))
        work = [regR[:, j * 160:j * 160 + NT * NE] for j in range(10)]
        oh1, oh2, chose, prefix, rank, slotm, lt = (w.rearrange("p (i e) -> p i e", i=NT) for w in work[:7])
        pick = work[7].rearrange("p (i e) -> p i e", i=NT)
        choseb = sb("choseb", [P, NT * NE], BF16)
        nexp, over, incl, excl, base = (tiny(NE) for _ in range(5))
        oq = regR[:, 1600:1600 + 4 * NE].rearrange("p (q e) -> p q e", q=4)
        ojn = regR[:, 1700:1700 + MAX_OVER * NE].rearrange("p (j e) -> p j e", j=MAX_OVER)
        oj2 = regR[:, 1900:1900 + MAX_OVER * NE].rearrange("p (j e) -> p j e", j=MAX_OVER)
        jexp, jfirst, jcnt = (tiny(MAX_OVER) for _ in range(3))

        T_NUM, T_EXP, T_COUNT = 0, 1, 16

        def yg(n):
            b = n % NYG
            return ring[:, 4 + b // 4, (b % 4) * D:(b % 4 + 1) * D]

        def moe_slots(par):
            return (1, 2, 3) if par == 0 else (4, 5, 0)

        QW = 1024

        def split_high(act, unit):
            lo, hi = SPLIT[unit]
            act.wait_ge(ring_in[lo], 32 if unit == "wo1" else 16)
            for q in range(4):
                c = slice(q * QW, (q + 1) * QW)
                nc.scalar.activation(ringR[:, hi, c], ring[:, lo, c], ACT.Copy).then_inc(hi_ready[unit], 1)

        def split_low(eng, engine, unit):
            lo, hi = SPLIT[unit]
            for q in range(4):
                c = slice(q * QW, (q + 1) * QW)
                eng.wait_ge(hi_ready[unit], q + 1)
                engine.tensor_tensor(ringR[:, lo, c], ring[:, lo, c], ringR[:, hi, c].bitcast(F32), ALU.subtract).then_inc(lo_ready[unit], 1)

        def both_parts(unit):
            return tuple(ringR[:, s, :].rearrange("p (k n) -> p k n", k=KD) for s in reversed(SPLIT[unit]))

        block = ctx.enter_context(nc.Block())

        @block.sync
        def _(sp):
            for i in range(NT):
                sp.dma_start(h[:, i, :], token_rows(x_prompt, x_sample, i)).then_inc(x_in[i], 16)
                if i == 0:
                    sp.dma_start(gB[:], g_mix[0].partition_broadcast(P)).then_inc(gB_in, 16)

            def load_in(s, col):
                sp.dma_start(slot3(s), w_in[:, col:col + DR].rearrange("(k p) n -> p k n", p=P)).then_inc(ring_in[s], 16)

            rows = lambda w, pat, **kw: w.rearrange(pat, **kw)
            for at_row, src in ((CONV_W, rows(conv_w, "k (c p) -> (k c) p", p=P)), (CONV_B, rows(conv_b, "o (c p) -> (o c) p", p=P)),
                                (B_A, rows(lru_b_a, "d (c p) -> (d c) p", p=P)), (B_X, rows(lru_b_x, "d (c p) -> (d c) p", p=P)),
                                (LAM, rows(lru_lambda, "d (c p) -> (d c) p", p=P)), (G_REC, rows(g_rec_out, "o (c p) -> (o c) p", p=P)),
                                (G_SGU, rows(g_sgu_out, "o (c p) -> (o c) p", p=P)), (B_S, sgu_b_s)):
                sp.dma_start(par_rows[at_row:at_row + src.shape[0], :], src).then_inc(par_in, 16)
            load_in(0, 0)
            sp.wait_ge(consts, 1)
            for g, src in enumerate((lru_w_a, lru_w_x)):
                for d in range(2):
                    for half in range(2):
                        lo = half * HD
                        dst = wbd[lo:lo + HD, (d * 2 + g) * C4 * P:(d * 2 + g + 1) * C4 * P].rearrange("i (c j) -> i c j", c=C4)[:, :, lo:lo + HD]
                        sp.dma_start(dst, src[d].rearrange("(c s) i j -> s i c j", s=2)[half]).then_inc(wbd_in, 16)
            sp.dma_start(w_s, sgu_w_s.rearrange("h t s -> t h s")).then_inc(ws_in, 16)
            load_in(2, 3 * DR)
            sp.dma_start(ln_g, sgu_ln_g[0].partition_broadcast(P)).then_inc(ln_in, 16)
            sp.dma_start(ln_b, sgu_ln_b[0].partition_broadcast(P)).then_inc(ln_in, 16)
            load_in(4, 2 * DR)
            sp.dma_start(wr[:, :, 0:NG], w_router_group.rearrange("(k p) n -> p k n", p=P)).then_inc(wr_in, 16)
            sp.dma_start(wr[:, :, NG:], w_router_expert.rearrange("(k p) n -> p k n", p=P)).then_inc(wr_in, 16)
            sp.dma_start(br[:, 0:NG], b_router_group[0].partition_broadcast(P)).then_inc(wr_in, 16)
            sp.dma_start(br[:, NG:], b_router_expert[0].partition_broadcast(P)).then_inc(wr_in, 16)
            wait_full(sp, f"xr{C4 - 1}1")
            load_in(1, DR)
            sp.wait_ge(consts, 16)
            more_rows = y_dram[NE * CAP:, :]
            whole = MAX_OVER * CAP // P
            for j in range(2):
                cols = slice(j * 512, (j + 1) * 512)
                sp.dma_start(more_rows[0:whole * P, cols].rearrange("(a p) d -> p a d", p=P),
                             zeros[:, :].unsqueeze(1).to_broadcast([P, whole, 512])).then_inc(zeroed, 16)
                sp.dma_start(more_rows[whole * P:, cols], zeros[0:MAX_OVER * CAP - whole * P, :]).then_inc(zeroed, 16)
            sp.wait_ge(v_ready, NT)
            wait_drained(sp, "wsT1")
            for i in range(NT):
                sp.dma_start(p_tm[:, i, :], token_rows(p_prompt, p_sample, i)).then_inc(p_in, 16)
            for j, (s, last) in enumerate(((3, "v5"), (0, "u5"))):
                wait_full(sp, last)
                sp.dma_start(slot3(s), w_out[:, j * 512:(j + 1) * 512].rearrange("(k p) n -> p k n", p=P)).then_inc(ring_in[s], 16)
            wait_full(sp, f"gr{C4 - 1}1")
            for i in range(NT):
                sp.dma_start(h[:, i, :], token_rows(x_prompt, x_sample, i)).then_inc(x_in[i], 16)

            def load_weights(s, src, e, waits):
                for sm, value in waits:
                    sp.wait_ge(sm, value)
                w = src[bass.ds(e, 1), :, :].rearrange("a r n -> (a r) n")
                dst = ring[:, s, :].rearrange("p (k n) -> p k n", k=F4) if src is w_exp_down else slot3(s)
                sp.dma_start(dst, w.rearrange("(k p) n -> p k n", p=P)).then_inc(ring_in[s], 16)

            def load_expert(par, e, waits):
                for s, src, wait in zip(moe_slots(par), (w_exp_gate, w_exp_up, w_exp_down), waits):
                    load_weights(s, src, e, wait)

            full = lambda name: (filled, number[name] + 1)
            load_weights(3, w_exp_down, 0, [full(f"out{NT - 1}0r")])
            load_weights(4, w_exp_gate, 1, [])
            load_weights(1, w_exp_gate, 0, [full(f"out{NT - 1}1r")])
            load_weights(2, w_exp_up, 0, [])
            load_weights(5, w_exp_up, 1, [full("pT11")])
            load_weights(0, w_exp_down, 1, [])
            with sp.Fori(1, NE // 2) as i:
                for par in range(2):
                    done = 2 * i + par - 1
                    gu, down = [(gu_full, 2 * done)], [(yhi_full, done), (thi_full, done)]
                    load_expert(par, 2 * i + par, (gu, gu, down))
            sp.wait_ge(routed, 1)
            more = sp.value_load(table[0:1, T_NUM:T_NUM + 1], min_val=0, max_val=MAX_OVER)
            with sp.If(more > 0):
                with sp.Fori(0, more) as j:
                    e = sp.value_load(table[0:1, bass.ds(j + T_EXP, 1)], min_val=0, max_val=NE - 1)
                    gu, down = [(gu_full, 2 * (NE + j))], [(yhi_full, NE + j), (thi_full, NE + j)]
                    load_expert(0, e, (gu, gu, down))
                sp.wait_ge(yhi_full, NE + more)
                sp.wait_ge(thi_full, NE + more)
                sp.sem_inc(last_over, 1)
            sp.wait_ge(gu_full, 2 * (NE - 1))
            for a, s in enumerate((1, 2)):
                sp.dma_start(slot3(s), w_ple_gate[:, a * 512:(a + 1) * 512].rearrange("(k p) n -> p k n", p=P)).then_inc(ring_in[s], 16)
            sp.wait_ge(yhi_full, NE - 1)
            sp.wait_ge(thi_full, NE - 1)
            sp.dma_start(ring[:, 3, 0:2 * D].rearrange("p (k n) -> p k n", k=2),
                         w_ple_proj.rearrange("(k p) n -> p k n", p=P)).then_inc(ring_in[3], 16)
            for i in range(NT):
                sp.wait_ge(fin_norm, i + 1)
                sp.dma_start(token_rows(y_prompt, y_sample, i), ntok[:, i, :]).then_inc(stored, 16)
            sp.wait_ge(stored, 16 * NT)

        @block.gpsimd
        def _(pool):
            nc.gpsimd.memset(wbd, 0.0).then_inc(consts, 1)
            nc.gpsimd.memset(zeros[:], 0.0).then_inc(consts, 1)
            nc.gpsimd.memset(ident[:], 0.0).then_inc(consts, 1)
            nc.gpsimd.memset(tri[:], 1.0).then_inc(consts, 1)
            pool.wait_ge(consts, 4)
            nc.gpsimd.affine_select(out=ident[:], in_=ident[:], compare_op=ALU.not_equal, fill=1.0, base=0,
                                    pattern=[[-1, P]], channel_multiplier=1).then_inc(consts, 1)
            nc.gpsimd.affine_select(out=tri[:], in_=tri[:], compare_op=ALU.is_gt, fill=0.0, base=0,
                                    pattern=[[1, P]], channel_multiplier=-1).then_inc(consts, 1)
            nc.gpsimd.memset(ones[:], 1.0).then_inc(consts, 1)
            nc.gpsimd.memset(onesb[:], 1.0).then_inc(consts, 1)
            nc.gpsimd.memset(nhalf, -0.5).then_inc(consts, 1)
            nc.gpsimd.memset(rankm[:, NE:NE + 2, :], -1.0).then_inc(consts, 1)
            nc.gpsimd.iota(iota[:], pattern=[[1, CAP]], base=0, channel_multiplier=0,
                           allow_small_or_imprecise_dtypes=True).then_inc(consts, 1)
            nc.gpsimd.iota(iota16[:], pattern=[[1, NE]], base=0, channel_multiplier=0,
                           allow_small_or_imprecise_dtypes=True).then_inc(consts, 1)
            nc.gpsimd.iota(iotaj, pattern=[[1, MAX_OVER]], base=0, channel_multiplier=0,
                           allow_small_or_imprecise_dtypes=True).then_inc(consts, 1)
            nc.gpsimd.iota(tokid[:, :, 0:1], pattern=[[0, NT], [0, 1]], base=0, channel_multiplier=1,
                           allow_small_or_imprecise_dtypes=True).then_inc(consts, 1)
            nc.gpsimd.iota(tokid[:, :, 1:2], pattern=[[P, NT], [0, 1]], base=0, channel_multiplier=0,
                           allow_small_or_imprecise_dtypes=True).then_inc(consts, 1)
            nc.gpsimd.iota(iota4[:], pattern=[[1, 4]], base=-4, channel_multiplier=0,
                           allow_small_or_imprecise_dtypes=True).then_inc(consts, 1)
            ch = Chain(pool, pool_seq)
            pool.wait_ge(consts, 16)

            def rstd_of(src, dst, n, scale, out_sem):
                ch.link(nc.gpsimd.tensor_scalar(src, src, scale, EPS, ALU.mult, ALU.add))
                nc.gpsimd.tensor_tensor(dst, src, nhalf[:, 0:n], ALU.pow).then_inc(out_sem, 1)

            def norm_rstd(k, tiles=range(NT)):
                for i in tiles:
                    pool.wait_ge(sumsq_done, k * NT + i + 1)
                    a = k * NT + i
                    rstd_of(ssum[:, a:a + 1], rstd[:, a:a + 1], 1, 1.0 / D, rstd_done)

            norm_rstd(0)
            split_low(pool, nc.gpsimd, "v")
            split_low(pool, nc.gpsimd, "u")
            for i in range(NT):
                pool.wait_ge(ln_var, i + 1)
                ch.link(nc.gpsimd.tensor_scalar(lvar[:, i:i + 1], mv[:, 2 * i + 1:2 * i + 2], 1.0, EPS, ALU.mult, ALU.add))
                nc.gpsimd.tensor_tensor(lrstd[:, i:i + 1], lvar[:, i:i + 1], nhalf[:, 0:1], ALU.pow).then_inc(ln_rstd, 1)
            split_low(pool, nc.gpsimd, "gr")
            pool.wait_ge(us_sq, NT)
            rstd_of(usum, urstd, NT, 1.0 / DR, us_rstd)
            split_low(pool, nc.gpsimd, "wo0")
            wait_drained(pool, "ssq")
            rstd_of(rsum, rrstd, NT, 1.0 / DR, rr_rstd)
            norm_rstd(1)
            pool.wait_ge(n2_stored, 16 * NT)

            def gather(r, par, ids_at):
                pool.wait_ge(ids_ready, 2 * (ids_at + 1))
                pool.sem_inc(gather_go, 1)
                nc.gpsimd.indirect_dma_start(moe["xg", par], None, n2_dram,
                                             bass.IndirectOffsetOnAxis(ap=idsi[:, par, 0:1], axis=0)).then_inc(gathered[par], 16)
                nc.gpsimd.indirect_dma_start(moe["xg2", par], None, n2_dram,
                                             bass.IndirectOffsetOnAxis(ap=idsi[0:CAP2, par, 1:2], axis=0)).then_inc(gathered[par], 16)

            wait_full(pool, f"route{NT - 1}")
            gather(0, 0, 0)
            gather(1, 1, 1)
            with pool.Fori(1, NE // 2 + 1) as i:
                for par in range(2):
                    r = 2 * i + par
                    pool.wait_ge(t_full, 3 * (r - 1))
                    gather(r, par, r)
            more = pool.value_load(table[0:1, T_NUM:T_NUM + 1], min_val=0, max_val=MAX_OVER)
            with pool.If(more > 0):
                with pool.Fori(0, more) as j:
                    pool.wait_ge(t_full, 3 * (NE + 1 + j))
                    gather(NE + j, 0, NE + 2 + j)
            pool.wait_ge(yhi_full, NE + more)
            pool.wait_ge(thi_full, NE + more)
            pool.wait_ge(y_stored[0], 32 * (NE // 2 + more))
            pool.wait_ge(y_stored[1], 32 * (NE // 2))
            pool.sem_inc(gather_go, 1)
            for i in range(NT):
                for a in range(2):
                    n = 2 * i + a
                    if n >= NYG:
                        pool.wait_ge(moe_added, n - NYG + 1)
                    nc.gpsimd.indirect_dma_start(yg(n), None, y_dram,
                                                 bass.IndirectOffsetOnAxis(ap=slots[:, a, i:i + 1], axis=0)).then_inc(yg_in[n % NYG], 16)
                if i >= NYG // 2 - 1:
                    norm_rstd(2, [i - NYG // 2 + 1])
            for i in range(NT + 1):
                if NT - NYG // 2 + 1 <= i + 2 < NT:
                    norm_rstd(2, [i + 2])
                if i >= 1:
                    pool.wait_ge(fin_sumsq, i)
                    rstd_of(fsum[:, i - 1:i], frstd[:, i - 1:i], 1, 1.0 / D, fin_rstd)

        @block.tensor
        def _(pe):
            pe.wait_ge(consts, 16)

            def transposes(name, parts):
                wait_bank(pe, name)
                at = 0
                for src, n in parts:
                    q = nc.tensor.transpose(ps(name)[:src.shape[1], at:at + n], src, ident[0:n, 0:n])
                    at += n
                q.then_inc(filled, 1)

            def product(name, out, pairs):
                wait_bank(pe, name)
                for k, (a, b) in enumerate(pairs):
                    q = nc.tensor.matmul(out, a, b, start=(k == 0), stop=(k == len(pairs) - 1))
                q.then_inc(filled, 1)

            def product3(name, out, terms):
                wait_bank(pe, name)
                passes = [(a[i], b[j]) for a, b in terms for i, j in ((0, 0), (0, 1), (1, 0))]
                for n, (a, b) in enumerate(passes):
                    q = nc.tensor.matmul(out, a, b, start=(n == 0), stop=(n == len(passes) - 1))
                q.then_inc(filled, 1)

            def n_cols(k, i0, n):
                return nT_hi[:, k, i0:i0 + n, :], nT_lo[:, k, i0:i0 + n, :]

            def n_tile(k, i):
                return nT_hi[:, k, i, :], nT_lo[:, k, i, :]

            def norm_transposes(prefix, k, tiles=range(NT)):
                for i in tiles:
                    pe.wait_ge(norm_done, k * NT + i + 1)
                    for j in range(2):
                        transposes(f"{prefix}{i}{j}", [(ntok[:, i, (4 * j + a) * P:(4 * j + a + 1) * P], P) for a in range(4)])

            norm_transposes("nT", 0)
            pe.wait_ge(par_in, 16 * 8)
            transposes("par", [(par_rows[:, :], NPAR)])
            for i in range(NT):
                for j in range(2):
                    wait_drained(pe, f"nT{i}{j}")
            pe.wait_ge(lo_ready["xr"], 4)

            def channel_major(unit, c, s):
                t0, n = SEGS[s]
                name = f"{unit}{c}{s}"
                w = both_parts(unit)
                product3(name, ps(name)[:, 0:n], [([x[:, k, c * P:(c + 1) * P] for x in w], n_cols(k, t0 // P, n // P)) for k in range(KD)])

            for c in range(C4):
                for s in range(2):
                    channel_major("xr", c, s)
            pe.wait_ge(ws_in, 16)
            for j in range(2):
                transposes(f"wsT{j}", [(w_s[:, 4 * j + a, :], P) for a in range(4)])

            def filler(name):
                if name[0] in "vu":
                    i, w = int(name[1]), both_parts(name[0])
                    pe.wait_ge(lo_ready[name[0]], 4)
                    product3(name, ps(name)[:, :], [(n_tile(k, i), [x[:, k, :] for x in w]) for k in range(KD)])
                elif name[:3] == "mix":
                    hh = int(name[3])
                    if hh == 0:
                        pe.wait_ge(v_ready, NT)
                        wait_drained(pe, "wsT1")
                    product(name, ps(name)[:, 0:NT * HD].rearrange("p (i c) -> p i c", i=NT),
                            [(wsT[:, hh, :], v_tm[:, :, hh * HD:(hh + 1) * HD])])
                else:
                    pe.wait_ge(lo_ready["gr"], 4)
                    channel_major("gr", int(name[2]), int(name[3]))

            for unit in range(8):
                c, d = unit // 2, unit % 2
                wait_drained(pe, f"xr{c}1")
                if unit == 0:
                    pe.wait_ge(wbd_in, 16 * 8)
                for g in range(2):
                    w = wbd[:, ((d * 2 + g) * C4 + c) * P:((d * 2 + g) * C4 + c + 1) * P]
                    for s, (t0, n) in enumerate(SEGS):
                        name = f"gate{unit}{g}{s}"
                        product(name, ps(name)[:, 0:n], [(w, xc[:, c, t0:t0 + n])])
                for name in fillers[unit]:
                    filler(name)
            for c in range(C4):
                for s, tiles in enumerate(((0, 1, 2, 3), (4, 5))):
                    if c == 0:
                        pe.wait_ge(us_scaled, tiles[-1] + 1)
                    transposes(f"ysT{c}{s}", [(u_tm[:, i, c * P:(c + 1) * P], P) for i in tiles])
            def out_product(i, j, g):
                w = both_parts(f"wo{j}")
                src, row = ((xc_hi, xc_lo), 0) if g == "r" else ((ys_hi, ys_lo), C4)
                name = f"out{i}{j}{g}"
                product3(name, ps(name)[:, :], [([x[:, c, i * P:(i + 1) * P] for x in src], [x[:, row + c, :] for x in w]) for c in range(C4)])

            for c in range(C4):
                for s in range(2):
                    wait_drained(pe, f"ysT{c}{s}")
            pe.wait_ge(lo_ready["wo0"], 4)
            for g, i in first_half:
                if g != "ssq":
                    out_product(i, 0, g)
                    continue
                pe.wait_ge(rec_sq, C4)
                wait_bank(pe, "ssq")
                for t in range(NT):
                    for c in range(C4):
                        q = nc.tensor.matmul(ps("ssq")[:, t:t + 1], gr[:, c, t * P:(t + 1) * P], ones[:, 0:1],
                                             start=(c == 0), stop=(c == C4 - 1))
                q.then_inc(filled, 1)
                pe.wait_ge(rec_g, C4)
            pe.wait_ge(lo_ready["wo1"], 4)
            pe.wait_ge(wr_in, 16 * 4)
            for i in range(NT + 2):
                if i < NT:
                    for g in "sr":
                        out_product(i, 1, g)
                if i == NT:
                    pe.wait_ge(p_in, 16 * NT)
                    for k in range(2):
                        for s, tiles in enumerate(((0, 1, 2, 3), (4, 5))):
                            transposes(f"pT{k}{s}", [(p_tm[:, t, k * P:(k + 1) * P], P) for t in tiles])
                if 1 <= i <= NT:
                    norm_transposes("n2T", 1, [i - 1])
                if i >= 2:
                    for j in range(2):
                        wait_drained(pe, f"n2T{i - 2}{j}")
                    name = f"route{i - 2}"
                    product(name, ps(name)[:, 0:NG + NE], [(n2T_buf[:, i % 2, k, :], wr[:, k, :]) for k in range(KD)])
            pe.wait_ge(chosen, 1)
            wait_bank(pe, "rank")
            for i in range(NT + 1):
                out = ps("rank")[:, i * NE:(i + 1) * NE]
                parts = [(onesb, t) for t in range(i)] + ([(tri, i)] if i < NT else [])
                for n, (w, t) in enumerate(parts):
                    q = nc.tensor.matmul(out, w[:], choseb[:, t * NE:(t + 1) * NE], start=(n == 0), stop=(n == len(parts) - 1))
            q.then_inc(filled, 1)
            wait_drained(pe, "rank")
            wait_drained(pe, f"n2T{NT - 1}1")

            def ids(at):
                pe.wait_ge(onehot_ready, at + 1)
                if not (isinstance(at, int) and at == 0):
                    pe.wait_ge(ids_ready, 2 * at)
                for t in range(NT):
                    nc.tensor.matmul(bank[5][:, 0:2], onehot[:, t, 0:P], tokid[:, t, :], start=(t == 0), stop=(t == NT - 1))
                for t in range(NT):
                    q = nc.tensor.matmul(bank[5][0:CAP2, 2:4], onehot[:, t, P:CAP], tokid[:, t, :], start=(t == 0), stop=(t == NT - 1))
                q.then_inc(ids_full, 1)

            def turn(part, par, t_at):
                if not (isinstance(t_at, int) and t_at == 0 and part == 0):
                    pe.wait_ge(t_drained, 3 * t_at + part)
                    pe.sem_inc(turn_go, 1)
                for a in range(4 if part < 2 else KD):
                    if part < 2:
                        k = 4 * part + a
                        q = nc.tensor.transpose(bank[4][:, a * P:(a + 1) * P], moe["xg", par][:, k * P:(k + 1) * P], ident[:])
                    else:
                        q = nc.tensor.transpose(bank[4][:, a * CAP2:(a + 1) * CAP2], moe["xg2", par][:, a * P:(a + 1) * P], ident[0:CAP2, 0:CAP2])
                q.then_inc(t_full, 1)

            def hidden(f, par, n):
                sg, su, _ = moe_slots(par)
                half, col = f // 2, (f % 2) * 256
                for b, s in ((2 * half, sg), (2 * half + 1, su)):
                    for k in range(KD):
                        q = nc.tensor.matmul(bank[b][:, col:col + n], slot3(s)[:, k, f * P:(f + 1) * P], moe["xT", par][:, k, 0:n],
                                             start=(k == 0), stop=(k == KD - 1))
                return q

            def down(out, par, lo, n, j, chunks):
                w = ring[:, moe_slots(par)[2], :].rearrange("p (k n) -> p k n", k=F4)
                for f in chunks:
                    q = nc.tensor.matmul(out[0:n, :], hid[:, f, lo:lo + n], w[:, f, j * 512:(j + 1) * 512],
                                         start=(f == 0), stop=(f == F4 - 1))
                return q

            def by_size(count, body, sizes=CLASSES):
                if len(sizes) == 1:
                    body(sizes[0])
                    return
                low = sizes[:len(sizes) // 2]
                with pe.If(count < low[-1] + 1):
                    by_size(count, body, low)
                with pe.Else():
                    by_size(count, body, sizes[len(low):])

            def one_round(r, par, loads, prev_hidden, turn_next):
                count = pe.value_load(table[0:1, bass.ds(r + T_COUNT, 1)], min_val=0, max_val=NTOK)
                sg, su, sd = moe_slots(par)
                pe.wait_ge(t_drained, 3 * (turn_next[1] if turn_next else r + 1))
                pe.wait_ge(ring_in[sg], loads[0])
                pe.wait_ge(ring_in[su], loads[1])
                for half in range(2):
                    if prev_hidden is not None:
                        pe.wait_ge(hid_done, 2 * prev_hidden + half + 1)

                    def body(n, half=half):
                        hidden(2 * half, par, n)
                        hidden(2 * half + 1, par, n).then_inc(gu_full, 1)
                    by_size(count, body)
                    if turn_next:
                        if half == 0:
                            pe.wait_ge(gathered[1 - par], turn_next[2])
                            if prev_hidden is not None:
                                pe.wait_ge(ylo_drained, 2 * r)
                                pe.wait_ge(yhi_drained, 2 * r)
                            ids(r + 2)
                        turn(half, 1 - par, turn_next[1])
                pe.wait_ge(ring_in[sd], loads[2])
                if prev_hidden is not None:
                    pe.wait_ge(ylo_drained, 2 * r)
                    pe.wait_ge(yhi_drained, 2 * r)
                for half in range(2):
                    pe.wait_ge(hid_done, 2 * r + half + 1)
                    for j in range(2):
                        q = down(bank[6 + j], par, 0, P, j, (2 * half, 2 * half + 1))
                        if half == 1:
                            q.then_inc((ylo_full, yhi_full)[j], 1)
                    if half == 0 and turn_next:
                        turn(2, 1 - par, turn_next[1])
                if turn_next:
                    pe.wait_ge(t_drained, 3 * (r + 2))
                    pe.wait_ge(ids_ready, 2 * (r + 3))
                with pe.If(count < P + 1):
                    pe.sem_inc(tlo_full, 1)
                    pe.sem_inc(thi_full, 1)
                with pe.Else():
                    down(bank[4], par, P, CAP2, 0, range(F4)).then_inc(tlo_full, 1)
                    down(bank[5], par, P, CAP2, 1, range(F4)).then_inc(thi_full, 1)

            before = {0: 2, 1: 1, 2: 1, 3: 1, 4: 1, 5: 0}

            ids(0)
            ids(1)
            pe.wait_ge(gathered[0], 32)
            for part in range(3):
                turn(part, 0, 0)
            pe.wait_ge(routed, 1)

            def main_round(i, par, first):
                r = 2 * i + par
                loads = [16 * (before[s] + 1 + i) for s in moe_slots(par)]
                count = 32 * (i + 1) if par == 0 else 32 * (i + 2)
                one_round(r, par, loads, None if first else r - 1, (None, r + 1, count))

            main_round(0, 0, True)
            main_round(0, 1, False)
            with pe.Fori(1, NE // 2) as i:
                main_round(i, 0, False)
                main_round(i, 1, False)
            more = pe.value_load(table[0:1, T_NUM:T_NUM + 1], min_val=0, max_val=MAX_OVER)
            with pe.If(more > 0):
                with pe.Fori(0, more) as j:
                    pe.wait_ge(ylo_drained, 2 * (NE + j))
                    pe.wait_ge(yhi_drained, 2 * (NE + j))
                    ids(NE + 2 + j)
                    pe.wait_ge(gathered[0], 32 * (NE // 2 + 2 + j))
                    for part in range(3):
                        turn(part, 0, NE + 1 + j)
                    pe.wait_ge(t_drained, 3 * (NE + 2 + j))
                    one_round(NE + j, 0, [16 * (before[s] + 1 + NE // 2 + j) for s in moe_slots(0)], NE - 1 + j, None)
            pe.wait_ge(ylo_drained, 2 * (NE + more))
            pe.wait_ge(yhi_drained, 2 * (NE + more))
            pe.wait_ge(t_drained, 3 * (NE + 1 + more))
            pe.wait_ge(ids_ready, 2 * (NE + 2 + more))
            pe.wait_ge(gathered[1], 32 * (NE // 2 + 1))
            pe.wait_ge(ring_in[3], 16 * (1 + NE // 2 + more + 1))

            def embed(i):
                for j in range(2):
                    name = f"pp{i}{j}"
                    product(name, ps(name)[:, :], [(pT[:, k, i * P:(i + 1) * P], ring[:, 3, k * D + j * 512:k * D + (j + 1) * 512]) for k in range(2)])

            for i in range(NT - 2):
                embed(i)
            for sl in (1, 2):
                pe.wait_ge(ring_in[sl], 16 * (1 + NE // 2 + more + 1))
            for i in range(NT + 1):
                if i < NT:
                    norm_transposes("n3T", 2, [i])
                if i < 2:
                    embed(NT - 2 + i)
                if i >= 1:
                    for j in range(2):
                        wait_drained(pe, f"n3T{i - 1}{j}")
                    for j in range(2):
                        name = f"pg{i - 1}{j}"
                        product(name, ps(name)[:, :], [(nT[:, k, (i - 1) * P:i * P], slot3((1, 2)[j])[:, k, :]) for k in range(KD)])

        @block.scalar
        def _(act):
            ch = Chain(act, act_seq)

            def sumsq(i, dst, ready, value, done=sumsq_done):
                act.wait_ge(ready, value)
                nc.scalar.activation(ntok[:, i, :], h[:, i, :], ACT.Square, accum_out=dst).then_inc(done, 1)

            def drain(name, out, func=ACT.Identity, view=None, **kw):
                wait_full(act, name)
                nc.scalar.activation(out, ps(name)[:, 0:out.free_size()] if view is None else view, func, **kw).then_inc(act_drained, 1)

            def drain_norm(prefix, tiles=range(NT)):
                for i in tiles:
                    name = f"{prefix}{i}1"
                    drain(name, nT[:, 4:8, i * P:(i + 1) * P], view=ps(name)[:, :].rearrange("p (k t) -> p k t", k=4))

            for i in range(NT):
                sumsq(i, ssum[:, i:i + 1], x_in[i], 16)
            for i in range(NT):
                for j in range(2):
                    name = f"nT{i}{j}"
                    wait_full(act, name)
                    nc.scalar.activation(nT_hi[:, 4 * j:4 * j + 4, i, :], ps(name)[:, :].rearrange("p (k t) -> p k t", k=4),
                                         ACT.Copy).then_inc(nT_high, 1)
            split_high(act, "xr")
            act.wait_ge(halves_ready, 1)
            nc.scalar.activation(lexp, lab, ACT.Exp, scale=-1.0).then_inc(exp_lam, 1)
            act.wait_ge(norm_done, NT)
            act.dma_start(gB[:], g_ffn[0].partition_broadcast(P)).then_inc(gB_in, 16)
            split_high(act, "v")
            for j in range(2):
                name = f"wsT{j}"
                drain(name, wsT[:, 4 * j:4 * j + 4, :], view=ps(name)[:, :].rearrange("p (h t) -> p h t", h=4))
            split_high(act, "u")

            def fill(name):
                if name[0] == "v":
                    drain(name, v_tm[:, int(name[1]), :], ACT.Gelu_apprx_tanh)
                elif name[0] == "u":
                    drain(name, u_tm[:, int(name[1]), :], ACT.Gelu_apprx_tanh)
                elif name[:2] == "gr":
                    t0, n = SEGS[int(name[3])]
                    wait_full(act, "mix7")
                    drain(name, gr[:, int(name[2]), t0:t0 + n], ACT.Gelu_apprx_tanh)

            for unit in range(8):
                c, d = unit // 2, unit % 2
                col = d * C4 + c
                if unit == 0:
                    act.wait_ge(decay_ready, 1)
                else:
                    act.wait_ge(scan_part, 2 * unit)
                    if unit >= 2:
                        act.wait_ge(rec_sum, unit // 2)
                for g, dst in enumerate((TR, TI)):
                    for s, (t0, n) in enumerate(SEGS):
                        drain(f"gate{unit}{g}{s}", dst[:, t0:t0 + n], ACT.Tanh, scale=0.5, bias=hb[:, g * 8 + col:g * 8 + col + 1])
                act.wait_ge(act_drained, drain_count[f"gate{unit}01"])
                nc.scalar.activation(A0, TR, ACT.Exp, scale=c4[:, col:col + 1], bias=c4[:, col:col + 1]).then_inc(rec_exp, 1)
                nc.scalar.activation(TT, TR, ACT.Tanh, scale=c2[:, col:col + 1], bias=c2[:, col:col + 1]).then_inc(rec_exp, 1)
                def root():
                    act.wait_ge(rec_m2, unit + 1)
                    nc.scalar.activation(TR, TR, ACT.Sqrt, scale=0.25).then_inc(rec_mult, 1)

                if unit == 3:
                    split_high(act, "gr")
                if unit == 7:
                    root()
                for name in fillers[unit]:
                    fill(name)
                if unit < 7:
                    root()
                if unit == 6:
                    for i in range(NT):
                        act.wait_ge(dve_drained, drain_count["mix7"])
                        nc.scalar.activation(v_tm[:, i, :], u_tm[:, i, :], ACT.Square, accum_out=usum[:, i:i + 1]).then_inc(us_sq, 1)
                        act.wait_ge(us_sq, i + 1)
                    split_high(act, "wo0")
            for c in range(C4):
                for s, (t0, n) in enumerate(((0, 512), (512, 256))):
                    name = f"ysT{c}{s}"
                    wait_full(act, name)
                    nc.scalar.activation(ys_hi[:, c, t0:t0 + n], ps(name)[:, 0:n], ACT.Copy,
                                         scale=chan[:, G_SGU + c:G_SGU + c + 1]).then_inc(ys_high, 1)
            for c in range(C4):
                act.wait_ge(rec_y, c + 1)
                nc.scalar.activation(gr[:, c, :], xc[:, c, :], ACT.Square).then_inc(rec_sq, 1)
            for c in range(C4):
                nc.scalar.activation(xc_hi[:, c, :], xc[:, c, :], ACT.Copy, scale=chan[:, G_REC + c:G_REC + c + 1]).then_inc(rec_high, 1)
            split_high(act, "wo1")
            wait_full(act, "ssq")
            for i in range(NT + 1):
                if i < NT:
                    sumsq(i, ssum[:, NT + i:NT + i + 1], dve_drained, drain_count[f"out{i}1r"])
                if i == NT:
                    for k in range(2):
                        drain(f"pT{k}1", pT[:, k, 512:768])
                if i >= 1:
                    act.wait_ge(norm_done, NT + i)
                    act.dma_start(n2_dram[(i - 1) * P:i * P, :], ntok[:, i - 1, :]).then_inc(n2_stored, 16)
                    name = f"n2T{i - 1}1"
                    drain(name, n2T_buf[:, (i - 1) % 2, 4:8, :], view=ps(name)[:, :].rearrange("p (k t) -> p k t", k=4))
            act.dma_start(gB[:], g_ple[0].partition_broadcast(P)).then_inc(gB_in, 16)
            act.wait_ge(route_max, 1)
            nc.scalar.activation(gexp, gsh, ACT.Exp).then_inc(route_exp, 1)
            nc.scalar.activation(xe, m2, ACT.Exp).then_inc(route_exp, 1)

            def turned(part, par, t_at):
                act.wait_ge(t_full, 3 * t_at + part + 1)
                if part < 2:
                    nc.scalar.activation(moe["xT", par][:, 4 * part:4 * part + 4, 0:P],
                                         bank[4][:, :].rearrange("p (k s) -> p k s", k=4), ACT.Copy).then_inc(t_drained, 1)
                else:
                    nc.scalar.activation(moe["xT", par][:, :, P:CAP],
                                         bank[4][:, 0:KD * CAP2].rearrange("p (k s) -> p k s", k=KD), ACT.Copy).then_inc(t_drained, 1)

            def silu_half(r, half, first):
                act.wait_ge(gu_full, 2 * r + half + 1)
                if not first:
                    act.wait_ge(hid_done, 2 * r - 1 + half)
                nc.scalar.activation(silu[:, 2 * half:2 * half + 2, :],
                                     bank[2 * half][:, :].rearrange("p (f s) -> p f s", f=2)[:, :, 0:CAP], ACT.Silu).then_inc(silu_done, 1)

            def y_out(r, par, first, store_count):
                act.wait_ge(yhi_full, r + 1)
                if store_count is not None:
                    act.wait_ge(y_stored[par], store_count)
                nc.scalar.activation(moe["y", par][:, 512:D], bank[7][:, :], ACT.Copy).then_inc(yhi_drained, 1)
                act.wait_ge(thi_full, r + 1)
                nc.scalar.activation(moe["y2", par][:, 512:D], bank[5][0:CAP2, :], ACT.Copy).then_inc(yhi_drained, 1)
                act.wait_ge(yhi_drained, 2 * r + 2)
                act.wait_ge(ylo_drained, 2 * r + 2)
                act.dma_start(y_dram[bass.ds(r * CAP, P), :], moe["y", par]).then_inc(y_stored[par], 16)
                act.dma_start(y_dram[bass.ds(r * CAP + P, CAP2), :], moe["y2", par]).then_inc(y_stored[par], 16)

            def main_round(i, par, first):
                r = 2 * i + par
                silu_half(r, 0, first)
                turned(0, 1 - par, r + 1)
                silu_half(r, 1, first)
                turned(1, 1 - par, r + 1)
                turned(2, 1 - par, r + 1)
                y_out(r, par, first, None if isinstance(i, int) else 32 * i)

            for part in range(3):
                turned(part, 0, 0)
            main_round(0, 0, True)
            main_round(0, 1, False)
            with act.Fori(1, NE // 2) as i:
                main_round(i, 0, False)
                main_round(i, 1, False)
            more = act.value_load(table[0:1, T_NUM:T_NUM + 1], min_val=0, max_val=MAX_OVER)
            with act.If(more > 0):
                with act.Fori(0, more) as j:
                    for part in range(3):
                        turned(part, 0, NE + 1 + j)
                    silu_half(NE + j, 0, False)
                    silu_half(NE + j, 1, False)
                    y_out(NE + j, 0, False, 32 * (NE // 2 + j))
            def take_embed(i):
                for j in range(2):
                    drain(f"pp{i}{j}", pp_sb[2 * i + j])

            for i in range(NT - 2):
                take_embed(i)
            act.wait_ge(y_stored[0], 32 * (NE // 2 + more))
            act.wait_ge(y_stored[1], 32 * (NE // 2))
            act.dma_start(gF, g_final.partition_broadcast(P)).then_inc(gF_in, 16)
            for i in range(-2, NT + 1):
                if 0 <= i < NT:
                    drain_norm("n3T", [i])
                if 0 <= i < 2:
                    take_embed(NT - 2 + i)
                if i + 2 < NT:
                    sumsq(i + 2, ssum[:, 2 * NT + i + 2:2 * NT + i + 3], moe_added, 2 * (i + 3))
                if i < 1:
                    continue
                for j in range(2):
                    n = 2 * (i - 1) + j
                    name = f"pg{i - 1}{j}"
                    if n >= 2:
                        act.wait_ge(pgm_done, n - 1)
                    wait_full(act, name)
                    nc.scalar.activation(sig[:, n % 2, :], ps(name)[:, :], ACT.Sigmoid).then_inc(act_drained, 1)
                sumsq(i - 1, fsum[:, i - 1:i], h_ready, 2 * i, fin_sumsq)


        @block.vector
        def _(dve):
            ch = Chain(dve, dve_seq)
            link = ch.link
            V = nc.vector

            def drain(name, make):
                wait_full(dve, name)
                make(ps(name)).then_inc(dve_drained, 1)

            def normalise(k, i, gain_loads, src, scale):
                dve.wait_ge(rstd_done, k * NT + i + 1)
                dve.wait_ge(gB_in, 16 * gain_loads)
                V.scalar_tensor_tensor(out=ntok[:, i, :], in0=h[:, i, :], scalar=scale[:, src:src + 1], in1=gB[:],
                                       op0=ALU.mult, op1=ALU.mult).then_inc(norm_done, 1)

            def drain_norm(prefix, tiles=range(NT)):
                for i in tiles:
                    drain(f"{prefix}{i}0", lambda b, i=i: V.tensor_copy(nT[:, 0:4, i * P:(i + 1) * P], b[:, :].rearrange("p (k t) -> p k t", k=4)))

            def low_nT(i):
                for j in range(2):
                    dve.wait_ge(nT_high, 2 * i + j + 1)
                    drain(f"nT{i}{j}", lambda b: V.tensor_tensor(nT_lo[:, 4 * j:4 * j + 4, i, :], b[:, :].rearrange("p (k t) -> p k t", k=4),
                                                                 nT_hi[:, 4 * j:4 * j + 4, i, :].bitcast(F32), ALU.subtract))

            for i in range(NT):
                normalise(0, i, 1, i, rstd)
                if i:
                    low_nT(i - 1)
            low_nT(NT - 1)
            split_low(dve, V, "xr")
            drain("par", lambda b: V.tensor_copy(chan[:, :], b[:, 0:NPAR]))
            dve.wait_ge(dve_drained, drain_count["par"])
            link(V.tensor_scalar(nlam, chan[:, LAM:LAM + 8], -1.0, None, ALU.mult))
            V.tensor_tensor(lab, chan[:, LAM:LAM + 8], nlam, ALU.max).then_inc(halves_ready, 1)
            link(V.tensor_scalar(hb, chan[:, B_A:B_A + 16], 0.5, None, ALU.mult))
            for c in range(C4):
                if c == 1:
                    dve.wait_ge(exp_lam, 1)
                    link(V.tensor_scalar(lden, lexp, 2.0, None, ALU.add))
                    link(V.reciprocal(lden, lden))
                    link(V.tensor_tensor(ls, lexp, lden, ALU.mult))
                    link(V.tensor_tensor(ls2, ls, ls, ALU.mult))
                    link(V.tensor_scalar(lpoly, ls2, 1.0 / 15, 1.0 / 13, ALU.mult, ALU.add))
                    for n in (11, 9, 7, 5, 3, 1):
                        link(V.tensor_tensor(lpoly, lpoly, ls2, ALU.mult))
                        link(V.tensor_scalar(lpoly, lpoly, 1.0 / n, None, ALU.add))
                    link(V.scalar_tensor_tensor(out=lpoly, in0=lpoly, scalar=2.0, in1=ls, op0=ALU.mult, op1=ALU.mult))
                    link(V.scalar_tensor_tensor(out=sp, in0=nlam, scalar=0.0, in1=lpoly, op0=ALU.max, op1=ALU.add))
                    link(V.tensor_scalar(c4, sp, -4.0, None, ALU.mult))
                    V.tensor_scalar(c2, sp, 2.0, None, ALU.mult).then_inc(decay_ready, 1)
                for s, (t0, n) in enumerate(SEGS):
                    name = f"xr{c}{s}"
                    wait_full(dve, name)
                    x = ps(name)
                    tap = lambda k: chan[:, CONV_W + k * C4 + c:CONV_W + k * C4 + c + 1]
                    o = xc[:, c, t0:t0 + n]
                    link(V.tensor_scalar(o, x[:, 0:n], tap(2), chan[:, CONV_B + c:CONV_B + c + 1], ALU.mult, ALU.add))
                    link(V.scalar_tensor_tensor(out=o[:, 1:n], in0=x[:, 0:n - 1], scalar=tap(1), in1=o[:, 1:n], op0=ALU.mult, op1=ALU.add))
                    link(V.scalar_tensor_tensor(out=o[:, 2:n], in0=x[:, 0:n - 2], scalar=tap(0), in1=o[:, 2:n], op0=ALU.mult, op1=ALU.add))
                    V.scalar_tensor_tensor(out=o[:, 0:n - 1], in0=x[:, 1:n], scalar=tap(3), in1=o[:, 0:n - 1],
                                           op0=ALU.mult, op1=ALU.add).then_inc(dve_drained, 1)

            def fill(name):
                if name[0] == "v":
                    i = int(name[1])
                    v = v_tm[:, i, :]
                    dve.wait_ge(act_drained, drain_count[name])
                    dve.wait_ge(ln_in, 32)
                    link(V.bn_stats(bn[:, 6 * i:6 * i + 6], v))
                    V.bn_aggr(mv[:, 2 * i:2 * i + 2], bn[:, 6 * i:6 * i + 6]).then_inc(ln_var, 1)
                    dve.wait_ge(ln_rstd, i + 1)
                    link(V.tensor_scalar(v, v, mv[:, 2 * i:2 * i + 1], lrstd[:, i:i + 1], ALU.subtract, ALU.mult))
                    link(V.tensor_tensor(v, v, ln_g, ALU.mult))
                    V.tensor_tensor(v, v, ln_b, ALU.add).then_inc(v_ready, 1)
                elif name[:3] == "mix":
                    hh = int(name[3])
                    if hh == 0:
                        dve.wait_ge(act_drained, drain_count["u5"])
                    uu = u_tm[:, :, hh * HD:(hh + 1) * HD]
                    drain(name, lambda b: V.scalar_tensor_tensor(out=uu, in0=b[:, 0:NT * HD].rearrange("p (i c) -> p i c", i=NT),
                                                                 scalar=chan[:, B_S + hh:B_S + hh + 1], in1=uu, op0=ALU.add, op1=ALU.mult))

            for unit in range(8):
                c, d = unit // 2, unit % 2
                dve.wait_ge(act_drained, drain_count[f"gate{unit}11"])
                link(V.scalar_tensor_tensor(out=TI, in0=TI, scalar=1.0, in1=xc[:, c, :], op0=ALU.add, op1=ALU.mult))
                dve.wait_ge(rec_exp, 2 * (unit + 1))
                link(V.scalar_tensor_tensor(out=TT, in0=A0, scalar=1.0, in1=TT, op0=ALU.add, op1=ALU.mult))
                link(V.tensor_scalar(A0, TT, -1.0, 1.0, ALU.mult, ALU.add))
                V.scalar_tensor_tensor(out=TR, in0=A0, scalar=1.0, in1=TT, op0=ALU.add, op1=ALU.mult).then_inc(rec_m2, 1)
                for name in fillers[unit]:
                    fill(name)
                dve.wait_ge(rec_mult, unit + 1)
                link(V.tensor_tensor(TI, TI, TR, ALU.mult))
                for s, (t0, n) in enumerate(SEGS):
                    if d == 0:
                        q = V.tensor_tensor_scan(HF[:, t0:t0 + n], A0[:, t0:t0 + n], TI[:, t0:t0 + n], 0.0, ALU.mult, ALU.add)
                    else:
                        rev = slice(t0 + n - 1, t0 - 1 if t0 else None, -1)
                        q = V.tensor_tensor_scan(TT[:, rev], A0[:, rev], TI[:, rev], 0.0, ALU.mult, ALU.add)
                    q.then_inc(scan_part, 1)
                dve.wait_ge(scan_part, 2 * (unit + 1))
                if d == 1:
                    V.tensor_tensor(xc[:, c, :], HF, TT, ALU.add).then_inc(rec_sum, 1)
                if unit == 6:
                    dve.wait_ge(us_rstd, 1)
                    for i in range(NT):
                        V.tensor_scalar(u_tm[:, i, :], u_tm[:, i, :], urstd[:, i:i + 1], None, ALU.mult).then_inc(us_scaled, 1)
            for c in range(C4):
                for s, (t0, n) in enumerate(((0, 512), (512, 256))):
                    dve.wait_ge(ys_high, 2 * c + s + 1)
                    drain(f"ysT{c}{s}", lambda b: V.scalar_tensor_tensor(out=ys_lo[:, c, t0:t0 + n], in0=b[:, 0:n], scalar=chan[:, G_SGU + c:G_SGU + c + 1],
                                                                         in1=ys_hi[:, c, t0:t0 + n].bitcast(F32), op0=ALU.mult, op1=ALU.subtract))
            for c in range(C4):
                dve.wait_ge(rec_sum, c + 1)
                dve.wait_ge(act_drained, drain_count[f"gr{c}1"])
                V.tensor_tensor(xc[:, c, :], xc[:, c, :], gr[:, c, :], ALU.mult).then_inc(rec_y, 1)
            for c in range(C4):
                dve.wait_ge(rec_high, c + 1)
                V.scalar_tensor_tensor(out=xc_lo[:, c, :], in0=xc[:, c, :], scalar=chan[:, G_REC + c:G_REC + c + 1],
                                       in1=xc_hi[:, c, :].bitcast(F32), op0=ALU.mult, op1=ALU.subtract).then_inc(rec_g, 1)
            def add_out(i, j, g):
                hs = h[:, i, j * 512:(j + 1) * 512]
                name = f"out{i}{j}{g}"
                if g == "r":
                    drain(name, lambda b: V.scalar_tensor_tensor(out=hs, in0=b[:, :], scalar=rrstd[:, i:i + 1], in1=hs, op0=ALU.mult, op1=ALU.add))
                else:
                    drain(name, lambda b: V.tensor_tensor(hs, b[:, :], hs, ALU.add))
                dve.wait_ge(dve_drained, drain_count[name])

            for n, (g, i) in enumerate(first_half):
                if g == "ssq":
                    drain("ssq", lambda b: V.tensor_copy(rsum, b[:, 0:NT]))
                    dve.wait_ge(rr_rstd, 1)
                    continue
                if n < 4 or i >= 4:
                    dve.wait_ge(x_in[i], 32)
                add_out(i, 0, g)
                if n == 8:
                    split_low(dve, V, "wo1")
            dve.wait_ge(wr_in, 64)

            def take_n2T(i):
                drain(f"n2T{i}0", lambda b: V.tensor_copy(n2T_buf[:, i % 2, 0:4, :], b[:, :].rearrange("p (k t) -> p k t", k=4)))

            def take_logits(i):
                drain(f"route{i}", lambda b: V.tensor_tensor(logit[:, i, :], b[:, 0:NG + NE], br[:, :], ALU.add))

            for i in range(NT):
                add_out(i, 1, "s")
                if i >= 1:
                    normalise(1, i - 1, 2, NT + i - 1, rstd)
                add_out(i, 1, "r")
                if i >= 1:
                    take_n2T(i - 1)
                if i >= 2:
                    take_logits(i - 2)
            for k in range(2):
                drain(f"pT{k}0", lambda b, k=k: V.tensor_copy(pT[:, k, 0:512], b[:, :]))
            normalise(1, NT - 1, 2, 2 * NT - 1, rstd)
            take_n2T(NT - 1)
            take_logits(NT - 2)
            take_logits(NT - 1)

            b3 = lambda a: a.unsqueeze(2).to_broadcast([P, NT, 4])
            idx4 = iota[:, 0:4].unsqueeze(1).to_broadcast([P, NT, 4])
            idxm = iota4[:, :].unsqueeze(1).to_broadcast([P, NT, 4])
            dve.wait_ge(dve_drained, drain_count[f"route{NT - 1}"])

            def first_max(x, mx, idx, onehot4):
                link(V.tensor_reduce(mx, x, AX.X, ALU.max))
                link(V.tensor_tensor(cand, x, b3(mx), ALU.is_equal))
                link(V.scalar_tensor_tensor(out=cand, in0=cand, scalar=-4.0, in1=idx4, op0=ALU.mult, op1=ALU.add))
                link(V.tensor_reduce(idx, cand, AX.X, ALU.min))
                link(V.tensor_tensor(onehot4, idxm, b3(idx), ALU.is_equal))

            first_max(logit[:, :, 0:NG], gmax, gidx, gone)
            link(V.tensor_tensor(gsh, logit[:, :, 0:NG], b3(gmax), ALU.subtract))
            link(V.tensor_tensor(e16, logit[:, :, NG:].rearrange("p i (g e) -> p i g e", g=NG),
                                 gone.unsqueeze(3).to_broadcast([P, NT, NG, NEG]), ALU.mult))
            link(V.tensor_reduce(el, e16.rearrange("p i g e -> p i e g"), AX.X, ALU.add))
            first_max(el, m1, i1, one1)
            link(V.scalar_tensor_tensor(out=el2, in0=one1, scalar=MASKED, in1=el, op0=ALU.mult, op1=ALU.add))
            first_max(el2, m2, i2, one2)
            V.tensor_tensor(m2, m2, m1, ALU.subtract).then_inc(route_max, 1)
            dve.wait_ge(route_max, 1)
            for oh, one in ((oh1, one1), (oh2, one2)):
                o4 = oh.rearrange("p i (g e) -> p i g e", g=NG)
                link(V.tensor_copy(o4, gone.unsqueeze(3).to_broadcast([P, NT, NG, NEG])))
                link(V.tensor_tensor(o4, o4, one.unsqueeze(2).to_broadcast([P, NT, NG, NEG]), ALU.mult))
            link(V.tensor_tensor(chose, oh1, oh2, ALU.add))
            V.tensor_copy(choseb[:].rearrange("p (i e) -> p i e", i=NT), chose).then_inc(chosen, 1)
            wait_full(dve, "rank")
            ranks = ps("rank")[:, 0:NT * NE].rearrange("p (i e) -> p i e", i=NT)
            link(V.scalar_tensor_tensor(out=pick, in0=ranks, scalar=1.0, in1=chose, op0=ALU.add, op1=ALU.mult))
            link(V.tensor_scalar(rankm[:, 0:NE, :], pick.rearrange("p i e -> p e i"), -1.0, None, ALU.add))

            def make_onehot(at, e, ramp):
                if not (isinstance(at, int) and at == 0):
                    dve.wait_ge(ids_full, at)
                V.tensor_tensor(onehot, ramp.unsqueeze(1).to_broadcast([P, NT, CAP]),
                                rankm[:, bass.ds(e, 1), :].rearrange("p a i -> p (a i)").unsqueeze(2).to_broadcast([P, NT, CAP]),
                                ALU.is_equal).then_inc(onehot_ready, 1)

            def take_ids(at, par, gathered_before):
                dve.wait_ge(ids_full, at + 1)
                if gathered_before is not None:
                    dve.wait_ge(gathered[par], gathered_before)
                V.tensor_reduce(idsf[:, par, 0:1], bank[5][:, 0:2], AX.X, ALU.add).then_inc(ids_sum, 1)
                V.tensor_reduce(idsf[0:CAP2, par, 1:2], bank[5][0:CAP2, 2:4], AX.X, ALU.add).then_inc(ids_sum, 1)
                dve.wait_ge(ids_sum, 2 * at + 2)
                V.tensor_copy(idsi[:, par, 0:1], idsf[:, par, 0:1]).then_inc(ids_ready, 1)
                V.tensor_copy(idsi[0:CAP2, par, 1:2], idsf[0:CAP2, par, 1:2]).then_inc(ids_ready, 1)

            make_onehot(0, 0, iota[:])
            link(V.tensor_copy(rank, ranks))
            V.tensor_copy(nexp, ps("rank")[:, NT * NE:(NT + 1) * NE]).then_inc(dve_drained, 1)
            take_ids(0, 0, None)
            make_onehot(1, 1, iota[:])
            take_ids(1, 1, None)
            for b in range(4):
                link(V.memset(bank[b][:, :], 0.0))
            link(V.memset(bank[5][:, 8:], 0.0))
            make_onehot(2, 2, iota[:])
            dve.wait_ge(route_exp, 2)
            link(V.tensor_reduce(gsum, gexp, AX.X, ALU.add))
            link(V.tensor_scalar(den, xe, 1.0, None, ALU.add))
            link(V.tensor_tensor(den, den, gsum, ALU.mult))
            link(V.reciprocal(wt1, den))
            link(V.tensor_tensor(wt2, wt1, xe, ALU.mult))
            for q in range(4):
                link(V.tensor_scalar(oq[:, q, :], nexp, float(CAP * (q + 1)), None, ALU.is_gt))
            link(V.tensor_reduce(over, oq.rearrange("p q e -> p e q"), AX.X, ALU.add))
            link(V.memset(base, 1.0))
            link(V.tensor_tensor_scan(incl, base, over, 0.0, ALU.mult, ALU.add))
            link(V.tensor_tensor(excl, incl, over, ALU.subtract))
            link(V.tensor_scalar(base, excl, float(CAP), float((NE - 1) * CAP), ALU.mult, ALU.add))
            link(V.tensor_scalar(lt, rank, float(CAP), None, ALU.is_lt))
            bE = lambda a: a.unsqueeze(1).to_broadcast([P, NT, NE])
            link(V.tensor_scalar(slotm, bE(iota16[:]), float(CAP), None, ALU.mult))
            link(V.tensor_tensor(slotm, slotm, bE(base), ALU.subtract))
            link(V.tensor_tensor(slotm, slotm, lt, ALU.mult))
            link(V.tensor_tensor(slotm, slotm, bE(base), ALU.add))
            link(V.tensor_tensor(slotm, slotm, rank, ALU.add))
            for a, oh in enumerate((oh1, oh2)):
                link(V.tensor_tensor(pick, oh, slotm, ALU.mult))
                link(V.tensor_reduce(slotf[:, a, :], pick, AX.X, ALU.add))
                link(V.tensor_copy(slots[:, a, :], slotf[:, a, :]))
            bJ = lambda a: a.unsqueeze(1).to_broadcast([P, MAX_OVER, NE])
            jE = lambda a: a.unsqueeze(2).to_broadcast([P, MAX_OVER, NE])
            link(V.tensor_tensor(ojn, bJ(incl), jE(iotaj), ALU.is_le))
            link(V.tensor_reduce(jexp, ojn, AX.X, ALU.add))
            link(V.tensor_tensor(ojn, bJ(iota16[:]), jE(jexp), ALU.is_equal))
            link(V.tensor_tensor(oj2, ojn, bJ(excl), ALU.mult))
            link(V.tensor_reduce(jfirst, oj2, AX.X, ALU.add))
            link(V.tensor_tensor(oj2, ojn, bJ(nexp), ALU.mult))
            link(V.tensor_reduce(jcnt, oj2, AX.X, ALU.add))
            link(V.tensor_tensor(jfirst, iotaj, jfirst, ALU.subtract))
            link(V.tensor_scalar(offs[:], jfirst, 1.0, float(CAP), ALU.add, ALU.mult))
            link(V.tensor_tensor(jcnt, jcnt, offs[:], ALU.subtract))
            link(V.tensor_scalar(jcnt, jcnt, 0.0, None, ALU.max))
            link(V.tensor_scalar(jexp, jexp, float(NE - 1), None, ALU.min))
            link(V.memset(table[:], 0))
            link(V.tensor_copy(table[:, T_NUM:T_NUM + 1], incl[:, NE - 1:NE]))
            link(V.tensor_copy(table[:, T_EXP:T_EXP + MAX_OVER], jexp))
            link(V.tensor_copy(table[:, T_COUNT:T_COUNT + NE], nexp))
            V.tensor_copy(table[:, T_COUNT + NE:T_COUNT + NROUND], jcnt).then_inc(routed, 1)


            def hid_half(r, half):
                dve.wait_ge(silu_done, 2 * r + half + 1)
                V.tensor_tensor(hid[:, 2 * half:2 * half + 2, :], silu[:, 2 * half:2 * half + 2, :],
                                bank[2 * half + 1][:, :].rearrange("p (f s) -> p f s", f=2)[:, :, 0:CAP], ALU.mult).then_inc(hid_done, 1)

            def y_out(r, par, store_count):
                dve.wait_ge(ylo_full, r + 1)
                if store_count is not None:
                    dve.wait_ge(y_stored[par], store_count)
                V.tensor_copy(moe["y", par][:, 0:512], bank[6][:, :]).then_inc(ylo_drained, 1)
                dve.wait_ge(tlo_full, r + 1)
                V.tensor_copy(moe["y2", par][:, 0:512], bank[4][0:CAP2, :]).then_inc(ylo_drained, 1)

            dve.wait_ge(routed, 1)

            def main_round(i, par):
                r = 2 * i + par
                hid_half(r, 0)
                take_ids(r + 2, par, 32 * (i + 1))
                hid_half(r, 1)
                y_out(r, par, None if isinstance(i, int) else 32 * i)

            main_round(0, 0)
            make_onehot(3, 3, iota[:])
            main_round(0, 1)
            with dve.Fori(1, NE // 2) as i:
                for par in range(2):
                    make_onehot(2 * i + par + 2, 2 * i + par + 2, iota[:])
                    main_round(i, par)
            more = dve.value_load(table[0:1, T_NUM:T_NUM + 1], min_val=0, max_val=MAX_OVER)
            with dve.If(more > 0):
                with dve.Fori(0, more) as j:
                    e = dve.value_load(table[0:1, bass.ds(j + T_EXP, 1)], min_val=0, max_val=NE - 1)
                    dve.wait_ge(onehot_ready, NE + 2 + j)
                    V.tensor_scalar(iota_o, iota[:], offs[:, bass.ds(j, 1)], None, ALU.add).then_inc(ramp_ready, 1)
                    dve.wait_ge(ramp_ready, j + 1)
                    make_onehot(NE + 2 + j, e, iota_o)
                    take_ids(NE + 2 + j, 0, 32 * (NE // 2 + 1 + j))
                    hid_half(NE + j, 0)
                    hid_half(NE + j, 1)
                    y_out(NE + j, 0, 32 * (NE // 2 + j))
            def final_norm(i):
                dve.wait_ge(fin_rstd, i + 1)
                dve.wait_ge(gF_in, 16)
                V.scalar_tensor_tensor(out=ntok[:, i, :], in0=h[:, i, :], scalar=frstd[:, i:i + 1], in1=gF,
                                       op0=ALU.mult, op1=ALU.mult).then_inc(fin_norm, 1)

            for i in range(-2, NT + 1):
                if 0 <= i < NT:
                    drain_norm("n3T", [i])
                if 0 <= i + 1 < NT:
                    normalise(2, i + 1, 3, 2 * NT + i + 1, rstd)
                if i + 2 < NT:
                    for a, wt in enumerate((wt1, wt2)):
                        n = 2 * (i + 2) + a
                        hs = h[:, i + 2, :]
                        dve.wait_ge(yg_in[n % NYG], 16 * (n // NYG + 1))
                        V.scalar_tensor_tensor(out=hs, in0=yg(n), scalar=wt[:, i + 2:i + 3], in1=hs,
                                               op0=ALU.mult, op1=ALU.add).then_inc(moe_added, 1)
                        dve.wait_ge(moe_added, n + 1)
                if i >= 2:
                    final_norm(i - 2)
                if i < 1:
                    continue
                for j in range(2):
                    n = 2 * (i - 1) + j
                    dve.wait_ge(act_drained, drain_count[f"pg{i - 1}{j}"])
                    V.tensor_tensor(pgm[:, n % 2, :], pp_sb[n], sig[:, n % 2, :], ALU.mult).then_inc(pgm_done, 1)
                    dve.wait_ge(pgm_done, n + 1)
                    hs = h[:, i - 1, j * 512:(j + 1) * 512]
                    V.tensor_tensor(hs, hs, pgm[:, n % 2, :], ALU.add).then_inc(h_ready, 1)
                    dve.wait_ge(h_ready, n + 1)
            final_norm(NT - 1)


_INS = ["x_prompt", "x_sample", "p_prompt", "p_sample", "g_mix", "w_in", "conv_w", "conv_b", "lru_w_a", "lru_b_a",
        "lru_w_x", "lru_b_x", "lru_lambda", "sgu_ln_g", "sgu_ln_b", "sgu_w_s", "sgu_b_s", "g_rec_out", "g_sgu_out",
        "w_out", "g_ffn", "w_router_group", "b_router_group", "w_router_expert", "b_router_expert", "w_exp_gate",
        "w_exp_up", "w_exp_down", "g_ple", "w_ple_gate", "w_ple_proj", "g_final"]
_SQUEEZE = {"x_prompt": 1, "x_sample": 1, "p_prompt": 2, "p_sample": 2, "w_in": 1, "conv_w": 1, "lru_w_a": 1,
            "lru_b_a": 1, "lru_w_x": 1, "lru_b_x": 1, "lru_lambda": 1, "sgu_w_s": 1, "sgu_b_s": 1, "w_out": 1,
            "w_router_group": 1, "w_router_expert": 1, "w_exp_gate": 1, "w_exp_up": 1, "w_exp_down": 1,
            "w_ple_gate": 1, "w_ple_proj": 1}


def kernel(**inputs):
    import numpy as _np
    import concourse.bacc as _bacc
    from concourse import mybir as _mybir
    from concourse.bass_utils import run_bass_kernel_spmd as _run

    nc = _bacc.Bacc("TRN2", target_bir_lowering=False, num_devices=1, dynamic_dma_scratch_size=8192)
    arrays, args = {}, []
    for name in _INS:
        a = _np.ascontiguousarray(inputs[name])
        a = a.reshape(a.shape[_SQUEEZE.get(name, 0):])
        arrays[f"in_{name}"] = a
        args.append(nc.dram_tensor(f"in_{name}", a.shape, _mybir.dt.from_np(a.dtype), kind="ExternalInput").ap())
    for name, n in (("y_prompt", NPROMPT), ("y_sample", NSAMPLE)):
        args.append(nc.dram_tensor(name, (n, D), F32, kind="ExternalOutput").ap())
    hybrid_encoder_kernel(nc, *args)
    r = _run(nc, [arrays], core_ids=[0])
    return (r.results[0]["y_prompt"].reshape(1, NPROMPT, D), r.results[0]["y_sample"].reshape(1, NSAMPLE, D))
```

```python
from contextlib import ExitStack

import concourse.bass as bass
from concourse import mybir

F32 = mybir.dt.float32
F32R = mybir.dt.float32r
BF16 = mybir.dt.bfloat16
I32 = mybir.dt.int32
ALU = mybir.AluOpType
ACT = mybir.ActivationFunctionType
AX = mybir.AxisListType

P = 128
D = 1024
KD = D // P
NPROMPT, NSAMPLE = 256, 512
NTOK = NPROMPT + NSAMPLE
NT = NTOK // P
SEGS = [(0, NPROMPT), (NPROMPT, NSAMPLE)]
DR = 512
C4 = DR // P
NH = 8
HD = DR // NH
NG, NEG = 4, 4
NE = NG * NEG
DE = 512
F4 = DE // P
DPLE = 256
EPS = 1e-6
CAP = 160
CAP2 = CAP - P
NO_ROWS = 4
FEW = 96
MAX_OVER = 2 * NTOK // CAP
NROUND = NE + MAX_OVER
NSLOT = NROUND * CAP
CLASSES = (64, 80, 96, 112, 128, 144, 160)
NYG = 4
MASKED = -3.0e38

CONV_W, CONV_B, B_A, B_X, LAM, G_REC, G_SGU, B_S = 0, 16, 20, 28, 36, 44, 48, 52
NPAR = 60


def hybrid_encoder_kernel(nc, x_prompt, x_sample, p_prompt, p_sample, g_mix, w_in, conv_w, conv_b, lru_w_a,
                          lru_b_a, lru_w_x, lru_b_x, lru_lambda, sgu_ln_g, sgu_ln_b, sgu_w_s, sgu_b_s,
                          g_rec_out, g_sgu_out, w_out, g_ffn, w_router_group, b_router_group,
                          w_router_expert, b_router_expert, w_exp_gate, w_exp_up, w_exp_down, g_ple,
                          w_ple_gate, w_ple_proj, g_final, y_prompt, y_sample):
    n2_dram = nc.dram_tensor("n2_scratch", (NTOK, D), F32, kind="Internal").ap()
    y_dram = nc.dram_tensor("y_scratch", (NSLOT, D), F32, kind="Internal").ap()

    def token_rows(prompt, sample, i):
        src, at = (prompt, i) if i < 2 else (sample, i - 2)
        return src[at * P:(at + 1) * P, :]

    with ExitStack() as ctx:
        def sb(name, shape, dt=F32):
            return ctx.enter_context(nc.sbuf_tensor(name, shape, dt))

        def sem(name):
            return ctx.enter_context(nc.semaphore(name))

        big_at = [(nc.sbuf_usable_end - 4 * (6 * 4096 + 3 * NT * D + 5 * NTOK + C4 * NTOK + NH * P)) // 32 * 32]

        def region(name, shape):
            at = big_at[0]
            big_at[0] += 4 * shape[1] * (shape[2] if len(shape) > 2 else 1)
            return (nc.alloc_sbuf_tensor_at(name, shape, F32, offset=at),
                    nc.alloc_sbuf_tensor_at(name + "_r", shape, F32R, offset=at))

        ring, ringR = region("ring", [P, 6, 4096])
        h, hR = region("h", [P, NT, D])
        regT, regTR = region("regT", [P, KD * NTOK])
        regN, regNR = region("regN", [P, NT * D])
        regR, regRR = region("regR", [P, 5 * NTOK])
        regX, regXR = region("regX", [P, C4 * NTOK])
        wsT, wsTR = region("wsT", [P, NH, P])

        def slot3(s):
            return ring[:, s, :].rearrange("p (k n) -> p k n", k=KD)

        early = ring[:, 5, :]
        wbd = early[:, 0:2048]
        w_s = early[:, 2048:3072].rearrange("p (h s) -> p h s", h=NH)
        ln_g = early[:, 3072:3584]
        ln_b = early[:, 3584:4096]
        nT_hi = regTR[:, :].rearrange("p (i k t) -> p k i t", i=NT, k=KD)
        nT_lo = hR[:, :, :].rearrange("p i (k t) -> p k i t", k=KD)
        ys_hi = regTR[:, 0:C4 * NTOK].rearrange("p (c t) -> p c t", c=C4)
        ys_lo = regTR[:, C4 * NTOK:2 * C4 * NTOK].rearrange("p (c t) -> p c t", c=C4)
        xc_hi = ringR[:, 2, 0:C4 * NTOK].rearrange("p (c t) -> p c t", c=C4)
        xc_lo = regXR[:, :].rearrange("p (c t) -> p c t", c=C4)
        SPLIT = {"xr": (0, 1), "v": (2, 3), "u": (4, 0), "gr": (1, 2), "wo0": (3, 4), "wo1": (0, 1), "pg0": (1, 4), "pg1": (2, 5)}
        n3T_hi, n3T_lo = (regTR[:, 0:4 * D].rearrange("p (b a k t) -> p b a k t", b=2, a=2, k=KD)[:, :, a] for a in range(2))
        yg_buf = [regT[:, 4 * D:5 * D], regT[:, 5 * D:6 * D], regX[:, NT * DPLE:NT * DPLE + D],
                  wsT[:, :, :].rearrange("p h t -> p (h t)")]
        n2T_buf = regR[:, 0:2 * D].rearrange("p (b k t) -> p b k t", b=2, k=KD)
        ntok = regN[:, :].rearrange("p (i d) -> p i d", i=NT)
        v_tm = regN[:, 0:NT * DR].rearrange("p (i d) -> p i d", i=NT)
        u_tm = regN[:, NT * DR:2 * NT * DR].rearrange("p (i d) -> p i d", i=NT)
        gr = regN[:, 0:C4 * NTOK].rearrange("p (c t) -> p c t", c=C4)
        TR, TI, A0, TT, HF = (regR[:, j * NTOK:(j + 1) * NTOK] for j in range(5))
        xc = regX[:, :].rearrange("p (c t) -> p c t", c=C4)

        ident = sb("ident", [P, P])
        zeros = sb("zeros", [P, 512])
        ones = sb("ones", [P, 2])
        gB = sb("gB", [P, D])
        par_rows = regR[0:NPAR, 0:P]
        chan = sb("chan", [P, NPAR])
        wr = sb("wr", [P, KD, NG + NE])
        br = sb("br", [P, NG + NE])
        tri = sb("tri", [P, P], BF16)
        onesb = sb("onesb", [P, P], BF16)
        tokid = sb("tokid", [P, NT, 2], BF16)
        iota = sb("iota", [P, CAP])
        iota16 = sb("iota16", [P, NE])
        iota4 = sb("iota4", [P, 4])
        small = sb("small", [P, 400])
        rankm = sb("rankm", [P, NE + 2, NT])
        table = sb("table", [P, 64], I32)
        slots = sb("slots", [P, 2, NT], I32)
        idsi = sb("idsi", [P, 2, 2], I32)
        idsf = sb("idsf", [P, 2, 2])
        offs = sb("offs", [P, MAX_OVER])
        iota_o = regR[:, 2200:2200 + CAP]
        onehot = regR[:, 2400:2400 + NT * CAP // 2].bitcast(BF16).rearrange("p (i s) -> p i s", i=NT)

        taken = [0]

        def tiny(n):
            at = taken[0]
            taken[0] += n
            assert taken[0] <= 400
            return small[:, at:at + n]

        nhalf = tiny(8)
        iotaj = tiny(MAX_OVER)
        moe = {}
        at = 0
        for b in range(2):
            moe["xg", b] = regT[:, at:at + D]
            moe["y", b] = regN[:, at:at + D]
            at += D
        for b in range(2):
            moe["xg2", b] = regT[0:CAP2, at:at + D]
            moe["y2", b] = regN[0:CAP2, at:at + D]
            at += D
        for b in range(2):
            moe["xT", b] = (regT if b == 0 else regN)[:, at:at + KD * CAP].rearrange("p (k s) -> p k s", k=KD)
        p_tm = early[:, 2048:2048 + NT * DPLE].rearrange("p (i d) -> p i d", i=NT)
        pT = regX[:, 0:NT * DPLE].rearrange("p (k t) -> p k t", k=2)
        sig = regR[:, 0:1024].rearrange("p (b n) -> p b n", b=2)
        pgm = regR[:, 1024:2048].rearrange("p (b n) -> p b n", b=2)
        gF = regR[:, 2048:2048 + D]
        pp_sb = [ring[:, 0, n * 512:(n + 1) * 512] if n < 8 else ring[:, 3, (n - 4) * 512:(n - 3) * 512] for n in range(2 * NT)]
        silu = regR[:, 0:F4 * CAP].rearrange("p (f s) -> p f s", f=F4)
        hid = regR[:, F4 * CAP:2 * F4 * CAP].rearrange("p (f s) -> p f s", f=F4)

        hid_hi = regRR[:, 2 * F4 * CAP:3 * F4 * CAP].rearrange("p (f s) -> p f s", f=F4)
        hid_lo = regRR[:, F4 * CAP:2 * F4 * CAP].rearrange("p (f s) -> p f s", f=F4)
        spare = at + KD * CAP
        wsT_flat = wsTR[:, :, :].rearrange("p h t -> p (h t)")
        down_hi = [[wsT_flat[:, 0:512], wsT_flat[:, 512:1024]],
                   [regXR[:, NT * DPLE:NT * DPLE + 512], regXR[:, NT * DPLE + 512:NT * DPLE + 1024]],
                   [regXR[:, NT * DPLE + 1024:NT * DPLE + 1536], regTR[:, spare:spare + 512]],
                   [regNR[:, spare:spare + 512], regRR[:, 2880:3392]]]

        def down_part(par, f, j):
            return ring[:, moe_slots(par)[2], f * D + j * 512:f * D + (j + 1) * 512]

        def down_low(par, f, j):
            return ringR[:, moe_slots(par)[2], f * D + j * 512:f * D + (j + 1) * 512]

        bank = [ctx.enter_context(nc.psum_tensor(f"bank{b}", [P, 512], F32)) for b in range(8)]

        x_in = [sem(f"x_in{i}") for i in range(NT)]
        ring_in = [sem(f"ring_in{s}") for s in range(6)]
        par_in = sem("par_in")
        wbd_in, ws_in, ln_in, wr_in, gB_in = sem("wbd_in"), sem("ws_in"), sem("ln_in"), sem("wr_in"), sem("gB_in")
        consts = sem("consts")
        filled = sem("filled")
        act_drained = sem("act_drained")
        dve_drained = sem("dve_drained")
        act_seq, dve_seq, pool_seq = sem("act_seq"), sem("dve_seq"), sem("pool_seq")
        sumsq_done, rstd_done, norm_done = sem("sumsq_done"), sem("rstd_done"), sem("norm_done")
        ln_var, ln_rstd, v_ready = sem("ln_var"), sem("ln_rstd"), sem("v_ready")
        zeroed = sem("zeroed")
        halves_ready, exp_lam, decay_ready = sem("halves_ready"), sem("exp_lam"), sem("decay_ready")
        rec_exp, rec_m2, rec_mult = sem("rec_exp"), sem("rec_m2"), sem("rec_mult")
        scan_part, rec_sum = sem("scan_part"), sem("rec_sum")
        us_sq, us_rstd, us_scaled = sem("us_sq"), sem("us_rstd"), sem("us_scaled")
        rec_y, rec_sq, rec_g = sem("rec_y"), sem("rec_sq"), sem("rec_g")
        rr_rstd = sem("rr_rstd")
        h_ready = sem("h_ready")
        n2_stored = sem("n2_stored")
        hi_ready = {u: sem(f"hi_ready_{u}") for u in SPLIT}
        lo_ready = {u: sem(f"lo_ready_{u}") for u in SPLIT}
        nT_high, ys_high, rec_high, n3T_high = sem("nT_high"), sem("ys_high"), sem("rec_high"), sem("n3T_high")
        route_max, route_exp, chosen, routed = sem("route_max"), sem("route_exp"), sem("chosen"), sem("routed")
        slots_ready = sem("slots_ready")
        ids_sum, ramp_ready = sem("ids_sum"), sem("ramp_ready")
        turn_go, gather_go = sem("turn_go"), sem("gather_go")
        last_over, store_go = sem("last_over"), sem("store_go")
        onehot_ready, ids_full, ids_ready = sem("onehot_ready"), sem("ids_full"), sem("ids_ready")
        gathered = [sem("gathered0"), sem("gathered1")]
        t_full, t_drained = sem("t_full"), sem("t_drained")
        gu_full, silu_done, hid_done = sem("gu_full"), sem("silu_done"), sem("hid_done")
        hid_raw, hid_high = sem("hid_raw"), sem("hid_high")
        down_high_done, down_low_done = sem("down_high_done"), sem("down_low_done")
        ylo_full, yhi_full = sem("ylo_full"), sem("yhi_full")
        tlo_full, thi_full = sem("tlo_full"), sem("thi_full")
        ylo_drained, yhi_drained = sem("ylo_drained"), sem("yhi_drained")
        y_stored = [sem("y_stored0"), sem("y_stored1")]
        yg_in = [sem(f"yg_in{b}") for b in range(NYG)]
        p_in = sem("p_in")
        moe_added = sem("moe_added")
        gF_in, pgm_done = sem("gF_in"), sem("pgm_done")
        fin_sumsq, fin_rstd, fin_norm = sem("fin_sumsq"), sem("fin_rstd"), sem("fin_norm")
        stored = sem("stored")

        groups = [(f"nT{i}{j}", "dve") for i in range(NT) for j in range(2)]
        groups += [("par", "dve")]
        groups += [(f"xr{c}{s}", "dve") for c in range(C4) for s in range(2)]
        groups += [(f"wsT{j}", "act") for j in range(2)]
        fillers = [[f"v{2 * j + a}" for a in range(2)] for j in range(3)]
        fillers += [[f"u{2 * j + a}" for a in range(2)] for j in range(3)]
        gates_right = [f"gr{c}{s}" for c in range(C4) for s in range(2)]
        fillers += [[f"mix{hh}" for hh in range(NH)] + gates_right[:4], gates_right[4:]]
        for unit in range(8):
            groups += [(f"gate{unit}{g}{s}", "act") for g in range(2) for s in range(2)]
            groups += [(x, "dve" if x[:3] == "mix" else "act") for x in fillers[unit]]
        ys_order = [(c, s) for s in range(2) for c in range(C4)]
        groups += [(f"ysT{c}{s}", "dve") for c, s in ys_order]
        first_half = [("s", i) for i in range(4)] + [("ssq", 0)] + [("r", i) for i in range(4)]
        first_half += [(g, i) for i in range(4, NT) for g in "sr"]
        groups += [("ssq" if g == "ssq" else f"out{i}0{g}", "dve") for g, i in first_half]
        pT_groups = [(f"pT{k}{s}", "act" if s else "dve") for k in range(2) for s in range(2)]
        for i in range(NT + 2):
            if i < NT:
                groups += [(f"out{i}1{g}", "dve") for g in "sr"]
            if i == NT:
                groups += pT_groups
            if 1 <= i <= NT:
                groups += [(f"n2T{i - 1}{j}", "act" if j else "dve") for j in range(2)]
            if i >= 2:
                groups += [(f"route{i - 2}", "dve")]
        groups += [("rank", "dve")]
        number = {name: n for n, (name, _) in enumerate(groups)}
        drain_count, seen = {}, {"act": 0, "dve": 0}
        for name, who in groups:
            seen[who] += 1
            drain_count[name] = seen[who]
        NGROUP = len(groups)
        late = [(f"pp{i}{j}", "act") for i in range(NT - 2) for j in range(2)]
        for i in range(NT + 1):
            if i < NT:
                late += [(f"n3T{i}{j}", "dve") for j in range(2)]
            if i < 2:
                late += [(f"pp{NT - 2 + i}{j}", "act") for j in range(2)]
            if i >= 1:
                late += [(f"pg{i - 1}{j}", "act") for j in range(2)]
        for n, (name, who) in enumerate(late):
            number[name] = NGROUP + n
            seen[who] += 1
            drain_count[name] = seen[who]
        allgroups = groups + late
        drainer = dict(allgroups)

        def ps(name):
            return bank[number[name] % 8]

        def wait_full(eng, name):
            eng.wait_ge(filled, number[name] + 1)

        def wait_drained(eng, name):
            eng.wait_ge(act_drained if drainer[name] == "act" else dve_drained, drain_count[name])

        def wait_bank(pe, name):
            n = number[name]
            if n >= 8 and not NGROUP <= n < NGROUP + 8:
                wait_drained(pe, allgroups[n - 8][0])

        class Chain:

            def __init__(self, eng, s):
                self.eng, self.sem, self.n = eng, s, 0

            def post(self, ins):
                self.n += 1
                ins.then_inc(self.sem, 1)

            def link(self, ins):
                self.post(ins)
                self.eng.wait_ge(self.sem, self.n)

        ssum, rstd = tiny(6 * 3), tiny(6 * 3)
        fsum, frstd = tiny(6), tiny(6)
        bn, mv, lvar, lrstd = tiny(6 * NT), tiny(2 * NT), tiny(NT), tiny(NT)
        usum, urstd, rsum, rrstd = tiny(NT), tiny(NT), tiny(NT), tiny(NT)
        hb = tiny(16)
        nlam, lab, lexp, lden, ls, ls2, lpoly, sp = (tiny(8) for _ in range(8))
        c4, c2 = tiny(8), tiny(8)
        wt1, wt2 = tiny(NT), tiny(NT)
        slotf = tiny(2 * NT).rearrange("p (a i) -> p a i", a=2)
        first = taken[0]

        def tiny(n):
            at = taken[0] - first
            taken[0] += n
            assert at + n <= 5 * NTOK - 2900
            return regR[:, 2900 + at:2900 + at + n]

        glog = tiny(NT * NG).rearrange("p (i n) -> p i n", i=NT)
        elog = tiny(NT * NE).rearrange("p (n e) -> p n e", e=NEG)
        gmax, gidx, gsum = tiny(NT), tiny(NT), tiny(NT)
        gsh, gexp, gone, gcand = (tiny(NT * NG).rearrange("p (i n) -> p i n", i=NT) for _ in range(4))
        el2, one1, one2, ecand = (tiny(NT * NE).rearrange("p (n e) -> p n e", e=NEG) for _ in range(4))
        m1g, m2g, e_idx = tiny(NT * NG), tiny(NT * NG), tiny(NT * NG)
        m1, m2, xe, den = (tiny(NT) for _ in range(4))
        work = [regR[:, j * 160:j * 160 + NT * NE] for j in range(10)]
        oh1, oh2, chose, prefix, rank, slotm, lt = (w.rearrange("p (i e) -> p i e", i=NT) for w in work[:7])
        pick = work[7].rearrange("p (i e) -> p i e", i=NT)
        choseb = sb("choseb", [P, NT * NE], BF16)
        nexp, over, incl, excl, base = (tiny(NE) for _ in range(5))
        oq = regR[:, 1600:1600 + 4 * NE].rearrange("p (q e) -> p q e", q=4)
        ojn = regR[:, 1700:1700 + MAX_OVER * NE].rearrange("p (j e) -> p j e", j=MAX_OVER)
        oj2 = regR[:, 1900:1900 + MAX_OVER * NE].rearrange("p (j e) -> p j e", j=MAX_OVER)
        jexp, jfirst, jcnt = (tiny(MAX_OVER) for _ in range(3))

        T_NUM, T_EXP, T_COUNT = 0, 1, 16

        def yg(n):
            return yg_buf[n % NYG]

        def added_at(step):
            return {-2: (0, 1), -1: ()}.get(step, (step + 2,) if step + 2 < NT else ())

        def moe_slots(par):
            return (1, 2, 3) if par == 0 else (4, 5, 0)

        QW = 1024

        def split_high(act, unit, loads=16):
            lo, hi = SPLIT[unit]
            act.wait_ge(ring_in[lo], loads)
            for q in range(4):
                c = slice(q * QW, (q + 1) * QW)
                nc.scalar.activation(ringR[:, hi, c], ring[:, lo, c], ACT.Copy).then_inc(hi_ready[unit], 1)

        def split_low(eng, engine, unit):
            lo, hi = SPLIT[unit]
            for q in range(4):
                c = slice(q * QW, (q + 1) * QW)
                eng.wait_ge(hi_ready[unit], q + 1)
                engine.tensor_tensor(ringR[:, lo, c], ring[:, lo, c], ringR[:, hi, c].bitcast(F32), ALU.subtract).then_inc(lo_ready[unit], 1)

        def both_parts(unit):
            return tuple(ringR[:, s, :].rearrange("p (k n) -> p k n", k=KD) for s in reversed(SPLIT[unit]))

        before = {0: 2, 1: 1, 2: 1, 3: 1, 4: 1, 5: 0}

        block = ctx.enter_context(nc.Block())

        @block.sync
        def _(sp):
            for i in range(NT):
                sp.dma_start(h[:, i, :], token_rows(x_prompt, x_sample, i)).then_inc(x_in[i], 16)
                if i == 0:
                    sp.dma_start(gB[:], g_mix[0].partition_broadcast(P)).then_inc(gB_in, 16)

            def load_in(s, col):
                sp.dma_start(slot3(s), w_in[:, col:col + DR].rearrange("(k p) n -> p k n", p=P)).then_inc(ring_in[s], 16)

            rows = lambda w, pat, **kw: w.rearrange(pat, **kw)
            for at_row, src in ((CONV_W, rows(conv_w, "k (c p) -> (k c) p", p=P)), (CONV_B, rows(conv_b, "o (c p) -> (o c) p", p=P)),
                                (B_A, rows(lru_b_a, "d (c p) -> (d c) p", p=P)), (B_X, rows(lru_b_x, "d (c p) -> (d c) p", p=P)),
                                (LAM, rows(lru_lambda, "d (c p) -> (d c) p", p=P)), (G_REC, rows(g_rec_out, "o (c p) -> (o c) p", p=P)),
                                (G_SGU, rows(g_sgu_out, "o (c p) -> (o c) p", p=P)), (B_S, sgu_b_s)):
                sp.dma_start(par_rows[at_row:at_row + src.shape[0], :], src).then_inc(par_in, 16)
            load_in(0, 0)
            sp.wait_ge(consts, 1)
            for g, src in enumerate((lru_w_a, lru_w_x)):
                for d in range(2):
                    for half in range(2):
                        lo = half * HD
                        dst = wbd[lo:lo + HD, (d * 2 + g) * C4 * P:(d * 2 + g + 1) * C4 * P].rearrange("i (c j) -> i c j", c=C4)[:, :, lo:lo + HD]
                        sp.dma_start(dst, src[d].rearrange("(c s) i j -> s i c j", s=2)[half]).then_inc(wbd_in, 16)
            sp.dma_start(w_s, sgu_w_s.rearrange("h t s -> t h s")).then_inc(ws_in, 16)
            load_in(2, 3 * DR)
            sp.dma_start(ln_g, sgu_ln_g[0].partition_broadcast(P)).then_inc(ln_in, 16)
            sp.dma_start(ln_b, sgu_ln_b[0].partition_broadcast(P)).then_inc(ln_in, 16)
            load_in(4, 2 * DR)
            sp.dma_start(wr[:, :, 0:NG], w_router_group.rearrange("(k p) n -> p k n", p=P)).then_inc(wr_in, 16)
            sp.dma_start(wr[:, :, NG:], w_router_expert.rearrange("(k p) n -> p k n", p=P)).then_inc(wr_in, 16)
            sp.dma_start(br[:, 0:NG], b_router_group[0].partition_broadcast(P)).then_inc(wr_in, 16)
            sp.dma_start(br[:, NG:], b_router_expert[0].partition_broadcast(P)).then_inc(wr_in, 16)
            wait_full(sp, f"xr{C4 - 1}1")
            load_in(1, DR)
            sp.wait_ge(consts, 16)
            more_rows = y_dram[NE * CAP:, :]
            whole = MAX_OVER * CAP // P
            for j in range(2):
                cols = slice(j * 512, (j + 1) * 512)
                sp.dma_start(more_rows[0:whole * P, cols].rearrange("(a p) d -> p a d", p=P),
                             zeros[:, :].unsqueeze(1).to_broadcast([P, whole, 512])).then_inc(zeroed, 16)
                sp.dma_start(more_rows[whole * P:, cols], zeros[0:MAX_OVER * CAP - whole * P, :]).then_inc(zeroed, 16)
                sp.dma_start(y_dram[0:NE * CAP, cols].rearrange("(e s) d -> s e d", s=CAP)[FEW:CAP],
                             zeros[0:CAP - FEW, :].unsqueeze(1).to_broadcast([CAP - FEW, NE, 512])).then_inc(zeroed, 16)
            sp.wait_ge(v_ready, NT)
            wait_drained(sp, "wsT1")
            for i in range(NT):
                sp.dma_start(p_tm[:, i, :], token_rows(p_prompt, p_sample, i)).then_inc(p_in, 16)
            for j, (s, last) in enumerate(((3, "v5"), (0, "u5"))):
                wait_full(sp, last)
                sp.dma_start(slot3(s), w_out[:, j * 512:(j + 1) * 512].rearrange("(k p) n -> p k n", p=P)).then_inc(ring_in[s], 16)
            wait_full(sp, f"gr{C4 - 1}1")
            for i in range(NT):
                sp.dma_start(h[:, i, :], token_rows(x_prompt, x_sample, i)).then_inc(x_in[i], 16)

            def load_weights(s, src, e, waits):
                for sm, value in waits:
                    sp.wait_ge(sm, value)
                w = src[bass.ds(e, 1), :, :].rearrange("a r n -> (a r) n")
                dst = ring[:, s, :].rearrange("p (k n) -> p k n", k=F4) if src is w_exp_down else slot3(s)
                sp.dma_start(dst, w.rearrange("(k p) n -> p k n", p=P)).then_inc(ring_in[s], 16)

            def load_expert(par, e, waits):
                for s, src, wait in zip(moe_slots(par), (w_exp_gate, w_exp_up, w_exp_down), waits):
                    load_weights(s, src, e, wait)

            full = lambda name: (filled, number[name] + 1)
            load_weights(3, w_exp_down, 0, [full(f"out{NT - 1}0r")])
            load_weights(4, w_exp_gate, 1, [])
            load_weights(1, w_exp_gate, 0, [full(f"out{NT - 1}1r")])
            load_weights(2, w_exp_up, 0, [])
            load_weights(5, w_exp_up, 1, [full("pT11"), (gathered[0], 32), (gathered[1], 32)])
            load_weights(0, w_exp_down, 1, [])
            with sp.Fori(1, NE // 2) as i:
                for par in range(2):
                    done = 2 * i + par - 1
                    gu, down = [(gu_full, 2 * done)], [(yhi_full, done), (thi_full, done)]
                    load_expert(par, 2 * i + par, (gu, gu, down))
            sp.wait_ge(routed, 1)
            more = sp.value_load(table[0:1, T_NUM:T_NUM + 1], min_val=0, max_val=MAX_OVER)
            with sp.If(more > 0):
                with sp.Fori(0, more) as j:
                    e = sp.value_load(table[0:1, bass.ds(j + T_EXP, 1)], min_val=0, max_val=NE - 1)
                    gu, down = [(gu_full, 2 * (NE + j))], [(yhi_full, NE + j), (thi_full, NE + j)]
                    load_expert(0, e, (gu, gu, down))
                sp.wait_ge(yhi_full, NE + more)
                sp.wait_ge(thi_full, NE + more)
                sp.sem_inc(last_over, 1)
            sp.wait_ge(gu_full, 2 * (NE - 1))
            for a, s in enumerate((1, 2)):
                sp.dma_start(slot3(s), w_ple_gate[:, a * 512:(a + 1) * 512].rearrange("(k p) n -> p k n", p=P)).then_inc(ring_in[s], 16)
            sp.wait_ge(yhi_full, NE - 1)
            sp.wait_ge(thi_full, NE - 1)
            sp.dma_start(ring[:, 3, 0:2 * D].rearrange("p (k n) -> p k n", k=2),
                         w_ple_proj.rearrange("(k p) n -> p k n", p=P)).then_inc(ring_in[3], 16)
            for i in range(NT):
                sp.wait_ge(fin_norm, i + 1)
                sp.dma_start(token_rows(y_prompt, y_sample, i), ntok[:, i, :]).then_inc(stored, 16)
            sp.wait_ge(stored, 16 * NT)

        @block.gpsimd
        def _(pool):
            nc.gpsimd.memset(wbd, 0.0).then_inc(consts, 1)
            nc.gpsimd.memset(zeros[:], 0.0).then_inc(consts, 1)
            nc.gpsimd.memset(ident[:], 0.0).then_inc(consts, 1)
            nc.gpsimd.memset(tri[:], 1.0).then_inc(consts, 1)
            pool.wait_ge(consts, 4)
            nc.gpsimd.affine_select(out=ident[:], in_=ident[:], compare_op=ALU.not_equal, fill=1.0, base=0,
                                    pattern=[[-1, P]], channel_multiplier=1).then_inc(consts, 1)
            nc.gpsimd.affine_select(out=tri[:], in_=tri[:], compare_op=ALU.is_gt, fill=0.0, base=0,
                                    pattern=[[1, P]], channel_multiplier=-1).then_inc(consts, 1)
            nc.gpsimd.memset(ones[:], 1.0).then_inc(consts, 1)
            nc.gpsimd.memset(onesb[:], 1.0).then_inc(consts, 1)
            nc.gpsimd.memset(nhalf, -0.5).then_inc(consts, 1)
            nc.gpsimd.memset(rankm[:, NE:NE + 2, :], -1.0).then_inc(consts, 1)
            nc.gpsimd.iota(iota[:], pattern=[[1, CAP]], base=0, channel_multiplier=0,
                           allow_small_or_imprecise_dtypes=True).then_inc(consts, 1)
            nc.gpsimd.iota(iota16[:], pattern=[[1, NE]], base=0, channel_multiplier=0,
                           allow_small_or_imprecise_dtypes=True).then_inc(consts, 1)
            nc.gpsimd.iota(iotaj, pattern=[[1, MAX_OVER]], base=0, channel_multiplier=0,
                           allow_small_or_imprecise_dtypes=True).then_inc(consts, 1)
            nc.gpsimd.iota(tokid[:, :, 0:1], pattern=[[0, NT], [0, 1]], base=0, channel_multiplier=1,
                           allow_small_or_imprecise_dtypes=True).then_inc(consts, 1)
            nc.gpsimd.iota(tokid[:, :, 1:2], pattern=[[P, NT], [0, 1]], base=0, channel_multiplier=0,
                           allow_small_or_imprecise_dtypes=True).then_inc(consts, 1)
            nc.gpsimd.iota(iota4[:], pattern=[[1, 4]], base=-4, channel_multiplier=0,
                           allow_small_or_imprecise_dtypes=True).then_inc(consts, 1)
            ch = Chain(pool, pool_seq)
            pool.wait_ge(consts, 16)

            def rstd_of(src, dst, n, scale, out_sem):
                ch.link(nc.gpsimd.tensor_scalar(src, src, scale, EPS, ALU.mult, ALU.add))
                nc.gpsimd.tensor_tensor(dst, src, nhalf[:, 0:n], ALU.pow).then_inc(out_sem, 1)

            def norm_rstd(k, tiles=range(NT)):
                for i in tiles:
                    pool.wait_ge(sumsq_done, k * NT + i + 1)
                    a = k * NT + i
                    rstd_of(ssum[:, a:a + 1], rstd[:, a:a + 1], 1, 1.0 / D, rstd_done)

            norm_rstd(0)
            split_low(pool, nc.gpsimd, "v")
            split_low(pool, nc.gpsimd, "u")
            for i in range(NT):
                pool.wait_ge(ln_var, i + 1)
                ch.link(nc.gpsimd.tensor_scalar(lvar[:, i:i + 1], mv[:, 2 * i + 1:2 * i + 2], 1.0, EPS, ALU.mult, ALU.add))
                nc.gpsimd.tensor_tensor(lrstd[:, i:i + 1], lvar[:, i:i + 1], nhalf[:, 0:1], ALU.pow).then_inc(ln_rstd, 1)
            split_low(pool, nc.gpsimd, "gr")
            pool.wait_ge(us_sq, NT)
            rstd_of(usum, urstd, NT, 1.0 / DR, us_rstd)
            split_low(pool, nc.gpsimd, "wo0")
            wait_drained(pool, "ssq")
            rstd_of(rsum, rrstd, NT, 1.0 / DR, rr_rstd)
            norm_rstd(1)
            pool.wait_ge(n2_stored, 16 * NT)

            def gather(r, par, ids_at, known=True):
                def rows(n):
                    nc.gpsimd.indirect_dma_start(moe["xg", par][0:n, :], None, n2_dram,
                                                 bass.IndirectOffsetOnAxis(ap=idsi[0:n, par, 0:1], axis=0)).then_inc(gathered[par], 16)

                def further_rows(n):
                    nc.gpsimd.indirect_dma_start(moe["xg2", par][0:n, :], None, n2_dram,
                                                 bass.IndirectOffsetOnAxis(ap=idsi[0:n, par, 1:2], axis=0)).then_inc(gathered[par], 16)

                count = pool.value_load(table[0:1, bass.ds(r + T_COUNT, 1)], min_val=0, max_val=NTOK) if known else None
                pool.wait_ge(ids_ready, 2 * (ids_at + 1))
                pool.sem_inc(gather_go, 1)
                if not known:
                    rows(P)
                    further_rows(CAP2)
                    return
                with pool.If(count < FEW + 1):
                    rows(FEW)
                with pool.Else():
                    rows(P)
                with pool.If(count < P + 1):
                    further_rows(NO_ROWS)
                with pool.Else():
                    further_rows(CAP2)

            wait_full(pool, f"route{NT - 1}")
            gather(0, 0, 0, known=False)
            gather(1, 1, 1, known=False)
            pool.wait_ge(routed, 1)
            with pool.Fori(1, NE // 2 + 1) as i:
                for par in range(2):
                    r = 2 * i + par
                    pool.wait_ge(t_full, 3 * (r - 1))
                    gather(r, par, r)
            more = pool.value_load(table[0:1, T_NUM:T_NUM + 1], min_val=0, max_val=MAX_OVER)
            with pool.If(more > 0):
                with pool.Fori(0, more) as j:
                    pool.wait_ge(t_full, 3 * (NE + 1 + j))
                    gather(NE + j, 0, NE + 2 + j)
            pool.wait_ge(yhi_full, NE + more)
            pool.wait_ge(thi_full, NE + more)
            pool.wait_ge(y_stored[0], 32 * (NE // 2 + more))
            pool.wait_ge(y_stored[1], 32 * (NE // 2))
            pool.wait_ge(slots_ready, 1)
            pool.sem_inc(gather_go, 1)
            for i in range(NT):
                for a in range(2):
                    n = 2 * i + a
                    if n >= NYG:
                        pool.wait_ge(moe_added, n - NYG + 1)
                    nc.gpsimd.indirect_dma_start(yg(n), None, y_dram,
                                                 bass.IndirectOffsetOnAxis(ap=slots[:, a, i:i + 1], axis=0)).then_inc(yg_in[n % NYG], 16)
                if i >= NYG // 2 - 1:
                    norm_rstd(2, [i - NYG // 2 + 1])
            for i in range(NT + 1):
                if NT - NYG // 2 + 1 <= i + 2 < NT:
                    norm_rstd(2, [i + 2])
                if i >= 1:
                    pool.wait_ge(fin_sumsq, i)
                    rstd_of(fsum[:, i - 1:i], frstd[:, i - 1:i], 1, 1.0 / D, fin_rstd)

        @block.tensor
        def _(pe):
            pe.wait_ge(consts, 16)

            def transposes(name, parts):
                wait_bank(pe, name)
                at = 0
                for src, n in parts:
                    q = nc.tensor.transpose(ps(name)[:src.shape[1], at:at + n], src, ident[0:n, 0:n])
                    at += n
                q.then_inc(filled, 1)

            def product(name, out, pairs):
                wait_bank(pe, name)
                for k, (a, b) in enumerate(pairs):
                    q = nc.tensor.matmul(out, a, b, start=(k == 0), stop=(k == len(pairs) - 1))
                q.then_inc(filled, 1)

            def product3(name, out, terms, quarters=None):
                wait_bank(pe, name)
                passes = [(a[i], b[j]) for a, b in terms for i, j in ((0, 0), (0, 1), (1, 0))]
                for n, (a, b) in enumerate(passes):
                    if quarters is not None and n % (len(passes) // 4) == 0:
                        pe.wait_ge(quarters, 4 * n // len(passes) + 1)
                    q = nc.tensor.matmul(out, a, b, start=(n == 0), stop=(n == len(passes) - 1))
                q.then_inc(filled, 1)

            def n_cols(k, i0, n):
                return nT_hi[:, k, i0:i0 + n, :], nT_lo[:, k, i0:i0 + n, :]

            def n_tile(k, i):
                return nT_hi[:, k, i, :], nT_lo[:, k, i, :]

            def norm_transposes(prefix, k, tiles=range(NT)):
                for i in tiles:
                    pe.wait_ge(norm_done, k * NT + i + 1)
                    for j in range(2):
                        transposes(f"{prefix}{i}{j}", [(ntok[:, i, (4 * j + a) * P:(4 * j + a + 1) * P], P) for a in range(4)])

            norm_transposes("nT", 0)
            pe.wait_ge(par_in, 16 * 8)
            transposes("par", [(par_rows[:, :], NPAR)])
            for i in range(NT):
                for j in range(2):
                    wait_drained(pe, f"nT{i}{j}")
            def channel_major(unit, c, s):
                t0, n = SEGS[s]
                name = f"{unit}{c}{s}"
                w = both_parts(unit)
                product3(name, ps(name)[:, 0:n], [([x[:, k, c * P:(c + 1) * P] for x in w], n_cols(k, t0 // P, n // P)) for k in range(KD)],
                         lo_ready["xr"] if name == "xr00" else None)

            for c in range(C4):
                for s in range(2):
                    channel_major("xr", c, s)
            pe.wait_ge(ws_in, 16)
            for j in range(2):
                transposes(f"wsT{j}", [(w_s[:, 4 * j + a, :], P) for a in range(4)])

            def filler(name):
                if name[0] in "vu":
                    i, w = int(name[1]), both_parts(name[0])
                    pe.wait_ge(lo_ready[name[0]], 4)
                    product3(name, ps(name)[:, :], [(n_tile(k, i), [x[:, k, :] for x in w]) for k in range(KD)])
                elif name[:3] == "mix":
                    hh = int(name[3])
                    if hh == 0:
                        pe.wait_ge(v_ready, NT)
                        wait_drained(pe, "wsT1")
                    product(name, ps(name)[:, 0:NT * HD].rearrange("p (i c) -> p i c", i=NT),
                            [(wsT[:, hh, :], v_tm[:, :, hh * HD:(hh + 1) * HD])])
                else:
                    pe.wait_ge(lo_ready["gr"], 4)
                    channel_major("gr", int(name[2]), int(name[3]))

            for unit in range(8):
                c, d = unit // 2, unit % 2
                wait_drained(pe, f"xr{c}1")
                if unit == 0:
                    pe.wait_ge(wbd_in, 16 * 8)
                for g in range(2):
                    w = wbd[:, ((d * 2 + g) * C4 + c) * P:((d * 2 + g) * C4 + c + 1) * P]
                    for s, (t0, n) in enumerate(SEGS):
                        name = f"gate{unit}{g}{s}"
                        product(name, ps(name)[:, 0:n], [(w, xc[:, c, t0:t0 + n])])
                for name in fillers[unit]:
                    filler(name)
            for c, s in ys_order:
                tiles = ((0, 1, 2, 3), (4, 5))[s]
                if c == 0:
                    pe.wait_ge(us_scaled, tiles[-1] + 1)
                transposes(f"ysT{c}{s}", [(u_tm[:, i, c * P:(c + 1) * P], P) for i in tiles])
            def out_product(i, j, g):
                w = both_parts(f"wo{j}")
                src, row = ((xc_hi, xc_lo), 0) if g == "r" else ((ys_hi, ys_lo), C4)
                name = f"out{i}{j}{g}"
                product3(name, ps(name)[:, :], [([x[:, c, i * P:(i + 1) * P] for x in src], [x[:, row + c, :] for x in w]) for c in range(C4)])

            pe.wait_ge(lo_ready["wo0"], 4)
            for g, i in first_half:
                if g == "s" and i in (0, 4):
                    for c in range(C4):
                        wait_drained(pe, f"ysT{c}{i // 4}")
                if g != "ssq":
                    out_product(i, 0, g)
                    continue
                pe.wait_ge(rec_sq, C4)
                wait_bank(pe, "ssq")
                for t in range(NT):
                    for c in range(C4):
                        q = nc.tensor.matmul(ps("ssq")[:, t:t + 1], gr[:, c, t * P:(t + 1) * P], ones[:, 0:1],
                                             start=(c == 0), stop=(c == C4 - 1))
                q.then_inc(filled, 1)
                pe.wait_ge(rec_g, C4)
            pe.wait_ge(lo_ready["wo1"], 4)
            pe.wait_ge(wr_in, 16 * 4)
            for i in range(NT + 2):
                if i < NT:
                    for g in "sr":
                        out_product(i, 1, g)
                if i == NT:
                    pe.wait_ge(p_in, 16 * NT)
                    for k in range(2):
                        for s, tiles in enumerate(((0, 1, 2, 3), (4, 5))):
                            transposes(f"pT{k}{s}", [(p_tm[:, t, k * P:(k + 1) * P], P) for t in tiles])
                if 1 <= i <= NT:
                    norm_transposes("n2T", 1, [i - 1])
                if i >= 2:
                    for j in range(2):
                        wait_drained(pe, f"n2T{i - 2}{j}")
                    name = f"route{i - 2}"
                    product(name, ps(name)[:, 0:NG + NE], [(n2T_buf[:, i % 2, k, :], wr[:, k, :]) for k in range(KD)])
            pe.wait_ge(chosen, 1)
            wait_bank(pe, "rank")
            for i in range(NT + 1):
                out = ps("rank")[:, i * NE:(i + 1) * NE]
                parts = [(onesb, t) for t in range(i)] + ([(tri, i)] if i < NT else [])
                for n, (w, t) in enumerate(parts):
                    q = nc.tensor.matmul(out, w[:], choseb[:, t * NE:(t + 1) * NE], start=(n == 0), stop=(n == len(parts) - 1))
            q.then_inc(filled, 1)
            wait_drained(pe, "rank")
            wait_drained(pe, f"n2T{NT - 1}1")

            def ids(at):
                pe.wait_ge(onehot_ready, at + 1)
                if not (isinstance(at, int) and at == 0):
                    pe.wait_ge(ids_ready, 2 * at)
                for t in range(NT):
                    nc.tensor.matmul(bank[5][:, 0:2], onehot[:, t, 0:P], tokid[:, t, :], start=(t == 0), stop=(t == NT - 1))
                for t in range(NT):
                    q = nc.tensor.matmul(bank[5][0:CAP2, 2:4], onehot[:, t, P:CAP], tokid[:, t, :], start=(t == 0), stop=(t == NT - 1))
                q.then_inc(ids_full, 1)

            def turn(part, par, t_at):
                if not (isinstance(t_at, int) and t_at == 0 and part == 0):
                    pe.wait_ge(t_drained, 3 * t_at + part)
                    pe.sem_inc(turn_go, 1)
                for a in range(4 if part < 2 else KD):
                    if part < 2:
                        k = 4 * part + a
                        q = nc.tensor.transpose(bank[4][:, a * P:(a + 1) * P], moe["xg", par][:, k * P:(k + 1) * P], ident[:])
                    else:
                        q = nc.tensor.transpose(bank[4][:, a * CAP2:(a + 1) * CAP2], moe["xg2", par][:, a * P:(a + 1) * P], ident[0:CAP2, 0:CAP2])
                q.then_inc(t_full, 1)

            def hidden(f, par, n):
                sg, su, _ = moe_slots(par)
                half, col = f // 2, (f % 2) * 256
                for b, s in ((2 * half, sg), (2 * half + 1, su)):
                    for k in range(KD):
                        q = nc.tensor.matmul(bank[b][:, col:col + n], slot3(s)[:, k, f * P:(f + 1) * P], moe["xT", par][:, k, 0:n],
                                             start=(k == 0), stop=(k == KD - 1))
                return q

            def down(out, par, lo, n, j, chunks):
                for f in chunks:
                    high, low = down_hi[f][j], down_low(par, f, j)
                    x_high, x_low = hid_hi[:, f, lo:lo + n], hid_lo[:, f, lo:lo + n]
                    nc.tensor.matmul(out[0:n, :], x_high, high, start=(f == 0), stop=False)
                    nc.tensor.matmul(out[0:n, :], x_high, low, start=False, stop=False)
                    q = nc.tensor.matmul(out[0:n, :], x_low, high, start=False, stop=(f == F4 - 1))
                return q

            def by_size(count, body, sizes=CLASSES):
                if len(sizes) == 1:
                    body(sizes[0])
                    return
                low = sizes[:len(sizes) // 2]
                with pe.If(count < low[-1] + 1):
                    by_size(count, body, low)
                with pe.Else():
                    by_size(count, body, sizes[len(low):])

            def one_round(r, par, loads, prev_hidden, turn_next):
                count = pe.value_load(table[0:1, bass.ds(r + T_COUNT, 1)], min_val=0, max_val=NTOK)
                sg, su, sd = moe_slots(par)
                pe.wait_ge(t_drained, 3 * (turn_next[1] if turn_next else r + 1))
                pe.wait_ge(ring_in[sg], loads[0])
                pe.wait_ge(ring_in[su], loads[1])
                for half in range(2):
                    if prev_hidden is not None:
                        pe.wait_ge(hid_done, 2 * prev_hidden + half + 1)

                    def body(n, half=half):
                        hidden(2 * half, par, n)
                        hidden(2 * half + 1, par, n).then_inc(gu_full, 1)
                    by_size(count, body)
                    if turn_next:
                        if half == 0:
                            pe.wait_ge(gathered[1 - par], turn_next[2])
                            if prev_hidden is not None:
                                pe.wait_ge(ylo_drained, 2 * r)
                                pe.wait_ge(yhi_drained, 2 * r)
                            ids(r + 2)
                        turn(half, 1 - par, turn_next[1])
                pe.wait_ge(down_low_done, 8 * (r + 1))
                if prev_hidden is not None:
                    pe.wait_ge(ylo_drained, 2 * r)
                    pe.wait_ge(yhi_drained, 2 * r)
                for half in range(2):
                    pe.wait_ge(hid_done, 2 * r + half + 1)
                    for j in range(2):
                        q = down(bank[6 + j], par, 0, P, j, (2 * half, 2 * half + 1))
                        if half == 1:
                            q.then_inc((ylo_full, yhi_full)[j], 1)
                    if half == 0 and turn_next:
                        turn(2, 1 - par, turn_next[1])
                if turn_next:
                    pe.wait_ge(t_drained, 3 * (r + 2))
                    pe.wait_ge(ids_ready, 2 * (r + 3))
                with pe.If(count < P + 1):
                    pe.sem_inc(tlo_full, 1)
                    pe.sem_inc(thi_full, 1)
                with pe.Else():
                    down(bank[4], par, P, CAP2, 0, range(F4)).then_inc(tlo_full, 1)
                    down(bank[5], par, P, CAP2, 1, range(F4)).then_inc(thi_full, 1)

            ids(0)
            ids(1)
            pe.wait_ge(gathered[0], 32)
            for part in range(3):
                turn(part, 0, 0)
            pe.wait_ge(routed, 1)

            def main_round(i, par, first):
                r = 2 * i + par
                loads = [16 * (before[s] + 1 + i) for s in moe_slots(par)]
                count = 32 * (i + 1) if par == 0 else 32 * (i + 2)
                one_round(r, par, loads, None if first else r - 1, (None, r + 1, count))

            main_round(0, 0, True)
            main_round(0, 1, False)
            with pe.Fori(1, NE // 2) as i:
                main_round(i, 0, False)
                main_round(i, 1, False)
            more = pe.value_load(table[0:1, T_NUM:T_NUM + 1], min_val=0, max_val=MAX_OVER)
            with pe.If(more > 0):
                with pe.Fori(0, more) as j:
                    pe.wait_ge(ylo_drained, 2 * (NE + j))
                    pe.wait_ge(yhi_drained, 2 * (NE + j))
                    ids(NE + 2 + j)
                    pe.wait_ge(gathered[0], 32 * (NE // 2 + 2 + j))
                    for part in range(3):
                        turn(part, 0, NE + 1 + j)
                    pe.wait_ge(t_drained, 3 * (NE + 2 + j))
                    one_round(NE + j, 0, [16 * (before[s] + 1 + NE // 2 + j) for s in moe_slots(0)], NE - 1 + j, None)
            pe.wait_ge(ylo_drained, 2 * (NE + more))
            pe.wait_ge(yhi_drained, 2 * (NE + more))
            pe.wait_ge(t_drained, 3 * (NE + 1 + more))
            pe.wait_ge(ids_ready, 2 * (NE + 2 + more))
            pe.wait_ge(gathered[1], 32 * (NE // 2 + 1))
            pe.wait_ge(ring_in[3], 16 * (1 + NE // 2 + more + 1))

            def embed(i):
                for j in range(2):
                    name = f"pp{i}{j}"
                    product(name, ps(name)[:, :], [(pT[:, k, i * P:(i + 1) * P], ring[:, 3, k * D + j * 512:k * D + (j + 1) * 512]) for k in range(2)])

            for i in range(NT - 2):
                embed(i)
            for i in range(NT + 1):
                if i < NT:
                    norm_transposes("n3T", 2, [i])
                if i < 2:
                    embed(NT - 2 + i)
                if i >= 1:
                    for j in range(2):
                        wait_drained(pe, f"n3T{i - 1}{j}")
                    for j in range(2):
                        if i == 1:
                            pe.wait_ge(lo_ready[f"pg{j}"], 4)
                        name, b = f"pg{i - 1}{j}", (i - 1) % 2
                        product3(name, ps(name)[:, :], [([n3T_hi[:, b, k, :], n3T_lo[:, b, k, :]], [x[:, k, :] for x in both_parts(f"pg{j}")]) for k in range(KD)])

        @block.scalar
        def _(act):
            ch = Chain(act, act_seq)

            def sumsq(i, dst, ready, value, done=sumsq_done):
                act.wait_ge(ready, value)
                nc.scalar.activation(ntok[:, i, :], h[:, i, :], ACT.Square, accum_out=dst).then_inc(done, 1)

            def drain(name, out, func=ACT.Identity, view=None, **kw):
                wait_full(act, name)
                nc.scalar.activation(out, ps(name)[:, 0:out.free_size()] if view is None else view, func, **kw).then_inc(act_drained, 1)

            def high_nT(i):
                for j in range(2):
                    name = f"nT{i}{j}"
                    wait_full(act, name)
                    nc.scalar.activation(nT_hi[:, 4 * j:4 * j + 4, i, :], ps(name)[:, :].rearrange("p (k t) -> p k t", k=4),
                                         ACT.Copy).then_inc(nT_high, 1)

            for i in range(NT + 2):
                if i < NT:
                    sumsq(i, ssum[:, i:i + 1], x_in[i], 16)
                if i >= 2:
                    high_nT(i - 2)
            split_high(act, "xr")
            act.wait_ge(halves_ready, 1)
            nc.scalar.activation(lexp, lab, ACT.Exp, scale=-1.0).then_inc(exp_lam, 1)
            act.wait_ge(norm_done, NT)
            act.dma_start(gB[:], g_ffn[0].partition_broadcast(P)).then_inc(gB_in, 16)
            split_high(act, "v")
            for j in range(2):
                name = f"wsT{j}"
                drain(name, wsT[:, 4 * j:4 * j + 4, :], view=ps(name)[:, :].rearrange("p (h t) -> p h t", h=4))
            split_high(act, "u")

            def fill(name):
                if name[0] == "v":
                    drain(name, v_tm[:, int(name[1]), :], ACT.Gelu_apprx_tanh)
                elif name[0] == "u":
                    drain(name, u_tm[:, int(name[1]), :], ACT.Gelu_apprx_tanh)
                elif name[:2] == "gr":
                    t0, n = SEGS[int(name[3])]
                    wait_full(act, "mix7")
                    drain(name, gr[:, int(name[2]), t0:t0 + n], ACT.Gelu_apprx_tanh)

            for unit in range(8):
                c, d = unit // 2, unit % 2
                col = d * C4 + c
                if unit == 0:
                    act.wait_ge(decay_ready, 1)
                else:
                    act.wait_ge(scan_part, 2 * unit)
                    if unit >= 2:
                        act.wait_ge(rec_sum, unit // 2)
                for g, dst in enumerate((TR, TI)):
                    for s, (t0, n) in enumerate(SEGS):
                        drain(f"gate{unit}{g}{s}", dst[:, t0:t0 + n], ACT.Tanh, scale=0.5, bias=hb[:, g * 8 + col:g * 8 + col + 1])
                act.wait_ge(act_drained, drain_count[f"gate{unit}01"])
                nc.scalar.activation(A0, TR, ACT.Exp, scale=c4[:, col:col + 1], bias=c4[:, col:col + 1]).then_inc(rec_exp, 1)
                nc.scalar.activation(TT, TR, ACT.Tanh, scale=c2[:, col:col + 1], bias=c2[:, col:col + 1]).then_inc(rec_exp, 1)
                def root():
                    act.wait_ge(rec_m2, unit + 1)
                    nc.scalar.activation(TR, TR, ACT.Sqrt, scale=0.25).then_inc(rec_mult, 1)

                if unit == 3:
                    split_high(act, "gr")
                if unit >= 6:
                    root()
                if unit == 6:
                    act.wait_ge(zeroed, 16 * 6)
                    for i in range(NT):
                        act.wait_ge(dve_drained, drain_count["mix7"])
                        nc.scalar.activation(zeros[:, :], u_tm[:, i, :], ACT.Square, accum_out=usum[:, i:i + 1]).then_inc(us_sq, 1)
                        act.wait_ge(us_sq, i + 1)
                if unit == 7:
                    split_high(act, "wo0")
                for name in fillers[unit]:
                    fill(name)
                if unit < 6:
                    root()
            for c, s in ys_order:
                t0, n = ((0, 512), (512, 256))[s]
                name = f"ysT{c}{s}"
                wait_full(act, name)
                nc.scalar.activation(ys_hi[:, c, t0:t0 + n], ps(name)[:, 0:n], ACT.Copy,
                                     scale=chan[:, G_SGU + c:G_SGU + c + 1]).then_inc(ys_high, 1)
            for c in range(C4):
                act.wait_ge(rec_y, c + 1)
                nc.scalar.activation(gr[:, c, :], xc[:, c, :], ACT.Square).then_inc(rec_sq, 1)
            for c in range(C4):
                nc.scalar.activation(xc_hi[:, c, :], xc[:, c, :], ACT.Copy, scale=chan[:, G_REC + c:G_REC + c + 1]).then_inc(rec_high, 1)
            split_high(act, "wo1", 32)
            wait_full(act, "ssq")
            for i in range(NT + 1):
                if i < NT:
                    sumsq(i, ssum[:, NT + i:NT + i + 1], dve_drained, drain_count[f"out{i}1r"])
                if i == NT:
                    for k in range(2):
                        drain(f"pT{k}1", pT[:, k, 512:768])
                if i >= 1:
                    act.wait_ge(norm_done, NT + i)
                    act.dma_start(n2_dram[(i - 1) * P:i * P, :], ntok[:, i - 1, :]).then_inc(n2_stored, 16)
                    name = f"n2T{i - 1}1"
                    drain(name, n2T_buf[:, (i - 1) % 2, 4:8, :], view=ps(name)[:, :].rearrange("p (k t) -> p k t", k=4))
            act.dma_start(gB[:], g_ple[0].partition_broadcast(P)).then_inc(gB_in, 16)

            def turned(part, par, t_at):
                act.wait_ge(t_full, 3 * t_at + part + 1)
                if part < 2:
                    nc.scalar.activation(moe["xT", par][:, 4 * part:4 * part + 4, 0:P],
                                         bank[4][:, :].rearrange("p (k s) -> p k s", k=4), ACT.Copy).then_inc(t_drained, 1)
                else:
                    nc.scalar.activation(moe["xT", par][:, :, P:CAP],
                                         bank[4][:, 0:KD * CAP2].rearrange("p (k s) -> p k s", k=KD), ACT.Copy).then_inc(t_drained, 1)

            def silu_half(r, half, first):
                act.wait_ge(gu_full, 2 * r + half + 1)
                if not first:
                    act.wait_ge(hid_done, 2 * r - 1 + half)
                nc.scalar.activation(silu[:, 2 * half:2 * half + 2, :],
                                     bank[2 * half][:, :].rearrange("p (f s) -> p f s", f=2)[:, :, 0:CAP], ACT.Silu).then_inc(silu_done, 1)

            def hid_high_half(r, half):
                act.wait_ge(hid_raw, 2 * r + half + 1)
                nc.scalar.activation(hid_hi[:, 2 * half:2 * half + 2, :], hid[:, 2 * half:2 * half + 2, :], ACT.Copy).then_inc(hid_high, 1)

            def down_high(par, loads):
                act.wait_ge(ring_in[moe_slots(par)[2]], loads)
                for f in range(F4):
                    for j in range(2):
                        nc.scalar.activation(down_hi[f][j], down_part(par, f, j), ACT.Copy).then_inc(down_high_done, 1)

            def y_out(r, par, first, store_count):
                count = act.value_load(table[0:1, bass.ds(r + T_COUNT, 1)], min_val=0, max_val=NTOK)
                act.wait_ge(yhi_full, r + 1)
                if store_count is not None:
                    act.wait_ge(y_stored[par], store_count)
                nc.scalar.activation(moe["y", par][:, 512:D], bank[7][:, :], ACT.Copy).then_inc(yhi_drained, 1)
                act.wait_ge(thi_full, r + 1)
                nc.scalar.activation(moe["y2", par][:, 512:D], bank[5][0:CAP2, :], ACT.Copy).then_inc(yhi_drained, 1)
                act.wait_ge(yhi_drained, 2 * r + 2)
                act.wait_ge(ylo_drained, 2 * r + 2)
                act.sem_inc(store_go, 1)
                with act.If(count < FEW + 1):
                    act.dma_start(y_dram[bass.ds(r * CAP, FEW), :], moe["y", par][0:FEW, :]).then_inc(y_stored[par], 16)
                with act.Else():
                    act.dma_start(y_dram[bass.ds(r * CAP, P), :], moe["y", par]).then_inc(y_stored[par], 16)
                with act.If(count < P + 1):
                    act.dma_start(y_dram[bass.ds(r * CAP + P, NO_ROWS), :], moe["y2", par][0:NO_ROWS, :]).then_inc(y_stored[par], 16)
                with act.Else():
                    act.dma_start(y_dram[bass.ds(r * CAP + P, CAP2), :], moe["y2", par]).then_inc(y_stored[par], 16)

            def main_round(i, par, first):
                r = 2 * i + par
                down_high(par, 16 * (before[moe_slots(par)[2]] + 1 + i))
                silu_half(r, 0, first)
                turned(0, 1 - par, r + 1)
                hid_high_half(r, 0)
                silu_half(r, 1, first)
                hid_high_half(r, 1)
                turned(1, 1 - par, r + 1)
                turned(2, 1 - par, r + 1)
                y_out(r, par, first, None if isinstance(i, int) else 32 * i)

            for part in range(3):
                turned(part, 0, 0)
            act.wait_ge(route_max, 1)
            nc.scalar.activation(gexp, gsh, ACT.Exp).then_inc(route_exp, 1)
            nc.scalar.activation(xe, m2, ACT.Exp).then_inc(route_exp, 1)
            act.wait_ge(slots_ready, 1)
            main_round(0, 0, True)
            main_round(0, 1, False)
            with act.Fori(1, NE // 2) as i:
                main_round(i, 0, False)
                main_round(i, 1, False)
            more = act.value_load(table[0:1, T_NUM:T_NUM + 1], min_val=0, max_val=MAX_OVER)
            with act.If(more > 0):
                with act.Fori(0, more) as j:
                    for part in range(3):
                        turned(part, 0, NE + 1 + j)
                    down_high(0, 16 * (before[moe_slots(0)[2]] + 1 + NE // 2 + j))
                    silu_half(NE + j, 0, False)
                    hid_high_half(NE + j, 0)
                    silu_half(NE + j, 1, False)
                    hid_high_half(NE + j, 1)
                    y_out(NE + j, 0, False, 32 * (NE // 2 + j))
            def take_embed(i):
                for j in range(2):
                    drain(f"pp{i}{j}", pp_sb[2 * i + j])

            act.wait_ge(thi_full, NE + more)
            ple_loads = 16 * (1 + NE // 2 + more + 1)
            split_high(act, "pg0", ple_loads)
            take_embed(0)
            take_embed(1)
            split_high(act, "pg1", ple_loads)
            take_embed(2)
            act.wait_ge(y_stored[0], 32 * (NE // 2 + more))
            act.wait_ge(y_stored[1], 32 * (NE // 2))
            act.dma_start(gF, g_final.partition_broadcast(P)).then_inc(gF_in, 16)
            for i in range(-2, NT + 1):
                if 0 <= i < NT:
                    for j in range(2):
                        name = f"n3T{i}{j}"
                        wait_full(act, name)
                        nc.scalar.activation(n3T_hi[:, i % 2, 4 * j:4 * j + 4, :], ps(name)[:, :].rearrange("p (k t) -> p k t", k=4),
                                             ACT.Copy).then_inc(n3T_high, 1)
                if 0 <= i < 2:
                    take_embed(NT - 2 + i)
                for t in added_at(i):
                    sumsq(t, ssum[:, 2 * NT + t:2 * NT + t + 1], moe_added, 2 * (t + 1))
                if i == -2:
                    take_embed(3)
                if i < 1:
                    continue
                for j in range(2):
                    n = 2 * (i - 1) + j
                    name = f"pg{i - 1}{j}"
                    if n >= 2:
                        act.wait_ge(pgm_done, n - 1)
                    wait_full(act, name)
                    nc.scalar.activation(sig[:, n % 2, :], ps(name)[:, :], ACT.Sigmoid).then_inc(act_drained, 1)
                sumsq(i - 1, fsum[:, i - 1:i], h_ready, 2 * i, fin_sumsq)


        @block.vector
        def _(dve):
            ch = Chain(dve, dve_seq)
            link, post = ch.link, ch.post
            V = nc.vector

            def drain(name, make):
                wait_full(dve, name)
                make(ps(name)).then_inc(dve_drained, 1)

            def normalise(k, i, gain_loads, src, scale):
                dve.wait_ge(rstd_done, k * NT + i + 1)
                dve.wait_ge(gB_in, 16 * gain_loads)
                V.scalar_tensor_tensor(out=ntok[:, i, :], in0=h[:, i, :], scalar=scale[:, src:src + 1], in1=gB[:],
                                       op0=ALU.mult, op1=ALU.mult).then_inc(norm_done, 1)

            def low_nT(i):
                for j in range(2):
                    dve.wait_ge(nT_high, 2 * i + j + 1)
                    drain(f"nT{i}{j}", lambda b: V.tensor_tensor(nT_lo[:, 4 * j:4 * j + 4, i, :], b[:, :].rearrange("p (k t) -> p k t", k=4),
                                                                 nT_hi[:, 4 * j:4 * j + 4, i, :].bitcast(F32), ALU.subtract))

            for i in range(NT):
                normalise(0, i, 1, i, rstd)
                if i >= 2:
                    low_nT(i - 2)
            low_nT(NT - 2)
            low_nT(NT - 1)
            split_low(dve, V, "xr")
            drain("par", lambda b: V.tensor_copy(chan[:, :], b[:, 0:NPAR]))
            dve.wait_ge(dve_drained, drain_count["par"])
            link(V.tensor_scalar(nlam, chan[:, LAM:LAM + 8], -1.0, None, ALU.mult))
            V.tensor_tensor(lab, chan[:, LAM:LAM + 8], nlam, ALU.max).then_inc(halves_ready, 1)
            link(V.tensor_scalar(hb, chan[:, B_A:B_A + 16], 0.5, None, ALU.mult))
            for c in range(C4):
                if c == 1:
                    dve.wait_ge(exp_lam, 1)
                    link(V.tensor_scalar(lden, lexp, 2.0, None, ALU.add))
                    link(V.reciprocal(lden, lden))
                    link(V.tensor_tensor(ls, lexp, lden, ALU.mult))
                    link(V.tensor_tensor(ls2, ls, ls, ALU.mult))
                    link(V.tensor_scalar(lpoly, ls2, 1.0 / 15, 1.0 / 13, ALU.mult, ALU.add))
                    for n in (11, 9, 7, 5, 3, 1):
                        link(V.tensor_tensor(lpoly, lpoly, ls2, ALU.mult))
                        link(V.tensor_scalar(lpoly, lpoly, 1.0 / n, None, ALU.add))
                    link(V.scalar_tensor_tensor(out=lpoly, in0=lpoly, scalar=2.0, in1=ls, op0=ALU.mult, op1=ALU.mult))
                    link(V.scalar_tensor_tensor(out=sp, in0=nlam, scalar=0.0, in1=lpoly, op0=ALU.max, op1=ALU.add))
                    link(V.tensor_scalar(c4, sp, -4.0, None, ALU.mult))
                    V.tensor_scalar(c2, sp, 2.0, None, ALU.mult).then_inc(decay_ready, 1)
                for s, (t0, n) in enumerate(SEGS):
                    name = f"xr{c}{s}"
                    wait_full(dve, name)
                    x = ps(name)
                    tap = lambda k: chan[:, CONV_W + k * C4 + c:CONV_W + k * C4 + c + 1]
                    o = xc[:, c, t0:t0 + n]
                    link(V.tensor_scalar(o, x[:, 0:n], tap(2), chan[:, CONV_B + c:CONV_B + c + 1], ALU.mult, ALU.add))
                    link(V.scalar_tensor_tensor(out=o[:, 1:n], in0=x[:, 0:n - 1], scalar=tap(1), in1=o[:, 1:n], op0=ALU.mult, op1=ALU.add))
                    link(V.scalar_tensor_tensor(out=o[:, 2:n], in0=x[:, 0:n - 2], scalar=tap(0), in1=o[:, 2:n], op0=ALU.mult, op1=ALU.add))
                    V.scalar_tensor_tensor(out=o[:, 0:n - 1], in0=x[:, 1:n], scalar=tap(3), in1=o[:, 0:n - 1],
                                           op0=ALU.mult, op1=ALU.add).then_inc(dve_drained, 1)

            def fill(name):
                if name[0] == "v":
                    i = int(name[1])
                    v = v_tm[:, i, :]
                    dve.wait_ge(act_drained, drain_count[name])
                    dve.wait_ge(ln_in, 32)
                    link(V.bn_stats(bn[:, 6 * i:6 * i + 6], v))
                    V.bn_aggr(mv[:, 2 * i:2 * i + 2], bn[:, 6 * i:6 * i + 6]).then_inc(ln_var, 1)
                    dve.wait_ge(ln_rstd, i + 1)
                    link(V.tensor_scalar(v, v, mv[:, 2 * i:2 * i + 1], lrstd[:, i:i + 1], ALU.subtract, ALU.mult))
                    link(V.tensor_tensor(v, v, ln_g, ALU.mult))
                    V.tensor_tensor(v, v, ln_b, ALU.add).then_inc(v_ready, 1)
                elif name[:3] == "mix":
                    hh = int(name[3])
                    if hh == 0:
                        dve.wait_ge(act_drained, drain_count["u5"])
                    uu = u_tm[:, :, hh * HD:(hh + 1) * HD]
                    drain(name, lambda b: V.scalar_tensor_tensor(out=uu, in0=b[:, 0:NT * HD].rearrange("p (i c) -> p i c", i=NT),
                                                                 scalar=chan[:, B_S + hh:B_S + hh + 1], in1=uu, op0=ALU.add, op1=ALU.mult))

            for unit in range(8):
                c, d = unit // 2, unit % 2
                dve.wait_ge(act_drained, drain_count[f"gate{unit}11"])
                link(V.scalar_tensor_tensor(out=TI, in0=TI, scalar=1.0, in1=xc[:, c, :], op0=ALU.add, op1=ALU.mult))
                dve.wait_ge(rec_exp, 2 * (unit + 1))
                link(V.scalar_tensor_tensor(out=TT, in0=A0, scalar=1.0, in1=TT, op0=ALU.add, op1=ALU.mult))
                link(V.tensor_scalar(A0, TT, -1.0, 1.0, ALU.mult, ALU.add))
                V.scalar_tensor_tensor(out=TR, in0=A0, scalar=1.0, in1=TT, op0=ALU.add, op1=ALU.mult).then_inc(rec_m2, 1)
                for name in fillers[unit]:
                    fill(name)
                dve.wait_ge(rec_mult, unit + 1)
                link(V.tensor_tensor(TI, TI, TR, ALU.mult))
                for s, (t0, n) in enumerate(SEGS):
                    if d == 0:
                        q = V.tensor_tensor_scan(HF[:, t0:t0 + n], A0[:, t0:t0 + n], TI[:, t0:t0 + n], 0.0, ALU.mult, ALU.add)
                    else:
                        rev = slice(t0 + n - 1, t0 - 1 if t0 else None, -1)
                        q = V.tensor_tensor_scan(TT[:, rev], A0[:, rev], TI[:, rev], 0.0, ALU.mult, ALU.add)
                    q.then_inc(scan_part, 1)
                dve.wait_ge(scan_part, 2 * (unit + 1))
                if d == 1:
                    V.tensor_tensor(xc[:, c, :], HF, TT, ALU.add).then_inc(rec_sum, 1)
                if unit == 6:
                    dve.wait_ge(us_rstd, 1)
                    for i in range(NT):
                        V.tensor_scalar(u_tm[:, i, :], u_tm[:, i, :], urstd[:, i:i + 1], None, ALU.mult).then_inc(us_scaled, 1)
            for at, (c, s) in enumerate(ys_order):
                t0, n = ((0, 512), (512, 256))[s]
                dve.wait_ge(ys_high, at + 1)
                drain(f"ysT{c}{s}", lambda b: V.scalar_tensor_tensor(out=ys_lo[:, c, t0:t0 + n], in0=b[:, 0:n], scalar=chan[:, G_SGU + c:G_SGU + c + 1],
                                                                     in1=ys_hi[:, c, t0:t0 + n].bitcast(F32), op0=ALU.mult, op1=ALU.subtract))
            for c in range(C4):
                dve.wait_ge(rec_sum, c + 1)
                dve.wait_ge(act_drained, drain_count[f"gr{c}1"])
                V.tensor_tensor(xc[:, c, :], xc[:, c, :], gr[:, c, :], ALU.mult).then_inc(rec_y, 1)
            for c in range(C4):
                dve.wait_ge(rec_high, c + 1)
                V.scalar_tensor_tensor(out=xc_lo[:, c, :], in0=xc[:, c, :], scalar=chan[:, G_REC + c:G_REC + c + 1],
                                       in1=xc_hi[:, c, :].bitcast(F32), op0=ALU.mult, op1=ALU.subtract).then_inc(rec_g, 1)
            def add_out(i, j, g):
                hs = h[:, i, j * 512:(j + 1) * 512]
                name = f"out{i}{j}{g}"
                if g == "r":
                    drain(name, lambda b: V.scalar_tensor_tensor(out=hs, in0=b[:, :], scalar=rrstd[:, i:i + 1], in1=hs, op0=ALU.mult, op1=ALU.add))
                else:
                    drain(name, lambda b: V.tensor_tensor(hs, b[:, :], hs, ALU.add))
                dve.wait_ge(dve_drained, drain_count[name])

            for n, (g, i) in enumerate(first_half):
                if g == "ssq":
                    drain("ssq", lambda b: V.tensor_copy(rsum, b[:, 0:NT]))
                    dve.wait_ge(rr_rstd, 1)
                    continue
                if n < 4 or i >= 4:
                    dve.wait_ge(x_in[i], 32)
                add_out(i, 0, g)
                if n == 8:
                    split_low(dve, V, "wo1")
            dve.wait_ge(wr_in, 64)

            def take_n2T(i):
                drain(f"n2T{i}0", lambda b: V.tensor_copy(n2T_buf[:, i % 2, 0:4, :], b[:, :].rearrange("p (k t) -> p k t", k=4)))

            def take_logits(i):
                wait_full(dve, f"route{i}")
                post(V.tensor_tensor(glog[:, i, :], ps(f"route{i}")[:, 0:NG], br[:, 0:NG], ALU.add))
                drain(f"route{i}", lambda b: V.tensor_tensor(elog[:, i * NG:(i + 1) * NG, :].rearrange("p g e -> p (g e)"), b[:, NG:NG + NE],
                                                             br[:, NG:], ALU.add))

            for i in range(NT):
                add_out(i, 1, "s")
                if i >= 1:
                    normalise(1, i - 1, 2, NT + i - 1, rstd)
                add_out(i, 1, "r")
                if i >= 1:
                    take_n2T(i - 1)
                if i >= 2:
                    take_logits(i - 2)
            for k in range(2):
                drain(f"pT{k}0", lambda b, k=k: V.tensor_copy(pT[:, k, 0:512], b[:, :]))
            normalise(1, NT - 1, 2, 2 * NT - 1, rstd)
            take_n2T(NT - 1)
            take_logits(NT - 2)
            take_logits(NT - 1)

            dve.wait_ge(dve_drained, drain_count[f"route{NT - 1}"])
            groups4 = [P, NT, NG]
            experts = [P, NT * NG, NEG]
            gi, gim = (x[:, 0:4].unsqueeze(1).to_broadcast(groups4) for x in (iota, iota4))
            ei, eim = (x[:, 0:4].unsqueeze(1).to_broadcast(experts) for x in (iota, iota4))

            def first_max(x, mx, idx, onehot, cand, index, index_less, size):
                wide = lambda a: a.unsqueeze(2).to_broadcast(size)
                return [lambda: V.tensor_reduce(mx, x, AX.X, ALU.max),
                        lambda: V.tensor_tensor(cand, x, wide(mx), ALU.is_equal),
                        lambda: V.scalar_tensor_tensor(out=cand, in0=cand, scalar=-4.0, in1=index, op0=ALU.mult, op1=ALU.add),
                        lambda: V.tensor_reduce(idx, cand, AX.X, ALU.min),
                        lambda: V.tensor_tensor(onehot, index_less, wide(idx), ALU.is_equal)]

            for group_step, expert_step in zip(first_max(glog, gmax, gidx, gone, gcand, gi, gim, groups4),
                                               first_max(elog, m1g, e_idx, one1, ecand, ei, eim, experts)):
                post(group_step())
                link(expert_step())
            post(V.tensor_tensor(gsh, glog, gmax.unsqueeze(2).to_broadcast(groups4), ALU.subtract))
            link(V.scalar_tensor_tensor(out=el2, in0=one1, scalar=MASKED, in1=elog, op0=ALU.mult, op1=ALU.add))
            for step in first_max(el2, m2g, e_idx, one2, ecand, ei, eim, experts):
                link(step())
            gflat = gone.rearrange("p i g -> p (i g)")
            in_group = gflat.unsqueeze(2).to_broadcast(experts)
            o4 = lambda oh: oh.rearrange("p i (g e) -> p (i g) e", g=NG)
            link(V.tensor_tensor(ecand, one1, one2, ALU.add))
            V.tensor_tensor(choseb[:].rearrange("p (n e) -> p n e", e=NEG), ecand, in_group, ALU.mult).then_inc(chosen, 1)
            post(V.tensor_tensor(o4(chose), ecand, in_group, ALU.mult))
            post(V.tensor_tensor(o4(oh1), one1, in_group, ALU.mult))
            post(V.tensor_tensor(o4(oh2), one2, in_group, ALU.mult))
            post(V.tensor_tensor(m1g, m1g, gflat, ALU.mult))
            link(V.tensor_tensor(m2g, m2g, gflat, ALU.mult))
            by_tile = lambda a: a.rearrange("p (i g) -> p i g", i=NT)
            post(V.tensor_reduce(m1, by_tile(m1g), AX.X, ALU.add))
            link(V.tensor_reduce(m2, by_tile(m2g), AX.X, ALU.add))
            V.tensor_tensor(m2, m2, m1, ALU.subtract).then_inc(route_max, 1)
            wait_full(dve, "rank")
            ranks = ps("rank")[:, 0:NT * NE].rearrange("p (i e) -> p i e", i=NT)
            link(V.scalar_tensor_tensor(out=pick, in0=ranks, scalar=1.0, in1=chose, op0=ALU.add, op1=ALU.mult))
            link(V.tensor_scalar(rankm[:, 0:NE, :], pick.rearrange("p i e -> p e i"), -1.0, None, ALU.add))

            def make_onehot(at, e, ramp):
                if not (isinstance(at, int) and at == 0):
                    dve.wait_ge(ids_full, at)
                V.tensor_tensor(onehot, ramp.unsqueeze(1).to_broadcast([P, NT, CAP]),
                                rankm[:, bass.ds(e, 1), :].rearrange("p a i -> p (a i)").unsqueeze(2).to_broadcast([P, NT, CAP]),
                                ALU.is_equal).then_inc(onehot_ready, 1)

            def take_ids(at, par, gathered_before):
                dve.wait_ge(ids_full, at + 1)
                if gathered_before is not None:
                    dve.wait_ge(gathered[par], gathered_before)
                V.tensor_reduce(idsf[:, par, 0:1], bank[5][:, 0:2], AX.X, ALU.add).then_inc(ids_sum, 1)
                V.tensor_reduce(idsf[0:CAP2, par, 1:2], bank[5][0:CAP2, 2:4], AX.X, ALU.add).then_inc(ids_sum, 1)
                dve.wait_ge(ids_sum, 2 * at + 2)
                V.tensor_copy(idsi[:, par, 0:1], idsf[:, par, 0:1]).then_inc(ids_ready, 1)
                V.tensor_copy(idsi[0:CAP2, par, 1:2], idsf[0:CAP2, par, 1:2]).then_inc(ids_ready, 1)

            make_onehot(0, 0, iota[:])
            link(V.tensor_copy(rank, ranks))
            V.tensor_copy(nexp, ps("rank")[:, NT * NE:(NT + 1) * NE]).then_inc(dve_drained, 1)
            take_ids(0, 0, None)
            make_onehot(1, 1, iota[:])
            take_ids(1, 1, None)
            for b in range(4):
                post(V.memset(bank[b][:, :].rearrange("p (f s) -> p f s", f=2)[:, :, CLASSES[0]:CAP], 0.0))
            post(V.memset(bank[5][0:CAP2, 8:], 0.0))
            post(V.memset(table[:], 0))
            post(V.memset(base, 1.0))
            make_onehot(2, 2, iota[:])
            for q in range(4):
                (post if q < 3 else link)(V.tensor_scalar(oq[:, q, :], nexp, float(CAP * (q + 1)), None, ALU.is_gt))
            link(V.tensor_reduce(over, oq.rearrange("p q e -> p e q"), AX.X, ALU.add))
            link(V.tensor_tensor_scan(incl, base, over, 0.0, ALU.mult, ALU.add))
            link(V.tensor_tensor(excl, incl, over, ALU.subtract))
            bJ = lambda a: a.unsqueeze(1).to_broadcast([P, MAX_OVER, NE])
            jE = lambda a: a.unsqueeze(2).to_broadcast([P, MAX_OVER, NE])
            link(V.tensor_tensor(ojn, bJ(incl), jE(iotaj), ALU.is_le))
            link(V.tensor_reduce(jexp, ojn, AX.X, ALU.add))
            link(V.tensor_tensor(ojn, bJ(iota16[:]), jE(jexp), ALU.is_equal))
            link(V.tensor_tensor(oj2, ojn, bJ(excl), ALU.mult))
            link(V.tensor_reduce(jfirst, oj2, AX.X, ALU.add))
            link(V.tensor_tensor(oj2, ojn, bJ(nexp), ALU.mult))
            link(V.tensor_reduce(jcnt, oj2, AX.X, ALU.add))
            link(V.tensor_tensor(jfirst, iotaj, jfirst, ALU.subtract))
            link(V.tensor_scalar(offs[:], jfirst, 1.0, float(CAP), ALU.add, ALU.mult))
            link(V.tensor_tensor(jcnt, jcnt, offs[:], ALU.subtract))
            link(V.tensor_scalar(jcnt, jcnt, 0.0, None, ALU.max))
            link(V.tensor_scalar(jexp, jexp, float(NE - 1), None, ALU.min))
            post(V.tensor_copy(table[:, T_NUM:T_NUM + 1], incl[:, NE - 1:NE]))
            post(V.tensor_copy(table[:, T_EXP:T_EXP + MAX_OVER], jexp))
            post(V.tensor_copy(table[:, T_COUNT:T_COUNT + NE], nexp))
            V.tensor_copy(table[:, T_COUNT + NE:T_COUNT + NROUND], jcnt).then_inc(routed, 1)

            dve.wait_ge(route_exp, 2)
            link(V.tensor_reduce(gsum, gexp, AX.X, ALU.add))
            link(V.tensor_scalar(den, xe, 1.0, None, ALU.add))
            link(V.tensor_tensor(den, den, gsum, ALU.mult))
            link(V.reciprocal(wt1, den))
            link(V.tensor_tensor(wt2, wt1, xe, ALU.mult))
            link(V.tensor_scalar(base, excl, float(CAP), float((NE - 1) * CAP), ALU.mult, ALU.add))
            link(V.tensor_scalar(lt, rank, float(CAP), None, ALU.is_lt))
            bE = lambda a: a.unsqueeze(1).to_broadcast([P, NT, NE])
            link(V.tensor_scalar(slotm, bE(iota16[:]), float(CAP), None, ALU.mult))
            link(V.tensor_tensor(slotm, slotm, bE(base), ALU.subtract))
            link(V.tensor_tensor(slotm, slotm, lt, ALU.mult))
            link(V.tensor_tensor(slotm, slotm, bE(base), ALU.add))
            link(V.tensor_tensor(slotm, slotm, rank, ALU.add))
            for a, oh in enumerate((oh1, oh2)):
                link(V.tensor_tensor(pick, oh, slotm, ALU.mult))
                link(V.tensor_reduce(slotf[:, a, :], pick, AX.X, ALU.add))
                link(V.tensor_copy(slots[:, a, :], slotf[:, a, :]))
            dve.sem_inc(slots_ready, 1)


            def hid_half(r, half):
                dve.wait_ge(silu_done, 2 * r + half + 1)
                V.tensor_tensor(hid[:, 2 * half:2 * half + 2, :], silu[:, 2 * half:2 * half + 2, :],
                                bank[2 * half + 1][:, :].rearrange("p (f s) -> p f s", f=2)[:, :, 0:CAP], ALU.mult).then_inc(hid_raw, 1)
                dve.wait_ge(hid_high, 2 * r + half + 1)
                V.tensor_tensor(hid_lo[:, 2 * half:2 * half + 2, :], hid[:, 2 * half:2 * half + 2, :],
                                hid_hi[:, 2 * half:2 * half + 2, :].bitcast(F32), ALU.subtract).then_inc(hid_done, 1)

            def split_down(r, par):
                for f in range(F4):
                    for j in range(2):
                        dve.wait_ge(down_high_done, 8 * r + 2 * f + j + 1)
                        V.tensor_tensor(down_low(par, f, j), down_part(par, f, j), down_hi[f][j].bitcast(F32), ALU.subtract).then_inc(down_low_done, 1)

            def y_out(r, par, store_count):
                dve.wait_ge(ylo_full, r + 1)
                if store_count is not None:
                    dve.wait_ge(y_stored[par], store_count)
                V.tensor_copy(moe["y", par][:, 0:512], bank[6][:, :]).then_inc(ylo_drained, 1)
                dve.wait_ge(tlo_full, r + 1)
                V.tensor_copy(moe["y2", par][:, 0:512], bank[4][0:CAP2, :]).then_inc(ylo_drained, 1)

            dve.wait_ge(routed, 1)

            def main_round(i, par):
                r = 2 * i + par
                split_down(r, par)
                hid_half(r, 0)
                take_ids(r + 2, par, 32 * (i + 1))
                hid_half(r, 1)
                y_out(r, par, None if isinstance(i, int) else 32 * i)

            main_round(0, 0)
            make_onehot(3, 3, iota[:])
            main_round(0, 1)
            with dve.Fori(1, NE // 2) as i:
                for par in range(2):
                    make_onehot(2 * i + par + 2, 2 * i + par + 2, iota[:])
                    main_round(i, par)
            more = dve.value_load(table[0:1, T_NUM:T_NUM + 1], min_val=0, max_val=MAX_OVER)
            with dve.If(more > 0):
                with dve.Fori(0, more) as j:
                    e = dve.value_load(table[0:1, bass.ds(j + T_EXP, 1)], min_val=0, max_val=NE - 1)
                    dve.wait_ge(onehot_ready, NE + 2 + j)
                    V.tensor_scalar(iota_o, iota[:], offs[:, bass.ds(j, 1)], None, ALU.add).then_inc(ramp_ready, 1)
                    dve.wait_ge(ramp_ready, j + 1)
                    make_onehot(NE + 2 + j, e, iota_o)
                    take_ids(NE + 2 + j, 0, 32 * (NE // 2 + 1 + j))
                    split_down(NE + j, 0)
                    hid_half(NE + j, 0)
                    hid_half(NE + j, 1)
                    y_out(NE + j, 0, 32 * (NE // 2 + j))
            def final_norm(i):
                dve.wait_ge(fin_rstd, i + 1)
                dve.wait_ge(gF_in, 16)
                V.scalar_tensor_tensor(out=ntok[:, i, :], in0=h[:, i, :], scalar=frstd[:, i:i + 1], in1=gF,
                                       op0=ALU.mult, op1=ALU.mult).then_inc(fin_norm, 1)

            split_low(dve, V, "pg0")
            for i in range(-2, NT + 1):
                if 0 <= i < NT:
                    for j in range(2):
                        dve.wait_ge(n3T_high, 2 * i + j + 1)
                        drain(f"n3T{i}{j}", lambda b: V.tensor_tensor(n3T_lo[:, i % 2, 4 * j:4 * j + 4, :], b[:, :].rearrange("p (k t) -> p k t", k=4),
                                                                      n3T_hi[:, i % 2, 4 * j:4 * j + 4, :].bitcast(F32), ALU.subtract))
                if 0 <= i + 1 < NT:
                    normalise(2, i + 1, 3, 2 * NT + i + 1, rstd)
                if i == 0:
                    split_low(dve, V, "pg1")
                for t in added_at(i):
                    for a, wt in enumerate((wt1, wt2)):
                        n = 2 * t + a
                        hs = h[:, t, :]
                        dve.wait_ge(yg_in[n % NYG], 16 * (n // NYG + 1))
                        V.scalar_tensor_tensor(out=hs, in0=yg(n), scalar=wt[:, t:t + 1], in1=hs,
                                               op0=ALU.mult, op1=ALU.add).then_inc(moe_added, 1)
                        dve.wait_ge(moe_added, n + 1)
                if i >= 2:
                    final_norm(i - 2)
                if i < 1:
                    continue
                for j in range(2):
                    n = 2 * (i - 1) + j
                    dve.wait_ge(act_drained, drain_count[f"pg{i - 1}{j}"])
                    V.tensor_tensor(pgm[:, n % 2, :], pp_sb[n], sig[:, n % 2, :], ALU.mult).then_inc(pgm_done, 1)
                    dve.wait_ge(pgm_done, n + 1)
                    hs = h[:, i - 1, j * 512:(j + 1) * 512]
                    V.tensor_tensor(hs, hs, pgm[:, n % 2, :], ALU.add).then_inc(h_ready, 1)
                    dve.wait_ge(h_ready, n + 1)
            final_norm(NT - 1)


_INS = ["x_prompt", "x_sample", "p_prompt", "p_sample", "g_mix", "w_in", "conv_w", "conv_b", "lru_w_a", "lru_b_a",
        "lru_w_x", "lru_b_x", "lru_lambda", "sgu_ln_g", "sgu_ln_b", "sgu_w_s", "sgu_b_s", "g_rec_out", "g_sgu_out",
        "w_out", "g_ffn", "w_router_group", "b_router_group", "w_router_expert", "b_router_expert", "w_exp_gate",
        "w_exp_up", "w_exp_down", "g_ple", "w_ple_gate", "w_ple_proj", "g_final"]
_SQUEEZE = {"x_prompt": 1, "x_sample": 1, "p_prompt": 2, "p_sample": 2, "w_in": 1, "conv_w": 1, "lru_w_a": 1,
            "lru_b_a": 1, "lru_w_x": 1, "lru_b_x": 1, "lru_lambda": 1, "sgu_w_s": 1, "sgu_b_s": 1, "w_out": 1,
            "w_router_group": 1, "w_router_expert": 1, "w_exp_gate": 1, "w_exp_up": 1, "w_exp_down": 1,
            "w_ple_gate": 1, "w_ple_proj": 1}


def kernel(**inputs):
    import numpy as _np
    import concourse.bacc as _bacc
    from concourse import mybir as _mybir
    from concourse.bass_utils import run_bass_kernel_spmd as _run

    nc = _bacc.Bacc("TRN2", target_bir_lowering=False, num_devices=1, dynamic_dma_scratch_size=8192)
    arrays, args = {}, []
    for name in _INS:
        a = _np.ascontiguousarray(inputs[name])
        a = a.reshape(a.shape[_SQUEEZE.get(name, 0):])
        arrays[f"in_{name}"] = a
        args.append(nc.dram_tensor(f"in_{name}", a.shape, _mybir.dt.from_np(a.dtype), kind="ExternalInput").ap())
    for name, n in (("y_prompt", NPROMPT), ("y_sample", NSAMPLE)):
        args.append(nc.dram_tensor(name, (n, D), F32, kind="ExternalOutput").ap())
    hybrid_encoder_kernel(nc, *args)
    r = _run(nc, [arrays], core_ids=[0])
    return (r.results[0]["y_prompt"].reshape(1, NPROMPT, D), r.results[0]["y_sample"].reshape(1, NSAMPLE, D))
```
